# Optimizing a Trainium2 kernel written in Bass

```python
import math
import jax, jax.numpy as jnp
from jax import lax
import numpy as np

D_MODEL = 1024
BATCH = 1
SEQ = 512
DEPTH = 2

N_A = max(1, DEPTH // 2)
N_B = DEPTH - N_A
HGRN_HEADS = 8
HGRN_DK = D_MODEL // HGRN_HEADS
HGRN_DV = D_MODEL // HGRN_HEADS
HGRN_FDIM = HGRN_HEADS * HGRN_DK
HGRN_CHUNK = 16
SB_HEADS = 8
SB_HEAD_DIM = 128
SB_DIM = SB_HEADS * SB_HEAD_DIM
SB_QBLOCK = 128
PEER_HEADS = 4
PEER_NKEYS = 128
PEER_N = PEER_NKEYS * PEER_NKEYS
PEER_DK = 256
PEER_TOPK = 16
PEER_TOKEN_BLOCK = 128
NORM_EPS = 1e-6


def rms_norm(x, g):
    xf = x.astype(jnp.float32)
    y = xf * lax.rsqrt(jnp.mean(xf * xf, axis=-1, keepdims=True) + NORM_EPS)
    return (y * g.astype(jnp.float32)).astype(x.dtype)

def modulate(xn, shift, scale):
    return xn * (1 + scale[:, None, :]) + shift[:, None, :]

def hgrn2_mixer(xn, w_in, lb, onorm_g, w_out):
    b, s, _ = xn.shape
    nc = s // HGRN_CHUNK
    proj = xn @ w_in
    q, f, i, g = jnp.split(proj, [HGRN_FDIM, 2 * HGRN_FDIM, 2 * HGRN_FDIM + D_MODEL], axis=-1)
    lbf = lb.astype(jnp.float32)
    fgate = lbf + (1 - lbf) * jax.nn.sigmoid(f.astype(jnp.float32))
    log_f = jnp.log(fgate)
    k = 1 - fgate
    q = jax.nn.silu(q.astype(jnp.float32))
    v = i.astype(jnp.float32)

    def to_chunks(t, d):
        return t.reshape(b, nc, HGRN_CHUNK, HGRN_HEADS, d).transpose(1, 0, 3, 2, 4)

    causal = jnp.tril(jnp.ones((HGRN_CHUNK, HGRN_CHUNK), dtype=bool))

    def step(state, inp):
        qc, kc, vc, lfc = inp
        cum = jnp.cumsum(lfc, axis=2)
        last = cum[:, :, -1:, :]
        qd = qc * jnp.exp(cum)
        kd = kc * jnp.exp(-cum)
        scores = jnp.where(causal, jnp.einsum('bhtk,bhsk->bhts', qd, kd), 0.0)
        o = (jnp.einsum('bhts,bhsv->bhtv', scores, vc)
             + jnp.einsum('bhtk,bhkv->bhtv', qd, state))
        new_state = (jnp.exp(last[:, :, 0, :])[..., None] * state
                     + jnp.einsum('bhsk,bhsv->bhkv', kc * jnp.exp(last - cum), vc))
        return new_state, o

    state0 = jnp.zeros((b, HGRN_HEADS, HGRN_DK, HGRN_DV), jnp.float32)
    _, o = lax.scan(step, state0, (to_chunks(q, HGRN_DK), to_chunks(k, HGRN_DK),
                                   to_chunks(v, HGRN_DV), to_chunks(log_f, HGRN_DK)))
    o = o.transpose(1, 0, 3, 2, 4).reshape(b, s, HGRN_HEADS, HGRN_DV)
    o = o * lax.rsqrt(jnp.mean(o * o, axis=-1, keepdims=True) + NORM_EPS)
    o = o.reshape(b, s, D_MODEL) * onorm_g.astype(jnp.float32) * jax.nn.silu(g.astype(jnp.float32))
    return o.astype(xn.dtype) @ w_out

def shared_kv(h, c_act, kv_ada_w, kv_ada_b, kv_norm_g, kv_w):
    b, s, _ = h.shape
    shift, scale = jnp.split(c_act @ kv_ada_w + kv_ada_b, 2, axis=-1)
    hn = modulate(rms_norm(h, kv_norm_g), shift, scale)
    kv = (hn @ kv_w).reshape(b, s, 2, SB_HEADS, SB_HEAD_DIM)
    k = kv[:, :, 0].transpose(0, 2, 1, 3)
    v = kv[:, :, 1].transpose(0, 2, 1, 3)
    return k, v

def stick_breaking_mixer(xn, k_sh, v_sh, w_q, w_out):
    b, s, _ = xn.shape
    nq = s // SB_QBLOCK
    q = (xn @ w_q).reshape(b, s, SB_HEADS, SB_HEAD_DIM).transpose(0, 2, 1, 3) * (1.0 / math.sqrt(SB_HEAD_DIM))
    loc = jnp.arange(SB_QBLOCK)
    tri = (loc[:, None] >= loc[None, :]).astype(jnp.float32)
    outs = []
    for i in range(nq):
        nk = i + 1
        qi = q[:, :, i * SB_QBLOCK:(i + 1) * SB_QBLOCK]
        kb = k_sh[:, :, :nk * SB_QBLOCK].reshape(b, SB_HEADS, nk, SB_QBLOCK, SB_HEAD_DIM)
        vb = v_sh[:, :, :nk * SB_QBLOCK].reshape(b, SB_HEADS, nk, SB_QBLOCK, SB_HEAD_DIM)
        z = jnp.einsum('bhqd,bhnsd->bhqns', qi, kb).astype(jnp.float32)
        s_pos = jnp.arange(nk * SB_QBLOCK).reshape(nk, SB_QBLOCK)
        t_pos = i * SB_QBLOCK + loc
        mask = s_pos[None, :, :] < t_pos[:, None, None]
        log_keep = jnp.where(mask, jax.nn.log_sigmoid(-z), 0.0)
        cs_in = jnp.einsum('bhqnj,js->bhqns', log_keep, tri)
        blk = cs_in[..., 0]
        after = lax.cumsum(blk, axis=3, reverse=True) - blk
        a = jnp.where(mask, jnp.exp(z + cs_in + after[..., None]), 0.0)
        outs.append(jnp.einsum('bhqns,bhnsd->bhqd', a.astype(vb.dtype), vb))
    o = jnp.concatenate(outs, axis=2)
    o = o.transpose(0, 2, 1, 3).reshape(b, s, SB_DIM)
    return o @ w_out

def peer_ffn(xn, w_q, subkeys, u, v):
    b, s, d = xn.shape
    t = b * s
    nb = t // PEER_TOKEN_BLOCK
    xt = xn.reshape(t, d)
    qr = (xt @ w_q).reshape(t, PEER_HEADS, 2, PEER_DK // 2)
    sc = jnp.einsum('thpd,hpnd->thpn', qr, subkeys).astype(jnp.float32)
    s1, i1 = lax.top_k(sc[:, :, 0], PEER_TOPK)
    s2, i2 = lax.top_k(sc[:, :, 1], PEER_TOPK)
    cand = (s1[..., :, None] + s2[..., None, :]).reshape(t, PEER_HEADS, PEER_TOPK * PEER_TOPK)
    best, flat = lax.top_k(cand, PEER_TOPK)
    e1 = jnp.take_along_axis(i1, flat // PEER_TOPK, axis=-1)
    e2 = jnp.take_along_axis(i2, flat % PEER_TOPK, axis=-1)
    experts = (e1 * PEER_NKEYS + e2).reshape(nb, PEER_TOKEN_BLOCK, PEER_HEADS * PEER_TOPK)
    gates = jax.nn.softmax(best, axis=-1).reshape(nb, PEER_TOKEN_BLOCK, PEER_HEADS * PEER_TOPK)

    def block(args):
        xc, ec, gc = args
        hid = jnp.einsum('cd,ced->ce', xc, jnp.take(u, ec, axis=0)).astype(jnp.float32)
        w = (gc * jax.nn.gelu(hid, approximate=False)).astype(xc.dtype)
        return jnp.einsum('ce,ced->cd', w, jnp.take(v, ec, axis=0))

    out = lax.map(block, (xt.reshape(nb, PEER_TOKEN_BLOCK, d), experts, gates))
    return out.reshape(b, s, d)

def first_inputs(seed: int = 0) -> dict:
    key = jax.random.key(seed)
    ks = jax.random.split(key, 22)
    D = D_MODEL

    def nrm(k, shape, std):
        return jax.random.normal(k, shape, jnp.float32) * std

    return {
        'x': nrm(ks[0], (BATCH, SEQ, D), 1.0),
        'c': nrm(ks[1], (BATCH, D), 1.0),
        'ada_w': nrm(ks[2], (DEPTH, D, 6 * D), 0.5 * D ** -0.5),
        'ada_b': nrm(ks[3], (DEPTH, 6 * D), 0.02),
        'norm_mix_g': 1.0 + nrm(ks[4], (DEPTH, D), 0.02),
        'norm_ffn_g': 1.0 + nrm(ks[5], (DEPTH, D), 0.02),
        'hgrn_w_in': nrm(ks[6], (N_A, D, 2 * HGRN_FDIM + 2 * D), D ** -0.5),
        'hgrn_lb_logits': nrm(ks[7], (N_A + 1, HGRN_FDIM), 0.5),
        'hgrn_onorm_g': 1.0 + nrm(ks[8], (N_A, D), 0.02),
        'hgrn_w_out': nrm(ks[9], (N_A, D, D), D ** -0.5),
        'kv_ada_w': nrm(ks[10], (D, 2 * D), 0.5 * D ** -0.5),
        'kv_ada_b': nrm(ks[11], (2 * D,), 0.02),
        'kv_norm_g': 1.0 + nrm(ks[12], (D,), 0.02),
        'kv_w': nrm(ks[13], (D, 2 * SB_DIM), D ** -0.5),
        'sb_w_q': nrm(ks[14], (N_B, D, SB_DIM), D ** -0.5),
        'sb_w_out': nrm(ks[15], (N_B, SB_DIM, D), SB_DIM ** -0.5),
        'peer_w_q': nrm(ks[16], (DEPTH, D, PEER_HEADS * PEER_DK), D ** -0.5),
        'peer_subkeys': nrm(ks[17], (DEPTH, PEER_HEADS, 2, PEER_NKEYS, PEER_DK // 2), (PEER_DK // 2) ** -0.5),
        'peer_u': nrm(ks[18], (DEPTH, PEER_N, D), D ** -0.5),
        'peer_v': nrm(ks[19], (DEPTH, PEER_N, D), PEER_HEADS ** -0.5),
        'final_norm_g': 1.0 + nrm(ks[20], (D,), 0.02),
    }

def first_block(x, c, ada_w, ada_b, norm_mix_g, norm_ffn_g, hgrn_w_in, hgrn_lb_logits,
              hgrn_onorm_g, hgrn_w_out, kv_ada_w, kv_ada_b, kv_norm_g, kv_w, sb_w_q,
              sb_w_out, peer_w_q, peer_subkeys, peer_u, peer_v, final_norm_g):
    c_act = jax.nn.silu(c)
    lb_all = jnp.cumsum(jax.nn.softmax(hgrn_lb_logits.astype(jnp.float32), axis=0), axis=0)
    h = x
    k_sh = None
    v_sh = None
    for l in range(DEPTH):
        mod = c_act @ ada_w[l] + ada_b[l]
        sh1, sc1, g1, sh2, sc2, g2 = jnp.split(mod, 6, axis=-1)
        hn = modulate(rms_norm(h, norm_mix_g[l]), sh1, sc1)
        if l < N_A:
            mix = hgrn2_mixer(hn, hgrn_w_in[l], lb_all[l], hgrn_onorm_g[l], hgrn_w_out[l])
        else:
            mix = stick_breaking_mixer(hn, k_sh, v_sh, sb_w_q[l - N_A], sb_w_out[l - N_A])
        h = h + g1[:, None, :] * mix
        hn = modulate(rms_norm(h, norm_ffn_g[l]), sh2, sc2)
        h = h + g2[:, None, :] * peer_ffn(hn, peer_w_q[l], peer_subkeys[l], peer_u[l], peer_v[l])
        if l == N_A - 1:
            k_sh, v_sh = shared_kv(h, c_act, kv_ada_w, kv_ada_b, kv_norm_g, kv_w)
    return rms_norm(h, final_norm_g)


DEPTH_2 = 1

CONV_CH = 512
CONV_WIDTH = 31
N_HEADS = 8
N_KV_HEADS = 2
HEAD_DIM = 64
WINDOW = 128
ATTN_BLOCK = 128
N_GROUPS = 4
EXPERTS_PER_GROUP = 8
N_EXPERTS = N_GROUPS * EXPERTS_PER_GROUP
EXPERT_TOP_K = 2
D_FF_EXPERT = 512
MOE_BLOCK = 128

Q_DIM = N_HEADS * HEAD_DIM
KV_DIM = N_KV_HEADS * HEAD_DIM
IN_COLS = 2 * CONV_CH + Q_DIM + 2 * KV_DIM + 2 * D_MODEL


def rms_norm_2(x, g):
    xf = x.astype(jnp.float32)
    y = xf * lax.rsqrt(jnp.mean(xf * xf, axis=-1, keepdims=True) + NORM_EPS)
    return (y * g.astype(jnp.float32)).astype(x.dtype)

def layer_norm(x, g, b):
    xf = x.astype(jnp.float32)
    mu = jnp.mean(xf, axis=-1, keepdims=True)
    var = jnp.mean(jnp.square(xf - mu), axis=-1, keepdims=True)
    y = (xf - mu) * lax.rsqrt(var + NORM_EPS)
    return (y * g.astype(jnp.float32) + b.astype(jnp.float32)).astype(x.dtype)

def alibi_slopes():
    return jnp.asarray(np.array([2.0 ** (-8.0 * (h + 1) / N_HEADS) for h in range(N_HEADS)], np.float32))

def conformer_conv(u, w_dw, b_dw, ln_g, ln_b):
    a, gate = jnp.split(u, 2, axis=-1)
    v = a * jax.nn.sigmoid(gate)
    y = lax.conv_general_dilated(
        v, w_dw, window_strides=(1,), padding=[(CONV_WIDTH - 1, 0)],
        dimension_numbers=("NWC", "WIO", "NWC"), feature_group_count=CONV_CH)
    y = y + b_dw
    return jax.nn.silu(layer_norm(y, ln_g, ln_b))

def sliding_window_attention(q, k, v, sinks):
    b, s = q.shape[0], q.shape[1]
    nb = s // ATTN_BLOCK
    grp = N_HEADS // N_KV_HEADS
    qb = q.reshape(b, nb, ATTN_BLOCK, N_KV_HEADS, grp, HEAD_DIM)
    kb = k.reshape(b, nb, ATTN_BLOCK, N_KV_HEADS, HEAD_DIM)
    vb = v.reshape(b, nb, ATTN_BLOCK, N_KV_HEADS, HEAD_DIM)

    def with_prev(t):
        prev = jnp.pad(t[:, :-1], ((0, 0), (1, 0), (0, 0), (0, 0), (0, 0)))
        return jnp.concatenate([prev, t], axis=2)

    kk, vv = with_prev(kb), with_prev(vb)
    scores = jnp.einsum("bnqhgd,bnkhd->bnhgqk", qb, kk,
                        preferred_element_type=jnp.float32) * (HEAD_DIM ** -0.5)
    qi = jnp.arange(ATTN_BLOCK)[:, None]
    kj = jnp.arange(2 * ATTN_BLOCK)[None, :]
    rel = ATTN_BLOCK + qi - kj
    in_window = (rel >= 0) & (rel < WINDOW)
    key_exists = (jnp.arange(nb)[:, None, None] * ATTN_BLOCK + kj[None] - ATTN_BLOCK) >= 0
    mask = in_window[None] & key_exists
    slopes = alibi_slopes().reshape(N_KV_HEADS, grp)
    scores = scores - slopes[:, :, None, None] * rel.astype(jnp.float32)
    scores = jnp.where(mask[None, :, None, None], scores, -jnp.inf)
    sink = sinks.astype(jnp.float32).reshape(N_KV_HEADS, grp)[None, None, :, :, None, None]
    m = jnp.maximum(jnp.max(scores, axis=-1, keepdims=True), sink)
    p = jnp.exp(scores - m)
    p = p / (jnp.sum(p, axis=-1, keepdims=True) + jnp.exp(sink - m))
    out = jnp.einsum("bnhgqk,bnkhd->bnqhgd", p.astype(v.dtype), vv)
    return out.reshape(b, s, Q_DIM)

def hierarchical_moe(xn, w_group, b_group, w_expert, b_expert, w_gate, w_up, w_down):
    b, s, d = xn.shape
    t = b * s
    xt = xn.reshape(t, d)
    g_logits = (xt @ w_group).astype(jnp.float32) + b_group.astype(jnp.float32)
    g_prob = jax.nn.softmax(g_logits, axis=-1)
    g_sel = jnp.argmax(g_logits, axis=-1).astype(jnp.int32)
    p_group = jnp.take_along_axis(g_prob, g_sel[:, None], axis=-1)[:, 0]
    e_logits = ((xt @ w_expert).astype(jnp.float32) + b_expert.astype(jnp.float32)).reshape(t, N_GROUPS, EXPERTS_PER_GROUP)
    e_in = jnp.take_along_axis(e_logits, g_sel[:, None, None], axis=1)[:, 0]
    top_val, top_idx = lax.top_k(e_in, EXPERT_TOP_K)
    weights = p_group[:, None] * jax.nn.softmax(top_val, axis=-1)
    expert_id = (g_sel[:, None] * EXPERTS_PER_GROUP + top_idx.astype(jnp.int32)).reshape(-1)
    token_id = jnp.repeat(jnp.arange(t, dtype=jnp.int32), EXPERT_TOP_K)
    w_flat = weights.reshape(-1)
    n_assign = t * EXPERT_TOP_K
    n_blocks = -(-(n_assign + N_EXPERTS * (MOE_BLOCK - 1)) // MOE_BLOCK)
    order = jnp.argsort(expert_id, stable=True)
    sorted_e = expert_id[order]
    counts = jnp.zeros((N_EXPERTS,), jnp.int32).at[expert_id].add(1)
    padded = ((counts + MOE_BLOCK - 1) // MOE_BLOCK) * MOE_BLOCK
    padded_ends = jnp.cumsum(padded)
    padded_starts = padded_ends - padded
    starts = jnp.cumsum(counts) - counts
    rank = jnp.arange(n_assign, dtype=jnp.int32) - starts[sorted_e]
    dest = padded_starts[sorted_e] + rank
    slot_token = jnp.zeros((n_blocks * MOE_BLOCK,), jnp.int32).at[dest].set(token_id[order])
    slot_w = jnp.zeros((n_blocks * MOE_BLOCK,), jnp.float32).at[dest].set(w_flat[order])
    block_start = jnp.arange(n_blocks, dtype=jnp.int32) * MOE_BLOCK
    block_expert = jnp.clip(jnp.searchsorted(padded_ends, block_start, side="right"), 0, N_EXPERTS - 1).astype(jnp.int32)

    def run_block(args):
        tok, wt, e = args
        xb = xt[tok]
        hmid = jax.nn.silu(xb @ w_gate[e]) * (xb @ w_up[e])
        return (hmid @ w_down[e]) * wt[:, None].astype(xb.dtype)

    ys = lax.map(run_block, (slot_token.reshape(n_blocks, MOE_BLOCK),
                             slot_w.reshape(n_blocks, MOE_BLOCK), block_expert))
    out = jnp.zeros((t, d), xn.dtype).at[slot_token].add(ys.reshape(-1, d))
    return out.reshape(b, s, d)

def second_inputs(seed: int = 0) -> dict:
    key = jax.random.key(seed)
    ks = jax.random.split(key, 24)
    f32 = jnp.float32

    def nrm(k, shape, scale):
        return jax.random.normal(k, shape, f32) * scale

    L = DEPTH_2
    return {
        "x": jax.random.normal(ks[0], (BATCH, SEQ, D_MODEL), f32),
        "g_mix": 1.0 + nrm(ks[1], (L, D_MODEL), 0.02),
        "w_in": nrm(ks[2], (L, D_MODEL, IN_COLS), D_MODEL ** -0.5),
        "w_dw": nrm(ks[3], (L, CONV_WIDTH, 1, CONV_CH), CONV_WIDTH ** -0.5),
        "b_dw": nrm(ks[4], (L, CONV_CH), 0.02),
        "ln_conv_g": 1.0 + nrm(ks[5], (L, CONV_CH), 0.02),
        "ln_conv_b": nrm(ks[6], (L, CONV_CH), 0.02),
        "sinks": nrm(ks[7], (L, N_HEADS), 0.5),
        "w_conv_out": nrm(ks[8], (L, CONV_CH, D_MODEL), CONV_CH ** -0.5),
        "w_attn_out": nrm(ks[9], (L, Q_DIM, D_MODEL), Q_DIM ** -0.5),
        "w_out": nrm(ks[10], (L, D_MODEL, D_MODEL), D_MODEL ** -0.5),
        "g_ffn": 1.0 + nrm(ks[11], (L, D_MODEL), 0.02),
        "w_group": nrm(ks[12], (L, D_MODEL, N_GROUPS), D_MODEL ** -0.5),
        "b_group": nrm(ks[13], (L, N_GROUPS), 0.01),
        "w_expert": nrm(ks[14], (L, D_MODEL, N_EXPERTS), D_MODEL ** -0.5),
        "b_expert": nrm(ks[15], (L, N_EXPERTS), 0.01),
        "w_gate": nrm(ks[16], (L, N_EXPERTS, D_MODEL, D_FF_EXPERT), D_MODEL ** -0.5),
        "w_up": nrm(ks[17], (L, N_EXPERTS, D_MODEL, D_FF_EXPERT), D_MODEL ** -0.5),
        "w_down": nrm(ks[18], (L, N_EXPERTS, D_FF_EXPERT, D_MODEL), D_FF_EXPERT ** -0.5),
        "g_final": 1.0 + nrm(ks[19], (D_MODEL,), 0.02),
    }

def second_block(x, g_mix, w_in, w_dw, b_dw, ln_conv_g, ln_conv_b, sinks, w_conv_out, w_attn_out,
              w_out, g_ffn, w_group, b_group, w_expert, b_expert, w_gate, w_up, w_down, g_final):
    b, s, _ = x.shape
    cuts = list(np.cumsum([2 * CONV_CH, Q_DIM, KV_DIM, KV_DIM, D_MODEL]))
    h = x
    for l in range(DEPTH_2):
        xn = rms_norm_2(h, g_mix[l])
        proj = xn @ w_in[l]
        u_conv, q, k, v, gate_conv, gate_attn = jnp.split(proj, cuts, axis=-1)
        conv_o = conformer_conv(u_conv, w_dw[l], b_dw[l], ln_conv_g[l], ln_conv_b[l]) @ w_conv_out[l]
        attn = sliding_window_attention(q.reshape(b, s, N_HEADS, HEAD_DIM),
                                        k.reshape(b, s, N_KV_HEADS, HEAD_DIM),
                                        v.reshape(b, s, N_KV_HEADS, HEAD_DIM), sinks[l])
        attn_o = attn @ w_attn_out[l]
        merged = jax.nn.sigmoid(gate_conv) * conv_o + jax.nn.sigmoid(gate_attn) * attn_o
        h = h + merged @ w_out[l]
        h = h + hierarchical_moe(rms_norm_2(h, g_ffn[l]), w_group[l], b_group[l], w_expert[l],
                                 b_expert[l], w_gate[l], w_up[l], w_down[l])
    return rms_norm_2(h, g_final)


def setup_inputs(seed=0):
    out = dict(first_inputs(seed))
    for name, value in second_inputs(seed + 1).items():
        if name != "x":
            out[name + "_2"] = value
    return out


def reference(
    x, c, ada_w, ada_b, norm_mix_g, norm_ffn_g, hgrn_w_in, hgrn_lb_logits, hgrn_onorm_g,
    hgrn_w_out, kv_ada_w, kv_ada_b, kv_norm_g, kv_w, sb_w_q, sb_w_out, peer_w_q, peer_subkeys,
    peer_u, peer_v, final_norm_g, g_mix_2, w_in_2, w_dw_2, b_dw_2, ln_conv_g_2, ln_conv_b_2,
    sinks_2, w_conv_out_2, w_attn_out_2, w_out_2, g_ffn_2, w_group_2, b_group_2, w_expert_2,
    b_expert_2, w_gate_2, w_up_2, w_down_2, g_final_2,
):
    x = first_block(
        x, c, ada_w, ada_b, norm_mix_g, norm_ffn_g, hgrn_w_in, hgrn_lb_logits, hgrn_onorm_g,
        hgrn_w_out, kv_ada_w, kv_ada_b, kv_norm_g, kv_w, sb_w_q, sb_w_out, peer_w_q,
        peer_subkeys, peer_u, peer_v, final_norm_g,
    )
    return second_block(
        x, g_mix_2, w_in_2, w_dw_2, b_dw_2, ln_conv_g_2, ln_conv_b_2, sinks_2, w_conv_out_2,
        w_attn_out_2, w_out_2, g_ffn_2, w_group_2, b_group_2, w_expert_2, b_expert_2, w_gate_2,
        w_up_2, w_down_2, g_final_2,
    )


_drawn_inputs = setup_inputs


def setup_inputs(seed=0):
    import zlib

    import numpy as np

    out = dict(_drawn_inputs(seed))
    spreads = {}
    factors = {'norm_mix_g': 3.157,
     'norm_ffn_g': 3.292,
     'hgrn_onorm_g': 2.845,
     'kv_ada_b': 3.149,
     'kv_norm_g': 3.787,
     'ln_conv_g_2': 2.969,
     'ln_conv_b_2': 3.198,
     'sinks_2': 3.951,
     'b_expert_2': 9.667,
     'b_group_2': 3.629}
    for name, (base, spread) in spreads.items():
        noise = np.random.default_rng([zlib.crc32(name.encode()), seed]).standard_normal(out[name].shape)
        drawn = base * np.exp(spread * noise) if base else spread * noise
        out[name] = __import__('jax').numpy.asarray(drawn.astype(out[name].dtype))
    for name, factor in factors.items():
        out[name] = (out[name] * factor).astype(out[name].dtype)
    return out
```

```python
import concourse.bass as bass
from concourse import mybir
from contextlib import ExitStack

F32 = mybir.dt.float32
I32 = mybir.dt.int32
U32 = mybir.dt.uint32
ALU = mybir.AluOpType
ACT = mybir.ActivationFunctionType
AXIS_X = mybir.AxisListType.X

P = 128
D = 1024
SEQ = 512
TT = SEQ // P
KD = D // P
EPS = 1e-6
HEADS = 8
CHUNK = 16
CPT = P // CHUNK
PH = 4
PK = 16
NKEYS = 128
NSEL = PH * PK
GR = 4
NEG = -1e30


def build_program(nc, A, out):
    ctx = ExitStack()
    with ctx:
        sems = {}

        def sem(name):
            if name not in sems:
                sems[name] = ctx.enter_context(nc.semaphore(name))
            return sems[name]

        REG = TT * D
        layout, at = {}, 0
        for name, words in (("h", REG), ("w0", REG), ("w1", REG), ("moda", 6 * D), ("r0", REG), ("r1", REG),
                            ("r2", REG), ("r3", REG), ("r4", REG), ("r5", REG), ("r6", REG), ("t", 3 * D),
                            ("ident", P), ("ones", P), ("negones", P), ("negtri", P), ("before", P),
                            ("chunk_causal", P), ("not_first", SEQ), ("c_rep", KD * P), ("cols", 128), ("iota", 64),
                            ("tiny", 384)):
            layout[name] = at
            at += words
        WORDS = at
        arena = ctx.enter_context(nc.sbuf_tensor("arena", [P, WORDS], F32))
        psum = ctx.enter_context(nc.psum_tensor("psum", [P, 8, 512], F32))

        def mem(name, off, *dims, parts=(0, P), dt=None):
            pat, step = [], 1
            for d in reversed(dims):
                if isinstance(d, tuple):
                    pat.append([d[0], d[1]])
                    step = d[0] * d[1]
                else:
                    pat.append([step, d])
                    step *= d
            ap = bass.AP(arena, parts[0] * WORDS + layout[name] + off, [[WORDS, parts[1]]] + pat[::-1])
            return ap if dt is None else ap.bitcast(dt)

        def bank(b, off=0, *dims, parts=(0, P)):
            pat, step = [], 1
            for d in reversed(dims or (512,)):
                if isinstance(d, tuple):
                    pat.append([d[0], d[1]])
                    step = d[0] * d[1]
                else:
                    pat.append([step, d])
                    step *= d
            return bass.AP(psum, parts[0] * 4096 + b * 512 + off, [[4096, parts[1]]] + pat[::-1])

        ident = mem("ident", 0, P)
        ones = mem("ones", 0, P)
        W = [mem("w0", 0, KD, 512), mem("w1", 0, KD, 512)]

        def wslot(i):
            return W[i % 2]

        COL_EPS, COL_LB, COL_OMLB, COL_ON, COL_EVEN, COL_ODD, COL_L0, COL_L1 = 0, 8, 16, 24, 32, 33, 40, 48
        COL_SS, COL_RMS, COL_RSTD = 56, 60, 64
        col = lambda c, n=1: mem("cols", c, n)

        stream = []

        def w_cols(ap, n0, n=512):
            return ap.rearrange("(k p) n -> p k n", p=P)[:, :, n0:n0 + n]

        marks = {}

        def add(name, items):
            marks[name] = len(stream)
            stream.extend(items)

        ada, kva, win = A["ada_w"], A["kv_ada_w"], A["hgrn_w_in"]
        add("mod0", [w_cols(ada[0], 512 * j) for j in range(12)])
        add("hgrn_in", [w_cols(win[0], D * part + 512 * c) for part in (1, 0, 2, 3) for c in range(2)])
        add("hgrn_out", [w_cols(A["hgrn_w_out"][0], 512 * c) for c in range(2)])
        add("peer_q0", [w_cols(A["peer_w_q"][0], 512 * c) for c in range(2)])
        add("mod1", [w_cols(kva, 512 * j) for j in range(4)] + [w_cols(ada[1], 512 * j) for j in range(12)])
        add("kv", [w_cols(A["kv_w"], 512 * c) for c in range(4)])
        add("sb_q", [w_cols(A["sb_w_q"][0], 512 * c) for c in range(2)])
        add("sb_out", [w_cols(A["sb_w_out"][0], 512 * c) for c in range(2)])
        add("peer_q1", [w_cols(A["peer_w_q"][1], 512 * c) for c in range(2)])
        w2 = A["w_in_2"][0]
        w2q = w2.rearrange("(k p) n -> p k n", p=P)[:, :, 1024:1536].rearrange("p k (a j c) -> a p k j c", a=2, c=64)
        add("in2", [w_cols(w2, 0), w_cols(w2, 512), w2q, w_cols(w2, 1536, 256)]
            + [w_cols(w2, 1792 + 512 * c) for c in range(4)])
        add("conv_out", [A["w_conv_out_2"][0].rearrange("(k p) n -> p k n", p=P)])
        add("attn_out", [A["w_attn_out_2"][0].rearrange("(a j p) n -> a p j n", a=2, p=64)])
        add("out2", [w_cols(A["w_out_2"][0], 512 * c) for c in range(2)])

        def load_weights(sp):
            for i, src in enumerate(stream):
                if i >= 2:
                    sp.wait_ge(sem("w_used"), i - 1)
                for l in range(2):
                    if 0 <= i - MOD_W[l] < len(MODS[l]):
                        mod_bias_dma(sp, l, i - MOD_W[l])
                if i == marks["in2"] + 2:
                    dst = wslot(i).rearrange("p k (j a c) -> p k j a c", a=2, c=64)
                    for a in range(2):
                        for k in range(KD):
                            sp.dma_start(dst[:, k, :, a, :], src[a][:, k]).then_inc(sem(f"w_ready{i % 2}"), 16)
                    continue
                if i == marks["attn_out"]:
                    dst = wslot(i).rearrange("p k n -> p (k n)").rearrange("p (j n) -> p j n", n=D)
                    for a in range(2):
                        sp.dma_start(dst[64 * a:64 * a + 64], src[a]).then_inc(sem(f"w_ready{i % 2}"), 16)
                    continue
                dst = wslot(i)
                if i == marks["conv_out"]:
                    dst = dst.rearrange("p k n -> p (k n)").rearrange("p (j n) -> p j n", n=D)
                elif src.shape[2] != 512:
                    dst = dst[:, :, 0:src.shape[2]]
                sp.dma_start(dst, src).then_inc(sem(f"w_ready{i % 2}"), 16)

        def w_arrived(pe, i):
            n = i // 2 + 1
            for c, more in ((marks["in2"] + 2, 2 * KD - 1), (marks["attn_out"], 1)):
                if i >= c and i % 2 == c % 2:
                    n += more
            pe.wait_ge(sem(f"w_ready{i % 2}"), 16 * n)

        ENG = ("pe", "act", "dve", "pool")

        def enter(eng, n):
            if n:
                for e in ENG:
                    eng.wait_ge(sem(f"left_{e}"), n)

        def leave(eng, who):
            eng.drain().then_inc(sem(f"left_{who}"), 1)

        chained = {"dve": 0, "act": 0, "pool": 0}

        def linker(eng, who):
            def link(ins):
                chained[who] += 1
                ins.then_inc(sem(f"chain_{who}"), 1)
                eng.wait_ge(sem(f"chain_{who}"), chained[who])
            return link

        def matmuls(pe, o, lhs, rhs, n, start=True, stop=True):
            for k in range(n):
                last = pe.matmul(o, lhsT=lhs(k), rhs=rhs(k), start=start and k == 0, stop=stop and k == n - 1)
            return last

        H = lambda t, n0=0, n=D: mem("h", t * D + n0, n)
        MOD0 = dict(sh1=("moda", 0), sc1=("moda", 1), g1=("moda", 2), sh2=("moda", 3), sc2=("moda", 4), g2=("moda", 5))
        names1 = ["shkv", "sckv", "sh1", "sc1", "g1", "sh2", "sc2", "g2"]
        MOD1 = {n: ("r5", i) for i, n in enumerate(names1)}
        mod = lambda m, n0=0, n=D: mem(m[0], m[1] * D + n0, n)

        def bias_row(l, j):
            return A["ada_b"][l:l + 1, 512 * j:512 * j + 512]

        MODS = {0: [(bias_row(0, j), MOD0[n], half, n[:2] == "sc") for j in range(12)
                    for n, half in [(["sh1", "sc1", "g1", "sh2", "sc2", "g2"][j // 2], j % 2)]],
                1: [((A["kv_ada_b"].rearrange("(a n) -> a n", a=1)[:, 512 * j:512 * j + 512] if j < 4 else bias_row(1, j - 4)),
                     MOD1[names1[j // 2]], j % 2, names1[j // 2][:2] == "sc") for j in range(16)]}
        MOD_BANKS = {0: (0, 1), 1: (0, 1)}
        MOD_ROWS = {0: lambda i: mem("t", 2 * D + 512 * (i % 2), 512, parts=(0, 1)),
                    1: lambda i: mem("not_first", 0, 512, parts=(0, 1)) if i % 2 else mem("moda", 4 * D + 512, 512, parts=(0, 1))}
        MOD_W = {0: marks["mod0"], 1: marks["mod1"]}

        def mod_pe(pe, l, js):
            for j in js:
                g = j + 12 * l
                if g >= 2:
                    pe.wait_ge(sem("mod_out"), g - 1)
                pe.wait_ge(sem(f"mod_bias{g % 2}"), 16 * (g // 2 + 1))
                w_arrived(pe, MOD_W[l] + j)
                w = wslot(MOD_W[l] + j)
                o = bank(MOD_BANKS[l][j % 2])
                matmuls(pe, o, lambda k: mem("c_rep", k * P, P), lambda k: w[:, k, :], KD, stop=False)\
                    .then_inc(sem("w_used"), 1)
                pe.matmul(o, lhsT=mem("ones", 0, P, parts=(0, 1)), rhs=MOD_ROWS[l](j), start=False, stop=True)\
                    .then_inc(sem("mod_sum"), 1)

        def mod_act(act, l, js):
            for j in js:
                g = j + 12 * l
                _, slot, half, is_scale = MODS[l][j]
                act.wait_ge(sem("mod_sum"), g + 1)
                act.activation(mod(slot, 512 * half, 512), bank(MOD_BANKS[l][j % 2]), ACT.Identity,
                               bias=col(COL_EPS + 1) if is_scale else 0.0).then_inc(sem("mod_out"), 1)

        def mod_bias_dma(eng, l, j):
            g = j + 12 * l
            if g >= 2:
                eng.wait_ge(sem("mod_sum"), g - 1)
            if l == 1 and j == 0:
                eng.wait_ge(sem("norm_xn"), 2 * TT)
            eng.dma_start(MOD_ROWS[l](j), MODS[l][j][0]).then_inc(sem(f"mod_bias{g % 2}"), 16)

        def setup_sp(sp):
            sp.dma_start(mem("tiny", 0, KD), A["c"][0].rearrange("(k p) -> p k", p=P),
                         allow_slow_non_contiguous=True).then_inc(sem("c_in"), 16)

        def setup_pool(pool):
            pool.memset(mem("ones", 0, P), 1.0)
            pool.memset(mem("negones", 0, P), -1.0)
            pool.memset(mem("ident", 0, P), 0.0)
            pool.memset(mem("not_first", 0, SEQ), 1.0)
            pool.memset(mem("cols", COL_EPS, 1), EPS)
            pool.memset(mem("cols", COL_EPS + 1, 1), 1.0)
            pool.iota(mem("iota", 0, 64), pattern=[[1, 64]], base=0, channel_multiplier=0,
                      allow_small_or_imprecise_dtypes=True)
            pool.iota(mem("tiny", 16, 1, dt=I32), pattern=[[1, 1]], base=0, channel_multiplier=1)
            pool.memset(mem("chunk_causal", 0, P, dt=I32), 1)
            pool.memset(mem("r1", 0, D), 0.0)
            link = linker(pool, "pool")
            link(pool.memset(mem("tiny", 17, 1), 0.0))
            pool.affine_select(out=ident, in_=ident, compare_op=ALU.not_equal, fill=1.0, base=0,
                               pattern=[[-1, P]], channel_multiplier=1)
            nf = mem("not_first", 0, SEQ // CHUNK, CHUNK)
            pool.affine_select(out=nf, in_=nf, compare_op=ALU.not_equal, fill=0.0, base=0,
                               pattern=[[0, SEQ // CHUNK], [1, CHUNK]], channel_multiplier=0)
            pool.affine_select(out=mem("negtri", 0, P), in_=mem("negones", 0, P), compare_op=ALU.is_ge, fill=0.0,
                               base=0, pattern=[[-1, P]], channel_multiplier=1)
            pool.affine_select(out=mem("before", 0, P), in_=ones, compare_op=ALU.is_gt, fill=0.0,
                               base=0, pattern=[[1, P]], channel_multiplier=-1)
            cc = mem("chunk_causal", 0, CPT, CHUNK, dt=I32)
            link(pool.affine_select(out=cc, in_=cc, compare_op=ALU.is_ge, fill=0.0, base=0,
                                    pattern=[[-CHUNK, CPT], [0, CHUNK]], channel_multiplier=1))
            pool.affine_select(out=cc, in_=cc, compare_op=ALU.is_ge, fill=0.0, base=0,
                               pattern=[[CHUNK, CPT], [1, CHUNK]], channel_multiplier=-1)
            pool.drain().then_inc(sem("consts"), 1)
            pool.wait_ge(sem("consts"), 1)
            zero_slots(pool)

        def setup_act(act):
            act.dma_start(mem("h", 0, TT, D), A["x"][0].rearrange("(t p) d -> p t d", p=P)).then_inc(sem("x_in"), 16)
            act.dma_start(mem("cols", COL_L0, 8), A["hgrn_lb_logits"][0].rearrange("(h p) -> p h", p=P),
                          allow_slow_non_contiguous=True).then_inc(sem("cols_in"), 16)
            act.dma_start(mem("cols", COL_L1, 8), A["hgrn_lb_logits"][1].rearrange("(h p) -> p h", p=P),
                          allow_slow_non_contiguous=True).then_inc(sem("cols_in"), 16)
            act.dma_start(mem("cols", COL_ON, 8), A["hgrn_onorm_g"][0].rearrange("(h p) -> p h", p=P),
                          allow_slow_non_contiguous=True).then_inc(sem("cols_in"), 16)
            act.dma_start(mem("t", 0, D), A["norm_mix_g"][0:1].broadcast_to([P, D])).then_inc(sem("g_in"), 16)
            act.dma_start(mem("t", D, D), A["norm_ffn_g"][0:1].broadcast_to([P, D])).then_inc(sem("g_in"), 16)
            act.wait_ge(sem("c_in"), 16)
            act.activation(mem("tiny", 8, KD), mem("tiny", 0, KD), ACT.Silu).then_inc(sem("c_silu"), 1)
            act.wait_ge(sem("lb_diff"), 1)
            act.activation(mem("cols", COL_LB, 8), mem("cols", COL_L0, 8), ACT.Sigmoid).then_inc(sem("lb"), 1)
            mod_act(act, 0, range(12))

        def setup_dve(dve):
            link = linker(dve, "dve")
            dve.wait_ge(sem("c_silu"), 1)
            dve.tensor_copy(mem("c_rep", 0, KD, P), mem("tiny", 8, (1, KD), (0, P))).then_inc(sem("c_rep"), 1)
            dve.wait_ge(sem("cols_in"), 48)
            dve.tensor_tensor(mem("cols", COL_L0, 8), mem("cols", COL_L0, 8), mem("cols", COL_L1, 8), ALU.subtract)\
               .then_inc(sem("lb_diff"), 1)
            dve.wait_ge(sem("consts"), 1)
            par = mem("tiny", 16, 1, dt=I32)
            link(dve.tensor_single_scalar(mem("tiny", 18, 1, dt=I32), par, CHUNK, ALU.bitwise_and))
            dve.tensor_scalar(mem("cols", COL_EVEN, 1), mem("tiny", 18, 1, dt=I32), 0.0, None, ALU.is_equal)
            dve.tensor_scalar(mem("cols", COL_ODD, 1), mem("tiny", 18, 1, dt=I32), float(CHUNK), None, ALU.is_equal)
            dve.wait_ge(sem("lb"), 1)
            dve.tensor_scalar(mem("cols", COL_OMLB, 8), mem("cols", COL_LB, 8), -1.0, 1.0, ALU.mult, ALU.add)
            dve.wait_ge(sem("g_in"), 32)
            dve.wait_ge(sem("mod_out"), 4)
            dve.tensor_tensor(mod(MOD0["sc1"]), mod(MOD0["sc1"]), mem("t", 0, D), ALU.mult)
            dve.wait_ge(sem("mod_out"), 10)
            dve.tensor_tensor(mod(MOD0["sc2"]), mod(MOD0["sc2"]), mem("t", D, D), ALU.mult)
            dve.wait_ge(sem("x_in"), 16)

        def setup_pe(pe):
            pe.wait_ge(sem("consts"), 1)
            pe.wait_ge(sem("c_rep"), 1)
            mod_pe(pe, 0, range(12))

        norms_turned = [0]

        def norm(n, scale, shift, xn, xT, dst_h=False):
            first = n * TT
            turned = norms_turned[0] * 2 * TT
            norms_turned[0] += xT is not None

            def act_part(act):
                for t in range(TT):
                    act.activation(mem("t", 2 * D, D), H(t), ACT.Square,
                                   accum_out=mem("cols", COL_SS + t, 1)).then_inc(sem("norm_sq"), 1)
                    act.wait_ge(sem("norm_sq"), first + t + 1)
                act.activation(mem("cols", COL_RMS, TT), mem("cols", COL_SS, TT), ACT.Sqrt, scale=1.0 / D,
                               bias=col(COL_EPS)).then_inc(sem("norm_rms"), 1)
                if xT is not None:
                    for t in range(TT):
                        for a in range(2):
                            act.wait_ge(sem("norm_tr"), turned + 2 * t + a + 1)
                            act.activation(mem(xT, 4 * a * SEQ + t * P, (SEQ, 4), P),
                                           bank((2 * t + a) % 4, 0, 4, P), ACT.Copy).then_inc(sem("norm_xT"), 1)

            def dve_part(dve):
                link = linker(dve, "dve")
                dve.wait_ge(sem("norm_rms"), n + 1)
                link(dve.reciprocal(mem("cols", COL_RSTD, TT), mem("cols", COL_RMS, TT)))
                for t in range(TT):
                    if xT is not None and t >= 2:
                        dve.wait_ge(sem("norm_tr"), turned + 2 * (t - 1))
                    ins = dve.scalar_tensor_tensor(xn(t), H(t), mem("cols", COL_RSTD + t, 1), scale, ALU.mult, ALU.mult)
                    if shift is not None:
                        link(ins)
                        ins = dve.tensor_tensor(xn(t), xn(t), shift, ALU.add)
                    ins.then_inc(sem("norm_xn"), 1)

            def pe_part(pe):
                if xT is None:
                    return
                for t in range(TT):
                    pe.wait_ge(sem("norm_xn"), first + t + 1)
                    for a in range(2):
                        g = 2 * t + a
                        if g >= 4:
                            pe.wait_ge(sem("norm_xT"), turned + g - 3)
                        for j in range(4):
                            last = pe.transpose(bank(g % 4, j * P, P), xn(t)[:, (4 * a + j) * P:(4 * a + j + 1) * P], ident)
                        last.then_inc(sem("norm_tr"), 1)
            return dict(pe=pe_part, act=act_part, dve=dve_part)

        xn_temp = lambda t: mem("t", (t % 2) * D, D)
        XT = lambda r, k, t0=0, n=SEQ: mem(r, k * SEQ + t0, n)

        def out_proj(nth, first, lhs, kn, gate, n_chunks=2):
            banks = 8
            before = nth * n_chunks * TT

            def pe_part(pe):
                for c in range(n_chunks):
                    w_arrived(pe, first + c)
                    w = wslot(first + c)
                    for t in range(TT):
                        g = c * TT + t
                        ins = matmuls(pe, bank(g % banks), lambda k: lhs(k, t), lambda k: w[:, k, :], kn)
                        ins.then_inc(sem("proj_mm"), 1)
                    pe.drain().then_inc(sem("w_used"), 1)

            def dve_part(dve):
                link = linker(dve, "dve")
                for c in range(n_chunks):
                    for t in range(TT):
                        g = c * TT + t
                        dve.wait_ge(sem("proj_mm"), before + g + 1)
                        src = bank(g % banks)
                        if gate is not None:
                            tmp = mem("t", (g % 4) * 512, 512)
                            link(dve.tensor_tensor(tmp, src, mod(gate, 512 * c, 512), ALU.mult))
                            src = tmp
                        dve.tensor_tensor(H(t, 512 * c, 512), H(t, 512 * c, 512), src, ALU.add)
            return dict(pe=pe_part, dve=dve_part)

        FM = lambda r, h, t0=0, n=SEQ: mem(r, h * SEQ + t0, n)
        EXP_LAST = lambda h=0, n=HEADS: mem("tiny", 128 + h * 32, n * 32)

        def hgrn_in_pe(pe):
            c0 = marks["hgrn_in"]
            for c in range(8):
                w_arrived(pe, c0 + c)
                w = wslot(c0 + c)
                for j in range(4):
                    b = (4 * c + j) % 8
                    if 2 <= c < 4:
                        pe.wait_ge(sem("f_out"), 4 * (c - 2) + j + 1)
                    elif 4 <= c < 6:
                        pe.wait_ge(sem("q_out"), 4 * (c - 4) + j + 1)
                    elif c >= 6:
                        pe.wait_ge(sem("v_out"), 4 * (c - 6) + j + 1)
                    if 4 <= c < 6:
                        ins = matmuls(pe, bank(b), lambda k: XT("r0", k, j * P, P), lambda k: w[:, k, :], KD)
                    else:
                        ins = matmuls(pe, bank(b), lambda k: w[:, k, j * P:(j + 1) * P], lambda k: XT("r0", k), KD)
                    ins.then_inc(sem("hg_mm"), 1)
                pe.drain().then_inc(sem("w_used"), 1)

        def hgrn_in_act(act):
            act.wait_ge(sem("cleared"), 16 * N_CLEAR)
            for h in range(HEADS):
                act.wait_ge(sem("hg_mm"), h + 1)
                act.activation(FM("r1", h), bank(h), ACT.Sigmoid).then_inc(sem("f_out"), 1)
            for h in range(HEADS):
                act.wait_ge(sem("hg_mm"), 8 + h + 1)
                act.activation(FM("r3", h), bank(h), ACT.Silu).then_inc(sem("q_out"), 1)
            for h in range(HEADS):
                act.wait_ge(sem("fgate"), h + 1)
                act.activation(FM("r2", h), FM("r1", h), ACT.Ln).then_inc(sem("ln_f"), 1)
            for h in range(HEADS):
                act.wait_ge(sem("cum"), h + 1)
                if h >= 2:
                    act.wait_ge(sem("qd"), h - 1)
                act.activation(mem("t", (h % 2) * SEQ, SEQ), FM("r2", h), ACT.Exp).then_inc(sem("e_cum"), 1)
                act.activation(FM("r4", h), FM("r2", h), ACT.Exp, scale=-1.0)
                act.activation(EXP_LAST(h, 1), mem("r2", h * SEQ + CHUNK - 1, (CHUNK, SEQ // CHUNK)), ACT.Exp)\
                   .then_inc(sem("e_neg"), 1)
            for h in range(HEADS):
                act.wait_ge(sem("rest"), h + 1)
                act.activation(FM("r2", h), FM("r2", h), ACT.Exp).then_inc(sem("e_rest"), 1)
            for h in range(HEADS):
                act.wait_ge(sem("hg_mm"), 24 + h + 1)
                act.activation(FM("r5", h), bank(h), ACT.Silu)

        def hgrn_in_dve(dve):
            for h in range(HEADS):
                dve.wait_ge(sem("f_out"), h + 1)
                dve.tensor_scalar(FM("r1", h), FM("r1", h), mem("cols", COL_OMLB + h, 1), mem("cols", COL_LB + h, 1),
                                  ALU.mult, ALU.add).then_inc(sem("fgate"), 1)
            for h in range(HEADS):
                dve.wait_ge(sem("ln_f"), h + 1)
                dve.tensor_scalar(FM("r1", h), FM("r1", h), -1.0, 1.0, ALU.mult, ALU.add)
                dve.tensor_tensor_scan(FM("r2", h), mem("not_first", 0, SEQ), FM("r2", h), 0.0, ALU.mult, ALU.add)\
                   .then_inc(sem("cum"), 1)
            for c in range(8):
                dve.wait_ge(sem("hg_mm"), 16 + c + 1)
                dve.tensor_copy(mem("r6", (c % 4) * D + (c // 4) * 512, 512), bank(c)).then_inc(sem("v_out"), 1)
                h = c
                dve.wait_ge(sem("e_cum"), h + 1)
                dve.tensor_tensor(FM("r3", h), FM("r3", h), mem("t", (h % 2) * SEQ, SEQ), ALU.mult).then_inc(sem("qd"), 1)
                dve.wait_ge(sem("e_neg"), h + 1)
                dve.tensor_tensor(FM("r4", h), FM("r4", h), FM("r1", h), ALU.mult)
                x = mem("r2", h * SEQ, SEQ // CHUNK, CHUNK)
                last = mem("r2", h * SEQ + CHUNK - 1, (CHUNK, SEQ // CHUNK), (0, CHUNK))
                dve.tensor_tensor(mem("t", D + (h % 2) * SEQ, SEQ // CHUNK, CHUNK), last, x, ALU.subtract).then_inc(sem("rest_t"), 1)
                dve.wait_ge(sem("rest_t"), h + 1)
                dve.tensor_copy(FM("r2", h), mem("t", D + (h % 2) * SEQ, SEQ)).then_inc(sem("rest"), 1)
            for h in range(HEADS):
                dve.wait_ge(sem("e_rest"), h + 1)
                dve.tensor_tensor(FM("r1", h), FM("r1", h), FM("r2", h), ALU.mult)

        K2 = lambda par, h, n=1: mem("r0", par * D + h * P, n * P)
        STATE = lambda par, h, n=1: mem("r0", 2 * D + par * D + h * P, n * P)
        SCT = lambda h, n=1: mem("t", h * P, n * P)

        def hgrn_scan_pe(pe):
            upd = lambda step, a: 2 * step + a + 1
            for t in range(TT):
                for a in range(2):
                    if t:
                        pe.wait_ge(sem("k2_out"), 2 * (t - 1) + a + 1)
                    for j in range(4):
                        h = 4 * a + j
                        last = pe.matmul(bank(6 + a, j * P, P), lhsT=FM("r4", h, t * P, P), rhs=FM("r3", h, t * P, P),
                                         start=True, stop=True)
                    last.then_inc(sem("sc_mm"), 1)
                for a in range(2):
                    pe.wait_ge(sem("sc_out"), 2 * t + a + 1)
                    for j in range(4):
                        last = pe.transpose(bank(6 + a, j * P, P), FM("r1", 4 * a + j, t * P, P), ident)
                    last.then_inc(sem("k2_tr"), 1)
                for a in range(2):
                    if t:
                        pe.wait_ge(sem("o_out"), 2 * (t - 1) + a + 1)
                    for j in range(4):
                        h = 4 * a + j
                        last = pe.matmul(bank(a, j * P, P), lhsT=mem("r6", t * D + h * P, P), rhs=SCT(h),
                                         start=j == 0, stop=False, skip_group_check=True)
                    last.then_inc(sem("intra"), 1)
                pe.wait_ge(sem("k2_out"), 2 * t + 2)
                for n in range(CPT):
                    step = t * CPT + n
                    p0 = 32 * (n // 2)
                    for a in range(2):
                        b = 2 + 2 * (n % 2) + a
                        if step >= 2:
                            pe.wait_ge(sem("state"), upd(step - 2, a))
                        for j in range(4):
                            h = 4 * a + j
                            last = pe.matmul(bank(b, j * P, P),
                                             lhsT=mem("r0", (n % 2) * D + h * P, P, parts=(p0, 32)),
                                             rhs=mem("r6", t * D + h * P, P, parts=(p0, 32)), start=True, stop=True)
                        last.then_inc(sem("delta"), 1)
                    for a in range(2):
                        if step:
                            pe.wait_ge(sem("state"), upd(step - 1, a))
                        for j in range(4):
                            h = 4 * a + j
                            last = pe.matmul(bank(a, j * P + n * CHUNK, CHUNK), lhsT=STATE(n % 2, h),
                                             rhs=FM("r3", h, t * P + n * CHUNK, CHUNK),
                                             start=False, stop=j == 3 and n == CPT - 1, skip_group_check=True)
                        if n == CPT - 1:
                            last.then_inc(sem("o_mm"), 1)

        def hgrn_scan_act(act):
            for t in range(TT):
                for a in range(2):
                    act.wait_ge(sem("k2_tr"), 2 * t + a + 1)
                    if t and a == 0:
                        act.wait_ge(sem("delta"), 2 * CPT * t)
                    act.activation(K2(0, 4 * a, 4), bank(6 + a), ACT.Copy, scale=mem("cols", COL_EVEN, 1))
                    act.activation(K2(1, 4 * a, 4), bank(6 + a), ACT.Copy, scale=mem("cols", COL_ODD, 1))\
                       .then_inc(sem("k2_out"), 1)
                for a in range(2):
                    act.wait_ge(sem("o_mm"), 2 * t + a + 1)
                    act.activation(mem("r2", 4 * a * SEQ + t * P, (SEQ, 4), P), bank(a, 0, 4, P), ACT.Copy)\
                       .then_inc(sem("o_out"), 1)

        def hgrn_scan_dve(dve):
            dve.memset(STATE(0, 0, HEADS), 0.0)
            link = linker(dve, "dve")
            link(dve.memset(SCT(0, HEADS), 0.0))
            for t in range(TT):
                for a in range(2):
                    dve.wait_ge(sem("sc_mm"), 2 * t + a + 1)
                    if t and a == 0:
                        dve.wait_ge(sem("intra"), 2 * t)
                    dve.copy_predicated(mem("t", 4 * a * P, 4, P), mem("chunk_causal", 0, (0, 4), P, dt=I32),
                                        bank(6 + a, 0, 4, P)).then_inc(sem("sc_out"), 1)
                for n in range(CPT):
                    step = t * CPT + n
                    for a in range(2):
                        dve.wait_ge(sem("delta"), 2 * step + a + 1)
                        if step:
                            dve.wait_ge(sem("state"), 2 * (step - 1) + a + 1)
                        for j in range(4):
                            h = 4 * a + j
                            last = dve.scalar_tensor_tensor(STATE((n + 1) % 2, h), STATE(n % 2, h),
                                                            mem("tiny", 128 + h * 32 + step, 1),
                                                            bank(2 + 2 * (n % 2) + a, j * P, P), ALU.mult, ALU.add)
                        last.then_inc(sem("state"), 1)

        def hgrn_out_norm_act(act):
            for h in range(HEADS):
                if h >= 2:
                    act.wait_ge(sem("osq_mm"), h - 1)
                act.activation(mem("t", (h % 2) * SEQ, SEQ), FM("r2", h), ACT.Square).then_inc(sem("osq"), 1)
            for h in range(HEADS):
                act.wait_ge(sem("osq_mm"), h + 1)
                if h >= 2:
                    act.wait_ge(sem("o_scaled"), h - 1)
                act.activation(mem("t", D + (h % 2) * SEQ, SEQ), bank(h), ACT.Sqrt, scale=1.0 / P, bias=col(COL_EPS))\
                   .then_inc(sem("o_rms"), 1)

        def hgrn_out_norm_pe(pe):
            for h in range(HEADS):
                pe.wait_ge(sem("osq"), h + 1)
                pe.matmul(bank(h), lhsT=ones, rhs=mem("t", (h % 2) * SEQ, SEQ), start=True, stop=True)\
                  .then_inc(sem("osq_mm"), 1)

        def hgrn_out_norm_dve(dve):
            link = linker(dve, "dve")
            for h in range(HEADS):
                dve.wait_ge(sem("o_rms"), h + 1)
                r = mem("t", D + (h % 2) * SEQ, SEQ)
                link(dve.reciprocal(r, r))
                link(dve.scalar_tensor_tensor(r, r, mem("cols", COL_ON + h, 1), FM("r5", h), ALU.mult, ALU.mult))
                dve.tensor_tensor(FM("r2", h), FM("r2", h), r, ALU.mult).then_inc(sem("o_scaled"), 1)

        Q2 = 2 * PH
        NG = NSEL // GR
        NR = 4
        TURNS = NG // NR
        DVE_ROWS = 2
        RING = lambda r, k: mem(("r2", "r4", "r3", ("moda", "moda", "moda", "t")[k])[r], k * D if r < 3 else (0, 1, 3, 2)[k] * D, D)
        SK_RAW = mem("r3", 0, Q2, P)
        SKT = lambda g, n=1: mem("r3", D + g * P, n * P)
        SC = lambda t, g: mem("r1", t * D + g * P, P)
        SC_REST = lambda g: mem("t", g * P, P)
        DIAG = lambda i: mem("t", D + i * P, P)
        small = lambda off, *dims, dt=None: mem("moda", 2 * D + off, *dims, dt=dt)
        O_V, O_I, O_IF, O_BEST, O_FLAT, O_A, O_B, O_AF, O_BF, O_E1, O_E2 = 0, 128, 256, 384, 448, 512, 576, 640, 704, 768, 832
        O_SUM, O_HH, O_ST = 896, 912, 928
        par_small = lambda off, t, *dims, dt=None: mem("moda", 4 * D + (t % 2) * 256 + off, *dims, dt=dt)
        par_reg = lambda off, t: layout["moda"] + 4 * D + (t % 2) * 256 + off
        O_GATE, O_IDX, O_HID, O_W = 0, 64, 128, 192

        def peer_load_keys(act, l):
            act.dma_start(SK_RAW, A["peer_subkeys"][l].rearrange("h p n d -> n (h p) d")).then_inc(sem("keys_in"), 16)

        def peer_query(l):
            first = marks[f"peer_q{l}"]

            def pe_part(pe):
                for c in range(2):
                    w_arrived(pe, first + c)
                    w = wslot(first + c)
                    for j in range(4):
                        matmuls(pe, bank(4 * c + j), lambda k: w[:, k, j * P:(j + 1) * P], lambda k: XT("r1", k), KD)\
                            .then_inc(sem("pq_mm"), 1)
                    pe.drain().then_inc(sem("w_used"), 1)
                pe.wait_ge(sem("keys_in"), 16 * (l + 1))
                for a in range(2):
                    pe.wait_ge(sem("pq_out"), Q2 * l + a + 1)
                    for j in range(4):
                        last = pe.transpose(bank(a, j * P, P), SK_RAW[:, 4 * a + j, :], ident)
                    last.then_inc(sem("key_tr"), 1)
                pe.wait_ge(sem("pq_out"), Q2 * (l + 1))
                pe.wait_ge(sem("skt"), 2 * (l + 1))
                for t in range(TT):
                    for a in range(2):
                        for j in range(4):
                            g = 4 * a + j
                            last = pe.matmul(bank(2 * t + a, j * P, P), lhsT=FM("r2", g, t * P, P), rhs=SKT(g),
                                             start=True, stop=True)
                        last.then_inc(sem("sc_mm_p"), 1)

            def act_part(act):
                for g in range(Q2):
                    act.wait_ge(sem("pq_mm"), Q2 * l + g + 1)
                    act.activation(FM("r2", g), bank(g), ACT.Copy).then_inc(sem("pq_out"), 1)
                for a in range(2):
                    act.wait_ge(sem("key_tr"), 2 * l + a + 1)
                    act.activation(SKT(4 * a, 4), bank(a), ACT.Copy).then_inc(sem("skt"), 1)
                for i in range(2 * TT):
                    act.wait_ge(sem("sc_mm_p"), 2 * TT * l + i + 1)
                    act.activation(mem("r1", i * 512, 512), bank(i), ACT.Copy)
            return dict(pe=pe_part, act=act_part)

        def peer(l):
            MOD = (MOD0, MOD1)[l]
            T0 = TT * l
            u_tab, v_tab = (A[n].rearrange("l n d -> (l n) d") for n in ("peer_u", "peer_v"))
            def route_dve(dve, t, link):
                V = lambda g, o, n=8: small(O_V + g * PK + o, n)
                I = lambda g, o: small(O_I + g * PK + o, 8, dt=U32)
                for g in range(Q2):
                    last = dve.max(V(g, 0), SC(t, g))
                link(last)
                for g in range(Q2):
                    dve.max_index(I(g, 0), V(g, 0), SC(t, g))
                    last = dve.match_replace(SC_REST(g), V(g, 0), SC(t, g), -3e38)
                link(last)
                for g in range(Q2):
                    last = dve.max(V(g, 8), SC_REST(g))
                link(last)
                for g in range(Q2):
                    last = dve.max_index(I(g, 8), V(g, 8), SC_REST(g))
                link(last)
                C1 = lambda h: mem("t", h * 256, 256)
                link(dve.tensor_tensor(mem("t", 0, PH, PK, PK), small(O_V, (2 * PK, PH), (1, PK), (0, PK)),
                                       small(O_V + PK, (2 * PK, PH), (0, PK), (1, PK)), ALU.add))
                dve.tensor_copy(small(O_IF, Q2 * PK), small(O_I, Q2 * PK, dt=U32))
                B = lambda h, o: small(O_BEST + h * PK + o, 8)
                Fl = lambda h, o: small(O_FLAT + h * PK + o, 8, dt=U32)
                for h in range(PH):
                    last = dve.max(B(h, 0), C1(h))
                link(last)
                for h in range(PH):
                    dve.max_index(Fl(h, 0), B(h, 0), C1(h))
                    last = dve.match_replace(C1(h), B(h, 0), C1(h), -3e38)
                link(last)
                for h in range(PH):
                    last = dve.max(B(h, 8), C1(h))
                link(last)
                gate = par_small(O_GATE, t, PH, PK)
                dve.tensor_tensor(gate, small(O_BEST, PH, PK), small(O_BEST, (PK, PH), (0, PK)), ALU.subtract)\
                   .then_inc(sem("best"), 1)
                for h in range(PH):
                    last = dve.max_index(Fl(h, 8), B(h, 8), C1(h))
                link(last)
                dve.tensor_single_scalar(small(O_A, NSEL, dt=U32), small(O_FLAT, NSEL, dt=U32), 4, ALU.logical_shift_right)
                link(dve.tensor_single_scalar(small(O_B, NSEL, dt=U32), small(O_FLAT, NSEL, dt=U32), PK - 1, ALU.bitwise_and))
                dve.tensor_copy(small(O_AF, NSEL), small(O_A, NSEL, dt=U32))
                link(dve.tensor_copy(small(O_BF, NSEL), small(O_B, NSEL, dt=U32)))
                oh = (mem("t", 0, NSEL, PK), mem("t", 0, PH, PK, PK))
                for o_sel, o_out, which in ((O_AF, O_E1, 0), (O_BF, O_E2, 1)):
                    link(dve.tensor_tensor(oh[0], small(o_sel, (1, NSEL), (0, PK)), mem("iota", 0, (0, NSEL), (1, PK)), ALU.is_equal))
                    link(dve.tensor_tensor(oh[1], oh[1], small(O_IF + which * PK, (2 * PK, PH), (0, PK), (1, PK)), ALU.mult))
                    link(dve.tensor_reduce(small(o_out, NSEL), oh[0], AXIS_X, ALU.add))
                link(dve.scalar_tensor_tensor(small(O_E1, NSEL), small(O_E1, NSEL), float(NKEYS), small(O_E2, NSEL),
                                              ALU.mult, ALU.add))
                if l:
                    link(dve.tensor_scalar(small(O_E1, NSEL), small(O_E1, NSEL), float(l * NKEYS * NKEYS), None, ALU.add))
                dve.tensor_copy(par_small(O_IDX, t, NSEL, dt=U32), small(O_E1, NSEL)).then_inc(sem("experts"), 1)

            def gather_pool(pool, t, v):
                tab = (u_tab, v_tab)[v]
                used = sem(("u_used", "v_used")[v])
                base = (T0 + t) * NG

                def group(i, r):
                    st = small(O_ST + r * GR, GR, dt=U32)
                    first = isinstance(i, int) and i == 0
                    if first:
                        if v:
                            pool.wait_ge(sem("u_used"), base + NG - NR + r + 1)
                        elif T0 + t:
                            pool.wait_ge(sem("v_used"), base - NR + r + 1)
                            pool.wait_ge(sem("v_used_dve"), (T0 + t) * (TURNS // 2) * NR - NR + r + 1)
                        src = par_small(O_IDX + r * GR, t, GR, dt=U32)
                    elif isinstance(i, int):
                        pool.wait_ge(used, i * NR + (base - NR + r + 1))
                        src = par_small(O_IDX + (i * NR + r) * GR, t, GR, dt=U32)
                    else:
                        pool.wait_ge(used, i * NR + (base - NR + r + 1))
                        pool.sem_inc(sem("pool_step"), 1)
                        src = arena[:, bass.ds(i * (NR * GR) + (par_reg(O_IDX, t) + r * GR), GR)].bitcast(U32)
                    pool.tensor_copy(st, src).then_inc(sem("staged"), 1)
                    pool.wait_ge(sem("staged"), i * NR + ((2 * (T0 + t) + v) * NG + r + 1))
                    pool.sem_inc(sem("pool_step"), 1)
                    for k in range(GR):
                        pool.indirect_dma_start(RING(r, k), None, tab,
                                                bass.IndirectOffsetOnAxis(ap=st[:, k:k + 1], axis=0))\
                            .then_inc(sem(f"ring{r}"), 16)
                if not v:
                    pool.wait_ge(sem("experts"), T0 + t + 1)
                for r in range(NR):
                    group(0, r)
                with pool.Fori(1, TURNS - v) as i:
                    for r in range(NR):
                        group(i, r)
                if v:
                    for r in range(NR):
                        pool.wait_ge(sem("v_used_dve"), ((T0 + t) * (TURNS // 2) + TURNS // 2 - 2) * NR + r + 1)
                        group(TURNS - 1, r)

            def rows_arrived(eng, i, r, t, v):
                turns = (2 * (T0 + t) + v) * (NG // NR)
                eng.wait_ge(sem(f"ring{r}"), i * (16 * GR) + 16 * GR * (turns + 1))

            def dot_dve(dve, t):
                with dve.Fori(0, NG // NR) as i:
                    for r in range(NR):
                        rows_arrived(dve, i, r, t, 0)
                        for k in range(GR):
                            last = dve.tensor_tensor_reduce(out=RING(r, k), in0=RING(r, k), in1=mem("r0", t * D, D), scale=1.0,
                                                            scalar=0.0, op0=ALU.mult, op1=ALU.add,
                                                            accum_out=small(O_HH + (r % 2) * GR + k, 1))
                        last.then_inc(sem("dots"), 1)
                        dve.wait_ge(sem("dots"), i * NR + ((T0 + t) * NG + r + 1))
                        dve.tensor_copy(arena[:, bass.ds(i * (NR * GR) + (par_reg(O_HID, t) + r * GR), GR)],
                                        small(O_HH + (r % 2) * GR, GR)).then_inc(sem("u_used"), 1)

            def gelu_act(act, t):
                act.wait_ge(sem("u_used"), (T0 + t + 1) * NG)
                act.activation(par_small(O_W, t, NSEL), par_small(O_HID, t, NSEL), ACT.Gelu).then_inc(sem("gelu"), 1)

            def weights_dve(dve, t, link):
                gate = par_small(O_GATE, t, PH, PK)
                dve.wait_ge(sem("gate_exp"), T0 + t + 1)
                link(dve.tensor_reduce(small(O_SUM, PH), gate, AXIS_X, ALU.add))
                link(dve.reciprocal(small(O_SUM, PH), small(O_SUM, PH)))
                link(dve.tensor_tensor(gate, gate, small(O_SUM, (1, PH), (0, PK)), ALU.mult))
                dve.wait_ge(sem("gelu"), T0 + t + 1)
                dve.tensor_tensor(par_small(O_W, t, NSEL), par_small(O_W, t, NSEL), par_small(O_GATE, t, NSEL), ALU.mult)\
                   .then_inc(sem("weights"), 1)

            def diag_act(act, t):
                act.wait_ge(sem("weights"), T0 + t + 1)
                base = (T0 + t) * NG

                def groups(i, rows=GR):
                    for half in range(2):
                        if base or not isinstance(i, int):
                            act.wait_ge(sem("v_used"), i * 2 + (base + half - 1))
                        for k in range(rows):
                            ins = act.activation(DIAG(half * GR + k), ident, ACT.Copy,
                                                 scale=arena[:, bass.ds(i * (2 * GR) + (par_reg(O_W, t) + half * GR + k), 1)])
                        ins.then_inc(sem("diag"), 1)
                groups(0)
                with act.Fori(1, NG // 4) as i:
                    groups(i)
                with act.Fori(NG // 4, NG // 2) as i:
                    groups(i, GR - DVE_ROWS)

            def sum_pe(pe, t):
                base = (T0 + t) * NG
                acc = (4 + 2 * (t % 2), 5 + 2 * (t % 2))
                if T0 + t >= 2:
                    pe.wait_ge(sem("acc_used"), T0 + t - 1)

                def turn(i, rows=GR, first=False):
                    for r in range(NR):
                        rows_arrived(pe, i, r, t, 1)
                        pe.wait_ge(sem("diag"), i * NR + (base + r + 1))
                        for k in range(rows):
                            for n in range(2):
                                last = pe.matmul(bank(acc[n]), lhsT=DIAG((r % 2) * GR + k), rhs=RING(r, k)[:, n * 512:(n + 1) * 512],
                                                 start=first and r == 0 and k == 0, stop=False, skip_group_check=True)
                        last.then_inc(sem("v_used"), 1)
                turn(0, first=True)
                for i in range(1, TURNS // 2):
                    turn(i)
                with pe.Fori(TURNS // 2, TURNS) as i:
                    turn(i, GR - DVE_ROWS)

            def sum_dve(dve, t, link):
                acc = mem("t", 0, D)
                link(dve.memset(acc, 0.0))
                with dve.Fori(TURNS // 2, TURNS) as i:
                    for r in range(NR):
                        rows_arrived(dve, i, r, t, 1)
                        for k in range(DVE_ROWS):
                            n = (T0 + t) * (TURNS // 2) * NR + r - (TURNS // 2) * NR
                            if k:
                                dve.wait_ge(sem("acc"), i * (NR * (DVE_ROWS - 1)) + (n * (DVE_ROWS - 1) + k))
                            else:
                                dve.wait_ge(sem("v_used_dve"), i * NR + n)
                            w = arena[:, bass.ds(i * (NR * GR) + (par_reg(O_W, t) + r * GR + GR - DVE_ROWS + k), 1)]
                            dve.scalar_tensor_tensor(acc, RING(r, GR - DVE_ROWS + k), w, acc, ALU.mult, ALU.add)\
                               .then_inc(sem("acc" if k < DVE_ROWS - 1 else "v_used_dve"), 1)
                dve.wait_ge(sem("v_used_dve"), (T0 + t + 1) * (TURNS // 2) * NR)

            def finish_dve(dve, t, link):
                dve.wait_ge(sem("v_used"), (T0 + t + 1) * NG)
                acc = 4 + 2 * (t % 2)
                dve.tensor_tensor(mem("t", 0, 512), mem("t", 0, 512), bank(acc), ALU.add)
                link(dve.tensor_tensor(mem("t", 512, 512), mem("t", 512, 512), bank(acc + 1), ALU.add))
                link(dve.tensor_tensor(mem("t", 0, D), mem("t", 0, D), mod(MOD["g2"]), ALU.mult))
                dve.tensor_tensor(H(t), H(t), mem("t", 0, D), ALU.add).then_inc(sem("acc_used"), 1)
                dve.wait_ge(sem("acc_used"), T0 + t + 1)

            def pe_part(pe):
                for t in range(TT):
                    if l == 0:
                        mod_pe(pe, 1, range(4 * t, 4 * t + 4))
                    sum_pe(pe, t)

            def act_part(act):
                for t in range(TT):
                    act.wait_ge(sem("best"), T0 + t + 1)
                    gate = par_small(O_GATE, t, NSEL)
                    act.activation(gate, gate, ACT.Exp).then_inc(sem("gate_exp"), 1)
                    if l == 0:
                        mod_act(act, 1, range(4 * t, 4 * t + 4))
                    gelu_act(act, t)
                    diag_act(act, t)

            def dve_part(dve):
                link = linker(dve, "dve")
                route_dve(dve, 0, link)
                for t in range(TT):
                    dot_dve(dve, t)
                    weights_dve(dve, t, link)
                    if t + 1 < TT:
                        route_dve(dve, t + 1, link)
                    sum_dve(dve, t, link)
                    finish_dve(dve, t, link)

            def pool_part(pool):
                for t in range(TT):
                    gather_pool(pool, t, 0)
                    gather_pool(pool, t, 1)
            return dict(pe=pe_part, act=act_part, dve=dve_part, pool=pool_part)

        def scale_rows_act(act):
            for i, row in enumerate((A["kv_norm_g"].rearrange("(a n) -> a n", a=1), A["norm_mix_g"][1:2],
                                     A["norm_ffn_g"][1:2])):
                act.dma_start(mem("t", i * D, D), row.broadcast_to([P, D])).then_inc(sem("scale_rows"), 16)

        def scale_rows_dve(dve):
            dve.wait_ge(sem("scale_rows"), 48)
            for i, m in enumerate(("sckv", "sc1", "sc2")):
                dve.tensor_tensor(mod(MOD1[m]), mod(MOD1[m]), mem("t", i * D, D), ALU.mult)

        def kv_pe(pe):
            first = marks["kv"]
            for c in range(4):
                w_arrived(pe, first + c)
                w = wslot(first + c)
                for j in range(4):
                    if c < 2:
                        ins = matmuls(pe, bank(4 * c + j), lambda k: w[:, k, j * P:(j + 1) * P], lambda k: XT("r0", k), KD)
                    else:
                        pe.wait_ge(sem("sbk_out"), 4 * (c - 2) + j + 1)
                        ins = matmuls(pe, bank(4 * (c - 2) + j), lambda k: XT("r0", k, j * P, P), lambda k: w[:, k, :], KD)
                    ins.then_inc(sem("kv_mm"), 1)
                pe.drain().then_inc(sem("w_used"), 1)

        def kv_act(act):
            for h in range(HEADS):
                act.wait_ge(sem("kv_mm"), h + 1)
                act.activation(FM("r1", h), bank(h), ACT.Copy).then_inc(sem("sbk_out"), 1)

        def kv_dve(dve):
            for c in range(8):
                dve.wait_ge(sem("kv_mm"), 8 + c + 1)
                dve.tensor_copy(mem("r2", (c % 4) * D + (c // 4) * 512, 512), bank(c))

        def sbq_pe(pe):
            first = marks["sb_q"]
            for c in range(2):
                w_arrived(pe, first + c)
                w = wslot(first + c)
                for j in range(4):
                    matmuls(pe, bank(4 * c + j), lambda k: w[:, k, j * P:(j + 1) * P], lambda k: XT("r0", k), KD)\
                        .then_inc(sem("sbq_mm"), 1)
                pe.drain().then_inc(sem("w_used"), 1)

        def sbq_act(act):
            for h in range(HEADS):
                act.wait_ge(sem("sbq_mm"), h + 1)
                act.activation(FM("r3", h), bank(h), ACT.Copy, scale=float(P) ** -0.5)

        BLK = {0: 0, 1: 512, 3: 896, 2: 1024}
        NQ = [SEQ - P * n for n in range(TT)]
        NZ = sum(NQ)
        ZB = lambda h, off, n: bank(3 * (h % 2), off, n)
        ZC = lambda h, off=0, n=NZ: mem("t", (h % 2) * NZ + off, n)
        SP_ = lambda h, off=0, n=NZ: mem("moda", (h % 2) * NZ + off, n)
        AW = lambda h, off=0, n=NZ: mem("moda", (2 + h % 2) * NZ + off, n)

        def sb_pe(pe):
            def scores(h):
                if h >= 2:
                    pe.wait_ge(sem("a_exp"), h - 1)
                for n in (0, 1, 3, 2):
                    last = pe.matmul(ZB(h, BLK[n], NQ[n]), lhsT=FM("r1", h, n * P, P), rhs=FM("r3", h, n * P, NQ[n]),
                                     start=n != 3, stop=False, skip_group_check=True)
                last.then_inc(sem("z_mm"), 1)
            scores(0)
            scores(1)
            for h in range(HEADS):
                pe.wait_ge(sem("sp"), h + 1)
                for n in range(TT):
                    for m in range(n, TT):
                        last = pe.matmul(ZB(h, BLK[n] + (m - n) * P, NQ[m]), lhsT=mem("negtri" if m == n else "negones", 0, P),
                                         rhs=SP_(h, BLK[m], NQ[m]), start=False, stop=m == TT - 1, skip_group_check=True)
                last.then_inc(sem("cs_mm"), 1)
                if h + 2 < HEADS:
                    scores(h + 2)
                pe.wait_ge(sem("a_sel"), h + 1)
                if h >= 2:
                    pe.wait_ge(sem("sbo_out"), h - 1)
                for n in range(TT):
                    last = pe.matmul(bank(6 + h % 2, n * P, NQ[n]), lhsT=mem("r2", n * D + h * P, P),
                                     rhs=AW(h, BLK[n], NQ[n]), start=n == 0, stop=n == TT - 1, skip_group_check=True)
                last.then_inc(sem("av_mm"), 1)

        def sb_dve(dve):
            link = linker(dve, "dve")

            def first(h):
                dve.wait_ge(sem("z_mm"), h + 1)
                link(dve.tensor_copy(ZC(h), ZB(h, 0, NZ)))
                if h >= 2:
                    dve.wait_ge(sem("av_mm"), h - 1)
                dve.scalar_tensor_tensor(AW(h), ZC(h), -1.0, ZC(h), ALU.mult, ALU.min).then_inc(sem("neg_abs"), 1)

            def second(h):
                dve.wait_ge(sem("ln1p"), h + 1)
                if h >= 2:
                    dve.wait_ge(sem("cs_mm"), h - 1)
                link(dve.scalar_tensor_tensor(SP_(h), ZC(h), 0.0, AW(h), ALU.max, ALU.add))
                for n in range(TT):
                    last = dve.tensor_tensor(SP_(h, BLK[n], P), SP_(h, BLK[n], P), mem("before", 0, P), ALU.mult)
                last.then_inc(sem("sp"), 1)
            first(0)
            for h in range(HEADS):
                if h + 1 < HEADS:
                    first(h + 1)
                second(h)

        def sb_act(act):
            def ln(h):
                act.wait_ge(sem("neg_abs"), h + 1)
                act.activation(AW(h), AW(h), ACT.Exp).then_inc(sem("e_abs"), 1)
                act.wait_ge(sem("e_abs"), h + 1)
                act.activation(AW(h), AW(h), ACT.Ln, bias=col(COL_EPS + 1)).then_inc(sem("ln1p"), 1)
            ln(0)
            for h in range(HEADS):
                if h + 1 < HEADS:
                    ln(h + 1)
                act.wait_ge(sem("cs_mm"), h + 1)
                act.activation(AW(h), ZB(h, 0, NZ), ACT.Exp).then_inc(sem("a_exp"), 1)
                if h:
                    act.wait_ge(sem("av_mm"), h)
                    act.activation(FM("r4", h - 1), bank(6 + (h - 1) % 2), ACT.Copy).then_inc(sem("sbo_out"), 1)
            act.wait_ge(sem("av_mm"), HEADS)
            act.activation(FM("r4", HEADS - 1), bank(6 + (HEADS - 1) % 2), ACT.Copy)

        def sb_pool(pool):
            for h in range(HEADS):
                pool.wait_ge(sem("a_exp"), h + 1)
                for n in range(TT):
                    last = pool.affine_select(out=AW(h, BLK[n], P), in_=AW(h, BLK[n], P), compare_op=ALU.is_gt, fill=0.0,
                                              base=0, pattern=[[1, P]], channel_multiplier=-1)
                last.then_inc(sem("a_sel"), 1)

        ROW2 = lambda i: mem("moda", i * D, D)

        def rows2_act(act):
            for i, name in enumerate(("final_norm_g", "g_mix_2", "g_ffn_2", "g_final_2")):
                row = A[name].rearrange("(a n) -> a n", a=1) if i in (0, 3) else A[name][0:1]
                act.dma_start(ROW2(i), row.broadcast_to([P, D])).then_inc(sem("rows2"), 16)

        def rows2_dve(dve):
            dve.wait_ge(sem("rows2"), 64)

        CW, CC = 31, 4
        PADW = CW - 1 + SEQ
        CV = lambda c, o=0, n=PADW: mem("r1", c * PADW + o, n)
        Y = lambda c: mem("r2", c * SEQ, SEQ)
        CROWS = CW + 3
        CCOL = lambda c, r, n=1: mem("tiny", c * CROWS + r, n)
        Q_2 = lambda j, t0=0, n=SEQ, parts=(0, P): mem("r6", j * SEQ + t0, n, parts=parts)
        K_2 = lambda t0, n, parts=(0, P): mem("r6", 4 * SEQ + t0, n, parts=parts)
        V_2 = lambda blk, c0=0, n=P: mem("r6", 4 * SEQ + 5 * P + blk * P + c0, n)
        conv_rows = mem("r3", 0, 512, parts=(0, CROWS))

        def conv_rows_dma(act):
            act.dma_start(mem("r3", 0, 512, parts=(0, CW)), A["w_dw_2"][0].rearrange("w a c -> w (a c)")).then_inc(sem("conv_rows"), 16)
            for i, name in enumerate(("b_dw_2", "ln_conv_g_2", "ln_conv_b_2")):
                act.dma_start(mem("r3", 0, 512, parts=(CW + i, 1)), A[name][0:1]).then_inc(sem("conv_rows"), 16)

        def in2_pe(pe):
            pe.wait_ge(sem("conv_rows"), 64)
            for c in range(CC):
                last = pe.transpose(bank(7, c * CROWS, CROWS), conv_rows[:, c * P:(c + 1) * P], mem("ident", 0, CROWS, parts=(0, CROWS)))
            last.then_inc(sem("conv_tr"), 1)
            first = marks["in2"]
            g = 0
            for c in range(8):
                w_arrived(pe, first + c)
                w = wslot(first + c)
                for j in range(4 if c != 3 else 2):
                    if g == 7:
                        pe.wait_ge(sem("conv_cols"), 1)
                    if 8 <= g < 12:
                        pe.wait_ge(sem("cv_out"), g - 7)
                    elif g >= 12:
                        pe.wait_ge(sem("in2_out"), g - 11)
                    b = g % 8
                    if c == 3 and j == 1:
                        for t in range(TT):
                            for k in range(KD):
                                last = pe.matmul(bank(b, t * P, P), lhsT=XT("r0", k, t * P, P), rhs=w[:, k, P:2 * P],
                                                 start=k == 0, stop=k == KD - 1)
                    else:
                        last = matmuls(pe, bank(b), lambda k: w[:, k, j * P:(j + 1) * P], lambda k: XT("r0", k), KD)
                    last.then_inc(sem("in2_mm"), 1)
                    g += 1
                pe.drain().then_inc(sem("w_used"), 1)
            pe.wait_ge(sem("in2_out"), 26)
            pe.wait_ge(sem("conv_done"), 1)
            matmuls(pe, bank(0), lambda c: ones, lambda c: Y(c), CC).then_inc(sem("ln_sum"), 1)
            pe.wait_ge(sem("ln_sq"), CC)
            matmuls(pe, bank(1), lambda c: ones, lambda c: mem("r3", c * SEQ, SEQ), CC).then_inc(sem("ln_sum"), 1)

        def in2_act(act):
            act.wait_ge(sem("conv_tr"), 1)
            act.activation(mem("tiny", 0, CC * CROWS), bank(7, 0, CC * CROWS), ACT.Copy).then_inc(sem("conv_cols"), 1)
            for g in range(4, 30):
                act.wait_ge(sem("in2_mm"), g + 1)
                src = bank(g % 8)
                if g < 8:
                    ins = act.activation(mem("t", (g - 4) * SEQ, SEQ), src, ACT.Sigmoid)
                elif g < 12:
                    ins = act.activation(Q_2(g - 8), src, ACT.Copy, scale=0.125)
                elif g == 12:
                    ins = act.activation(K_2(P, SEQ), src, ACT.Copy)
                elif g == 13:
                    ins = act.activation(V_2(1, 0, SEQ), src, ACT.Copy)
                elif g < 22:
                    ins = act.activation(FM("r4", g - 14), src, ACT.Sigmoid)
                else:
                    ins = act.activation(FM("r5", g - 22), src, ACT.Sigmoid)
                ins.then_inc(sem("in2_out"), 1)
            for c in range(CC):
                act.wait_ge(sem("centred"), c + 1)
                act.activation(mem("r3", c * SEQ, SEQ), Y(c), ACT.Square).then_inc(sem("ln_sq"), 1)
            act.wait_ge(sem("ln_sum"), 2)
            act.activation(mem("t", 0, SEQ), bank(1), ACT.Sqrt, scale=1.0 / 512, bias=col(COL_EPS)).then_inc(sem("ln_rms"), 1)
            for c in range(CC):
                act.wait_ge(sem("normed"), c + 1)
                act.activation(Y(c), Y(c), ACT.Silu, scale=CCOL(c, CW + 1), bias=CCOL(c, CW + 2))

        def in2_pool(pool):
            pool.memset(K_2(0, P), 0.0)
            pool.memset(V_2(0), 0.0)

        def in2_dve(dve):
            link = linker(dve, "dve")
            dve.memset(mem("r1", 0, (PADW, CC), CW - 1), 0.0)
            for c in range(CC):
                dve.wait_ge(sem("in2_out"), c + 1)
                dve.tensor_tensor(CV(c, CW - 1, SEQ), bank(c), mem("t", c * SEQ, SEQ), ALU.mult).then_inc(sem("cv_out"), 1)
            dve.wait_ge(sem("cv_out"), CC)
            dve.wait_ge(sem("conv_cols"), 1)
            for c in range(CC):
                dve.tensor_scalar(Y(c), CV(c, 0, SEQ), CCOL(c, 0), CCOL(c, CW), ALU.mult, ALU.add).then_inc(sem("tap"), 1)
            with dve.Fori(0, CW - 1) as i:
                for c in range(CC):
                    dve.wait_ge(sem("tap"), i * CC + (c + 1))
                    dve.scalar_tensor_tensor(Y(c), arena[:, bass.ds(i + (layout["r1"] + c * PADW + 1), SEQ)],
                                             arena[:, bass.ds(i + (layout["tiny"] + c * CROWS + 1), 1)], Y(c),
                                             ALU.mult, ALU.add).then_inc(sem("tap"), 1)
            dve.drain().then_inc(sem("conv_done"), 1)
            dve.wait_ge(sem("ln_sum"), 1)
            for c in range(CC):
                dve.scalar_tensor_tensor(Y(c), bank(0), -1.0 / 512, Y(c), ALU.mult, ALU.add).then_inc(sem("centred"), 1)
            dve.wait_ge(sem("ln_rms"), 1)
            link(dve.reciprocal(mem("t", 0, SEQ), mem("t", 0, SEQ)))
            dve.wait_ge(sem("ln_sq"), CC)
            for c in range(CC):
                dve.tensor_tensor(Y(c), Y(c), mem("t", 0, SEQ), ALU.mult).then_inc(sem("normed"), 1)

        AH = 8
        REL = mem("r3", 0, 2 * P)
        WIN = mem("r3", 256, 2 * P)
        BIAS2 = lambda h: mem("r3", 512 + (h % 2) * 256, 2 * P)
        SINKS = lambda h=0, n=1: mem("r3", 1024 + h, n)
        st2 = lambda off, h, n=TT: mem("r3", 1040 + (h % 2) * 64 + off, n)
        S2 = lambda h, o=0, n=2 * P * TT: mem("t", (h % 2) * D + o, n)
        PT2 = lambda h, o=0, n=P: mem("moda", (4 + h % 2) * D + o, n)
        O2 = lambda h, t0=0, n=SEQ: mem("r0", (h % 4) * SEQ + t0, n, parts=(64 * (h // 4), 64))
        SLOPE = [2.0 ** (-8.0 * (h + 1) / AH) for h in range(AH)]

        def attn2_pe(pe):
            def scores(h):
                pr = (64 * (h // 4), 64)
                if h >= 2:
                    pe.wait_ge(sem("s2_out"), h - 1)
                for n in range(TT):
                    b = 2 * (h % 2) + n // 2
                    last = pe.matmul(bank(b, (n % 2) * 256, 256), lhsT=Q_2(h % 4, n * P, P, parts=pr),
                                     rhs=K_2(n * P, 2 * P, parts=pr), start=True, stop=True)
                last.then_inc(sem("s2_mm"), 1)
            scores(0)
            for h in range(AH):
                if h + 1 < AH:
                    scores(h + 1)
                pe.wait_ge(sem("p2"), h + 1)
                for a in range(2):
                    if h:
                        pe.wait_ge(sem("pt2_out"), 2 * (h - 1) + a + 1)
                    for j in range(4):
                        last = pe.transpose(bank(4 + a, j * P, P), S2(h, (4 * a + j) * P, P), ident)
                    last.then_inc(sem("pt2_tr"), 1)
                pe.wait_ge(sem("pt2_out"), 2 * h + 2)
                if h >= 2:
                    pe.wait_ge(sem("o2_out"), h - 1)
                for n in range(TT):
                    for kb in range(2):
                        last = pe.matmul(bank(6 + h % 2, n * P, P, parts=(64 * (h // 4), 64)),
                                         lhsT=V_2(n + kb, 64 * (h // 4), 64), rhs=PT2(h, (2 * n + kb) * P, P),
                                         start=kb == 0, stop=kb == 1)
                last.then_inc(sem("o2_mm"), 1)

        def attn2_act(act):
            act.dma_start(SINKS(0, AH), A["sinks_2"][0:1].broadcast_to([P, AH])).then_inc(sem("sinks"), 16)
            act.wait_ge(sem("sinks"), 16)
            for h in range(AH):
                act.wait_ge(sem("m2"), h + 1)
                for n in range(TT):
                    act.activation(S2(h, n * 256, 256), S2(h, n * 256, 256), ACT.Exp, bias=st2(n, h, 1),
                                   accum_out=st2(8 + n, h, 1))
                act.activation(st2(16, h), st2(0, h), ACT.Exp, bias=SINKS(h)).then_inc(sem("e2"), 1)
                for a in range(2):
                    act.wait_ge(sem("pt2_tr"), 2 * h + a + 1)
                    act.activation(PT2(h, a * 512, 512), bank(4 + a), ACT.Copy).then_inc(sem("pt2_out"), 1)
                act.wait_ge(sem("o2_mm"), h + 1)
                act.activation(O2(h), bank(6 + h % 2, 0, 512, parts=(64 * (h // 4), 64)), ACT.Copy)\
                   .then_inc(sem("o2_out"), 1)

        def attn2_pool(pool):
            pool.iota(REL, pattern=[[-1, 2 * P]], base=P, channel_multiplier=1, allow_small_or_imprecise_dtypes=True)
            link = linker(pool, "pool")
            link(pool.memset(WIN, 0.0))
            link(pool.affine_select(out=WIN, in_=WIN, compare_op=ALU.is_ge, fill=NEG, base=P, pattern=[[-1, 2 * P]],
                                    channel_multiplier=1))
            pool.affine_select(out=WIN, in_=WIN, compare_op=ALU.is_ge, fill=NEG, base=-1, pattern=[[1, 2 * P]],
                               channel_multiplier=-1).then_inc(sem("window"), 1)

        def attn2_dve(dve):
            link = linker(dve, "dve")
            dve.wait_ge(sem("window"), 1)
            dve.wait_ge(sem("sinks"), 16)

            def first(h):
                link(dve.scalar_tensor_tensor(BIAS2(h), REL, -SLOPE[h], WIN, ALU.mult, ALU.add))
                dve.wait_ge(sem("s2_mm"), h + 1)
                if h >= 2:
                    dve.wait_ge(sem("pt2_tr"), 2 * (h - 1))
                for a in range(2):
                    last = dve.tensor_tensor(mem("t", (h % 2) * D + a * 512, 2, 256), bank(2 * (h % 2) + a, 0, 2, 256),
                                             mem("r3", 512 + (h % 2) * 256, (0, 2), (1, 256)), ALU.add)
                last.then_inc(sem("s2_out"), 1)
                dve.wait_ge(sem("s2_out"), h + 1)
                link(dve.memset(S2(h, 0, P), NEG))
                link(dve.tensor_reduce(st2(0, h), mem("t", (h % 2) * D, TT, 256), AXIS_X, ALU.max))
                dve.tensor_scalar(st2(0, h), st2(0, h), SINKS(h), -1.0, ALU.max, ALU.mult).then_inc(sem("m2"), 1)

            def second(h):
                dve.wait_ge(sem("e2"), h + 1)
                link(dve.tensor_tensor(st2(24, h), st2(8, h), st2(16, h), ALU.add))
                link(dve.reciprocal(st2(24, h), st2(24, h)))
                for n in range(TT):
                    last = dve.tensor_scalar(S2(h, n * 256, 256), S2(h, n * 256, 256), st2(24 + n, h, 1), None, ALU.mult)
                last.then_inc(sem("p2"), 1)
            first(0)
            for h in range(AH):
                if h + 1 < AH:
                    first(h + 1)
                second(h)

        def merge_pe(pe):
            for c, (name, kn) in enumerate((("conv_out", 4), ("attn_out", 4))):
                i = marks[name]
                w_arrived(pe, i)
                w = wslot(i).rearrange("p k n -> p (k n)").rearrange("p (j n) -> p j n", n=D)
                src = "r0" if c else "r2"
                for m in range(KD):
                    if c:
                        pe.wait_ge(sem("merge_out"), m + 1)
                    matmuls(pe, bank(m), lambda k: w[:, k, m * P:(m + 1) * P], lambda k: mem(src, k * SEQ, SEQ), kn)\
                        .then_inc(sem("merge_mm"), 1)
                pe.drain().then_inc(sem("w_used"), 1)

        def merge_dve(dve):
            link = linker(dve, "dve")
            for m in range(KD):
                dve.wait_ge(sem("merge_mm"), m + 1)
                dve.tensor_tensor(FM("r4", m), FM("r4", m), bank(m), ALU.mult).then_inc(sem("merge_out"), 1)
            for m in range(KD):
                dve.wait_ge(sem("merge_mm"), KD + m + 1)
                link(dve.tensor_tensor(FM("r5", m), FM("r5", m), bank(m), ALU.mult))
                dve.tensor_tensor(FM("r4", m), FM("r4", m), FM("r5", m), ALU.add)

        NGRP, EPG, TOPE, FF = 4, 8, 2, 512
        NE = NGRP * EPG
        SLOTS = 64
        MAXB = NE + SEQ * TOPE // SLOTS
        NF = FF // P
        x_slots = nc.dram_tensor("x_slots", [(MAXB + 1) * SLOTS, D], F32, kind="Internal").ap()
        y_slots = x_slots
        ZROWS = (MAXB + 1) * SLOTS

        def zero_slots(pool_or_act):
            done = 0
            while done < ZROWS:
                n = min(P, ZROWS - done)
                pool_or_act.dma_start(x_slots[done:done + n, :], mem("r1", 0, D, parts=(0, n))).then_inc(sem("cleared"), 16)
                done += n

        N_CLEAR = -(-ZROWS // P)
        ROUTER = lambda k: mem("w1", k * (NGRP + NE), NGRP + NE)
        RB = mem("w1", 512, NGRP + NE)
        m2 = lambda off, *dims, dt=None: mem("moda", 4 * D + off, *dims, dt=dt)
        NL = NGRP + NE
        (M_LG, M_GP, M_GM, M_GI, M_GF, M_OG, M_PG, M_EI, M_EM, M_EX, M_EXF, M_W, M_ID) = (
            0, 160, 192, 224, 256, 260, 276, 280, 312, 344, 376, 384, 392)
        (M_OH, M_A, M_CNT, M_NB, M_INC, M_BS, M_PB, M_DEST, M_DSTI, M_NBI, M_BSI, M_TOT, M_D1, M_R) = (
            400, 656, 784, 816, 848, 880, 912, 1040, 1048, 1056, 1088, 1120, 1124, 1128)
        M_BIG = 1152

        def route2_dma(act):
            act.dma_start(mem("w1", 0, (NL, KD), NGRP), A["w_group_2"][0].rearrange("(k p) n -> p k n", p=P),
                          allow_slow_non_contiguous=True).then_inc(sem("router"), 16)
            act.dma_start(mem("w1", NGRP, (NL, KD), NE), A["w_expert_2"][0].rearrange("(k p) n -> p k n", p=P))\
               .then_inc(sem("router"), 16)
            act.dma_start(mem("w1", 512, NGRP), A["b_group_2"][0:1].broadcast_to([P, NGRP])).then_inc(sem("router"), 16)
            act.dma_start(mem("w1", 512 + NGRP, NE), A["b_expert_2"][0:1].broadcast_to([P, NE])).then_inc(sem("router"), 16)

        def route2_pe(pe):
            pe.wait_ge(sem("router"), 64)
            for t in range(TT):
                matmuls(pe, bank(t, 0, NL), lambda k: XT("w0", k, t * P, P), ROUTER, KD).then_inc(sem("logits"), 1)
            pe.wait_ge(sem("chosen"), 1)
            for t in range(TT):
                for u in range(t + 1):
                    pe.matmul(bank(4, t * NE, NE), lhsT=mem("before", 0, P) if u == t else ones,
                              rhs=m2(M_A + u * NE, NE), start=u == 0, stop=u == t)
            matmuls(pe, bank(5, 0, NE), lambda t: ones, lambda t: m2(M_A + t * NE, NE), TT).then_inc(sem("counted"), 1)

        def route2_act(act):
            act.wait_ge(sem("g_shift"), 1)
            act.activation(m2(M_BIG, TT * NGRP), m2(M_BIG, TT * NGRP), ACT.Exp).then_inc(sem("g_exp"), 1)
            act.wait_ge(sem("e_shift"), 1)
            act.activation(m2(M_D1, TT), m2(M_D1, TT), ACT.Exp).then_inc(sem("e_exp"), 1)

        def route2_dve(dve):
            link = linker(dve, "dve")
            dve.memset(m2(M_GP, TT, EPG), -3e38)
            dve.wait_ge(sem("router"), 64)
            for t in range(TT):
                dve.wait_ge(sem("logits"), t + 1)
                last = dve.tensor_tensor(m2(M_LG + t * NL, NL), bank(t, 0, NL), RB, ALU.add)
            link(last)
            link(dve.tensor_copy(m2(M_GP, (EPG, TT), NGRP), m2(M_LG, (NL, TT), NGRP)))
            for t in range(TT):
                last = dve.max(m2(M_GM + t * 8, 8), m2(M_GP + t * EPG, EPG))
            link(last)
            for t in range(TT):
                last = dve.max_index(m2(M_GI + t * 8, 8, dt=U32), m2(M_GM + t * 8, 8), m2(M_GP + t * EPG, EPG))
            link(last)
            dve.tensor_tensor(m2(M_BIG, TT, NGRP), m2(M_LG, (NL, TT), NGRP), m2(M_GM, (8, TT), (0, NGRP)), ALU.subtract)\
               .then_inc(sem("g_shift"), 1)
            link(dve.tensor_copy(m2(M_GF, TT), m2(M_GI, (8, TT), dt=U32)))
            link(dve.tensor_tensor(m2(M_OG, TT, NGRP), m2(M_GF, (1, TT), (0, NGRP)), mem("iota", 0, (0, TT), (1, NGRP)), ALU.is_equal))
            dve.wait_ge(sem("g_exp"), 1)
            link(dve.tensor_reduce(m2(M_PG, TT), m2(M_BIG, TT, NGRP), AXIS_X, ALU.add))
            link(dve.reciprocal(m2(M_PG, TT), m2(M_PG, TT)))
            link(dve.tensor_tensor(m2(M_BIG, TT, NGRP, EPG), m2(M_LG + NGRP, (NL, TT), (EPG, NGRP), (1, EPG)),
                                   m2(M_OG, (NGRP, TT), (1, NGRP), (0, EPG)), ALU.mult))
            link(dve.tensor_reduce(m2(M_EI, TT, EPG), m2(M_BIG, (NE, TT), (1, EPG), (EPG, NGRP)), AXIS_X, ALU.add))
            for t in range(TT):
                last = dve.max(m2(M_EM + t * 8, 8), m2(M_EI + t * 8, 8))
            link(last)
            for t in range(TT):
                last = dve.max_index(m2(M_EX + t * 8, 8, dt=U32), m2(M_EM + t * 8, 8), m2(M_EI + t * 8, 8))
            link(last)
            link(dve.tensor_copy(m2(M_EXF, TT, TOPE), m2(M_EX, (8, TT), (1, TOPE), dt=U32)))
            link(dve.scalar_tensor_tensor(m2(M_ID, TT, TOPE), m2(M_GF, (1, TT), (0, TOPE)), float(EPG), m2(M_EXF, TT, TOPE),
                                          ALU.mult, ALU.add))
            link(dve.tensor_tensor(m2(M_OH, TT * TOPE, NE), m2(M_ID, (1, TT * TOPE), (0, NE)), mem("iota", 0, (0, TT * TOPE), (1, NE)),
                                   ALU.is_equal))
            dve.tensor_tensor(m2(M_A, TT, NE), m2(M_OH, (TOPE * NE, TT), NE), m2(M_OH + NE, (TOPE * NE, TT), NE), ALU.add)\
               .then_inc(sem("chosen"), 1)
            dve.tensor_tensor(m2(M_D1, TT), m2(M_EM + 1, (8, TT)), m2(M_EM, (8, TT)), ALU.subtract).then_inc(sem("e_shift"), 1)
            dve.wait_ge(sem("e_exp"), 1)
            link(dve.tensor_scalar(m2(M_R, TT), m2(M_D1, TT), 1.0, None, ALU.add))
            link(dve.reciprocal(m2(M_R, TT), m2(M_R, TT)))
            link(dve.tensor_tensor(m2(M_R, TT), m2(M_R, TT), m2(M_PG, TT), ALU.mult))
            dve.tensor_copy(m2(M_W, (TOPE, TT)), m2(M_R, TT))
            dve.tensor_tensor(m2(M_W + 1, (TOPE, TT)), m2(M_R, TT), m2(M_D1, TT), ALU.mult)
            dve.wait_ge(sem("counted"), 1)
            link(dve.tensor_copy(m2(M_CNT, NE), bank(5, 0, NE)))
            link(dve.tensor_scalar(m2(M_EI, EPG), mem("iota", 0, EPG), float(SLOTS), None, ALU.mult))
            link(dve.tensor_tensor(m2(M_BIG, NE, EPG), m2(M_CNT, (1, NE), (0, EPG)), m2(M_EI, (0, NE), (1, EPG)), ALU.is_gt))
            link(dve.tensor_reduce(m2(M_NB, NE), m2(M_BIG, NE, EPG), AXIS_X, ALU.add))
            link(dve.tensor_scalar(m2(M_NB, NE), m2(M_NB, NE), 1.0, None, ALU.max))
            link(dve.tensor_tensor_scan(m2(M_INC, NE), mem("ones", 0, NE), m2(M_NB, NE), 0.0, ALU.mult, ALU.add))
            link(dve.tensor_tensor(m2(M_BS, NE), m2(M_INC, NE), m2(M_NB, NE), ALU.subtract))
            dve.tensor_copy(m2(M_NBI, NE, dt=I32), m2(M_NB, NE))
            dve.tensor_copy(m2(M_BSI, NE, dt=I32), m2(M_BS, NE))
            dve.tensor_copy(m2(M_TOT, 1, dt=I32), m2(M_INC + NE - 1, 1))
            link(dve.scalar_tensor_tensor(m2(M_PB, TT, NE), m2(M_BS, (0, TT), (1, NE)), float(SLOTS), bank(4, 0, TT, NE),
                                          ALU.mult, ALU.add))
            link(dve.tensor_tensor(m2(M_BIG, TT, TOPE, NE), m2(M_OH, TT, TOPE, NE), m2(M_PB, (NE, TT), (0, TOPE), (1, NE)), ALU.mult))
            link(dve.tensor_reduce(m2(M_DEST, TT * TOPE), m2(M_BIG, TT * TOPE, NE), AXIS_X, ALU.add))
            dve.tensor_copy(m2(M_DSTI, TT * TOPE, dt=U32), m2(M_DEST, TT * TOPE)).then_inc(sem("slots"), 1)

        def dispatch_pool(pool):
            pool.wait_ge(sem("cleared"), 16 * N_CLEAR)
            pool.wait_ge(sem("slots"), 1)
            for i in range(TT * TOPE):
                pool.indirect_dma_start(x_slots, bass.IndirectOffsetOnAxis(ap=m2(M_DSTI + i, 1, dt=U32), axis=0),
                                        mem("r0", (i // TOPE) * D, D), None).then_inc(sem("sent"), 16)
            pool.wait_ge(sem("sent"), 16 * TT * TOPE)

        EW = [[mem(r, 0, KD, FF) for r in ("r1", "r2")] + [mem("r3", 0, NF, D)],
              [mem(r, 0, KD, FF) for r in ("r4", "r5")] + [mem("r6", 0, NF, D)]]
        eg = A["w_gate_2"][0].rearrange("e (k p) n -> e p k n", p=P)
        eu = A["w_up_2"][0].rearrange("e (k p) n -> e p k n", p=P)
        ed = A["w_down_2"][0].rearrange("e (k p) n -> e p k n", p=P)
        XB = mem("w1", 0, D, parts=(0, SLOTS))
        XBT = mem("w1", D, KD, SLOTS)
        SG = mem("w1", D + 512, NF, SLOTS)
        HT = mem("w1", D + 768, NF, SLOTS)
        YB = lambda n0=0, n=D: mem("w1", 2 * D + n0, n, parts=(0, SLOTS))

        def expert_weights_sp(sp):
            def load(e, s):
                for m, tab in enumerate((eg, eu, ed)):
                    sp.dma_start(EW[s][m], tab[e]).then_inc(sem(f"ew{s}_{m}"), 16)
            load(0, 0)
            load(1, 1)
            with sp.Fori(1, NE // 2) as i:
                for s in range(2):
                    sp.wait_ge(sem("expert_done"), i * 2 + (s - 1))
                    load(i * 2 + s, s)

        def experts_pe(pe):
            def transposes(wait):
                pe.wait_ge(sem("x_block"), wait)
                pe.sem_inc(sem("pe_step"), 1)
                for k in range(KD):
                    last = pe.transpose(bank(0, k * SLOTS, SLOTS), XB[:, k * P:(k + 1) * P], mem("ident", 0, SLOTS, parts=(0, SLOTS)))
                last.then_inc(sem("xb_tr"), 1)
            transposes(16)
            with pe.Fori(0, NE // 2) as i:
                for s in range(2):
                    e = i * 2 + s
                    ob = layout["moda"] + 4 * D
                    nb = pe.value_load(arena[0:1, bass.ds(i * 2 + (ob + M_NBI + s), 1)].bitcast(I32), min_val=1, max_val=8)
                    bs = pe.value_load(arena[0:1, bass.ds(i * 2 + (ob + M_BSI + s), 1)].bitcast(I32), min_val=0, max_val=MAXB - 1)
                    for m in range(3):
                        pe.wait_ge(sem(f"ew{s}_{m}"), i * 16 + 16)
                        pe.sem_inc(sem("pe_step"), 1)
                    with pe.Fori(0, nb) as j:
                        g = bs + j
                        pe.wait_ge(sem("xbT"), g + 1)
                        for m in range(2):
                            for f in range(NF):
                                last = matmuls(pe, bank(1 + m, f * SLOTS, SLOTS), lambda k: EW[s][m][:, k, f * P:(f + 1) * P],
                                               lambda k: XBT[:, k, :], KD)
                            last.then_inc(sem("gate_mm" if m == 0 else "up_mm"), 1)
                        transposes(g * 16 + 32)
                        pe.wait_ge(sem("hT"), g + 1)
                        pe.wait_ge(sem("y_out"), g * 2 + 2)
                        for n in range(2):
                            last = matmuls(pe, bank(3 + n, 0, 512, parts=(0, SLOTS)), lambda k: HT[:, k, :],
                                           lambda k: EW[s][2][:, k, n * 512:(n + 1) * 512], NF)
                        last.then_inc(sem("y_mm"), 1)
                    pe.drain().then_inc(sem("expert_done"), 1)

        def n_blocks(eng):
            return eng.value_load(m2(M_TOT, 1, dt=I32)[0:1], min_val=NE, max_val=MAXB)

        def experts_act(act):
            n = n_blocks(act)
            act.sem_inc(sem("y_out"), 2)
            act.wait_ge(sem("xb_tr"), 1)
            act.activation(XBT, bank(0, 0, KD, SLOTS), ACT.Copy).then_inc(sem("xbT"), 1)
            with act.Fori(0, n) as g:
                act.wait_ge(sem("gate_mm"), g + 1)
                act.activation(SG, bank(1, 0, NF, SLOTS), ACT.Silu).then_inc(sem("silu"), 1)
                act.wait_ge(sem("xb_tr"), g + 2)
                act.activation(XBT, bank(0, 0, KD, SLOTS), ACT.Copy).then_inc(sem("xbT"), 1)
                act.wait_ge(sem("y_mm"), g + 1)
                act.wait_ge(sem("y_free"), g + 1)
                act.activation(YB(0, 512), bank(3, 0, 512, parts=(0, SLOTS)), ACT.Copy).then_inc(sem("y_out"), 1)

        def experts_dve(dve):
            n = n_blocks(dve)
            with dve.Fori(0, n) as g:
                dve.wait_ge(sem("up_mm"), g + 1)
                dve.wait_ge(sem("silu"), g + 1)
                dve.tensor_tensor(HT, SG, bank(2, 0, NF, SLOTS), ALU.mult).then_inc(sem("hT"), 1)
                dve.wait_ge(sem("y_mm"), g + 1)
                dve.wait_ge(sem("y_free"), g + 1)
                dve.tensor_copy(YB(512, 512), bank(4, 0, 512, parts=(0, SLOTS))).then_inc(sem("y_out"), 1)

        def experts_pool(pool):
            n = n_blocks(pool)
            pool.dma_start(XB, x_slots[0:SLOTS, :]).then_inc(sem("x_block"), 16)
            pool.sem_inc(sem("y_free"), 1)
            with pool.Fori(0, n) as g:
                pool.wait_ge(sem("xb_tr"), g + 1)
                pool.sem_inc(sem("pool_step"), 1)
                pool.dma_start(XB, x_slots[bass.ds(g * SLOTS + SLOTS, SLOTS), :]).then_inc(sem("x_block"), 16)
                pool.wait_ge(sem("y_out"), g * 2 + 4)
                pool.sem_inc(sem("pool_step"), 1)
                pool.dma_start(y_slots[bass.ds(g * SLOTS, SLOTS), :], YB()).then_inc(sem("y_stored"), 16)
                pool.wait_ge(sem("y_stored"), g * 16 + 16)
                pool.sem_inc(sem("y_free"), 1)
            pool.wait_ge(sem("x_block"), 16)

        def combine_pool(pool):
            for i in range(TT * TOPE):
                pool.indirect_dma_start(mem("r1" if i < 4 else "r2", (i % 4) * D, D), None, y_slots,
                                        bass.IndirectOffsetOnAxis(ap=m2(M_DSTI + i, 1, dt=U32), axis=0))\
                    .then_inc(sem(f"y_back{i % TOPE}"), 16)

        def combine_dve(dve):
            for k in range(TOPE):
                dve.wait_ge(sem(f"y_back{k}"), 16 * TT)
                for t in range(TT):
                    i = t * TOPE + k
                    if k:
                        dve.wait_ge(sem("combined"), t + 1)
                    dve.scalar_tensor_tensor(H(t), mem("r1" if i < 4 else "r2", (i % 4) * D, D), m2(M_W + i, 1), H(t),
                                             ALU.mult, ALU.add).then_inc(sem("combined"), 1)

        nothing = lambda eng: None
        PHASES = []

        def phase(pe=nothing, act=nothing, dve=nothing, pool=nothing):
            PHASES.append(dict(pe=pe, act=act, dve=dve, pool=pool))

        phase(setup_pe, setup_act, setup_dve, setup_pool)
        phase(**norm(0, mod(MOD0["sc1"]), mod(MOD0["sh1"]), xn_temp, "r0"))
        phase(hgrn_in_pe, hgrn_in_act, hgrn_in_dve)
        phase(hgrn_scan_pe, hgrn_scan_act, hgrn_scan_dve)
        phase(hgrn_out_norm_pe, hgrn_out_norm_act, hgrn_out_norm_dve)
        phase(**out_proj(0, marks["hgrn_out"], lambda k, t: FM("r2", k, t * P, P), KD, MOD0["g1"]))
        n = norm(1, mod(MOD0["sc2"]), mod(MOD0["sh2"]), lambda t: mem("r0", t * D, D), "r1")
        phase(n["pe"], lambda act: (peer_load_keys(act, 0), n["act"](act)), n["dve"])
        phase(**peer_query(0))
        phase(**peer(0))
        phase(nothing, scale_rows_act, scale_rows_dve)
        phase(**norm(2, mod(MOD1["sckv"]), mod(MOD1["shkv"]), xn_temp, "r0"))
        phase(kv_pe, kv_act, kv_dve)
        phase(**norm(3, mod(MOD1["sc1"]), mod(MOD1["sh1"]), xn_temp, "r0"))
        phase(sbq_pe, sbq_act)
        phase(sb_pe, sb_act, sb_dve, sb_pool)
        phase(**out_proj(1, marks["sb_out"], lambda k, t: FM("r4", k, t * P, P), KD, MOD1["g1"]))
        n4 = norm(4, mod(MOD1["sc2"]), mod(MOD1["sh2"]), lambda t: mem("r0", t * D, D), "r1")
        phase(n4["pe"], lambda act: (peer_load_keys(act, 1), n4["act"](act)), n4["dve"])
        phase(**peer_query(1))
        phase(**peer(1))
        phase(nothing, rows2_act, rows2_dve)
        phase(**norm(5, ROW2(0), None, H, None))
        n6 = norm(6, ROW2(1), None, xn_temp, "r0")
        phase(n6["pe"], lambda act: (conv_rows_dma(act), n6["act"](act)), n6["dve"])
        phase(in2_pe, in2_act, in2_dve, in2_pool)
        phase(attn2_pe, attn2_act, attn2_dve, attn2_pool)
        phase(merge_pe, nothing, merge_dve)
        phase(**out_proj(2, marks["out2"], lambda k, t: FM("r4", k, t * P, P), KD, None))
        FREED = len(PHASES)
        n7 = norm(7, ROW2(2), None, lambda t: mem("r0", t * D, D), "w0")
        phase(n7["pe"], lambda act: (route2_dma(act), n7["act"](act)), n7["dve"])
        phase(route2_pe, route2_act, route2_dve, dispatch_pool)
        phase(experts_pe, experts_act, experts_dve, experts_pool)
        phase(nothing, nothing, combine_dve, combine_pool)
        phase(**norm(8, ROW2(3), None, H, None))

        nph = len(PHASES)
        block = ctx.enter_context(nc.Block())

        @block.sync
        def _(sp):
            setup_sp(sp)
            load_weights(sp)
            enter(sp, FREED)
            expert_weights_sp(sp)
            enter(sp, nph)
            sp.dma_start(out[0].rearrange("(t p) d -> p t d", p=P), mem("h", 0, TT, D)).then_inc(sem("stored"), 16)
            sp.wait_ge(sem("stored"), 16)

        @block.tensor
        def _(pe):
            for n, p in enumerate(PHASES):
                enter(pe, n)
                p["pe"](pe)
                leave(pe, "pe")

        @block.scalar
        def _(act):
            for n, p in enumerate(PHASES):
                enter(act, n)
                p["act"](act)
                leave(act, "act")

        @block.vector
        def _(dve):
            for n, p in enumerate(PHASES):
                enter(dve, n)
                p["dve"](dve)
                leave(dve, "dve")

        @block.gpsimd
        def _(pool):
            for n, p in enumerate(PHASES):
                enter(pool, n)
                p["pool"](pool)
                leave(pool, "pool")


_INS = [
    "x", "c", "ada_w", "ada_b", "norm_mix_g", "norm_ffn_g", "hgrn_w_in", "hgrn_lb_logits", "hgrn_onorm_g",
    "hgrn_w_out", "kv_ada_w", "kv_ada_b", "kv_norm_g", "kv_w", "sb_w_q", "sb_w_out", "peer_w_q",
    "peer_subkeys", "peer_u", "peer_v", "final_norm_g", "g_mix_2", "w_in_2", "w_dw_2", "b_dw_2",
    "ln_conv_g_2", "ln_conv_b_2", "sinks_2", "w_conv_out_2", "w_attn_out_2", "w_out_2", "g_ffn_2",
    "w_group_2", "b_group_2", "w_expert_2", "b_expert_2", "w_gate_2", "w_up_2", "w_down_2", "g_final_2",
]


def kernel(**inputs):
    import numpy as _np
    import concourse.bacc as _bacc
    from concourse import mybir as _mybir
    from concourse.bass_utils import run_bass_kernel_spmd as _run

    nc = _bacc.Bacc("TRN2", target_bir_lowering=False, num_devices=1)
    arrays, args = {}, {}
    for name in _INS:
        a = _np.ascontiguousarray(inputs[name])
        arrays[f"in_{name}_dram"] = a
        args[name] = nc.dram_tensor(f"in_{name}_dram", a.shape, _mybir.dt.from_np(a.dtype), kind="ExternalInput").ap()
    out = nc.dram_tensor("out_dram", (1, SEQ, D), F32, kind="ExternalOutput").ap()
    build_program(nc, args, out)
    r = _run(nc, [arrays], core_ids=[0])
    return r.results[0]["out_dram"]
```

```python
import concourse.bass as bass
from concourse import mybir
from contextlib import ExitStack

F32 = mybir.dt.float32
I32 = mybir.dt.int32
U32 = mybir.dt.uint32
ALU = mybir.AluOpType
ACT = mybir.ActivationFunctionType
AXIS_X = mybir.AxisListType.X

P = 128
D = 1024
SEQ = 512
TT = SEQ // P
KD = D // P
EPS = 1e-6
HEADS = 8
CHUNK = 16
CPT = P // CHUNK
PH = 4
PK = 16
NKEYS = 128
NSEL = PH * PK
GR = 4
NEG = -1e30


def build_program(nc, A, out):
    ctx = ExitStack()
    with ctx:
        sems = {}

        def sem(name):
            if name not in sems:
                sems[name] = ctx.enter_context(nc.semaphore(name))
            return sems[name]

        REG = TT * D
        layout, at = {}, 0
        for name, words in (("h", REG), ("w0", REG), ("w1", REG), ("moda", 6 * D), ("r0", REG), ("r1", REG),
                            ("r2", REG), ("r3", REG), ("r4", REG), ("r5", REG), ("r6", REG), ("t", 3 * D),
                            ("ident", P), ("ones", P), ("negones", P), ("negtri", P), ("before", P),
                            ("chunk_causal", P), ("not_first", SEQ), ("c_rep", KD * P), ("cols", 128), ("iota", 64),
                            ("tiny", 384)):
            layout[name] = at
            at += words
        WORDS = at
        arena = ctx.enter_context(nc.sbuf_tensor("arena", [P, WORDS], F32))
        psum = ctx.enter_context(nc.psum_tensor("psum", [P, 8, 512], F32))

        def mem(name, off, *dims, parts=(0, P), dt=None):
            pat, step = [], 1
            for d in reversed(dims):
                if isinstance(d, tuple):
                    pat.append([d[0], d[1]])
                    step = d[0] * d[1]
                else:
                    pat.append([step, d])
                    step *= d
            ap = bass.AP(arena, parts[0] * WORDS + layout[name] + off, [[WORDS, parts[1]]] + pat[::-1])
            return ap if dt is None else ap.bitcast(dt)

        def bank(b, off=0, *dims, parts=(0, P)):
            pat, step = [], 1
            for d in reversed(dims or (512,)):
                if isinstance(d, tuple):
                    pat.append([d[0], d[1]])
                    step = d[0] * d[1]
                else:
                    pat.append([step, d])
                    step *= d
            return bass.AP(psum, parts[0] * 4096 + b * 512 + off, [[4096, parts[1]]] + pat[::-1])

        ident = mem("ident", 0, P)
        ones = mem("ones", 0, P)
        W = [mem("w0", 0, KD, 512), mem("w1", 0, KD, 512)]

        def wslot(i):
            return W[i % 2]

        COL_EPS, COL_LB, COL_OMLB, COL_ON, COL_L0, COL_L1 = 0, 8, 16, 24, 40, 48
        COL_SS, COL_RMS, COL_RSTD = 56, 60, 64
        col = lambda c, n=1: mem("cols", c, n)

        stream = []

        def w_cols(ap, n0, n=512):
            return ap.rearrange("(k p) n -> p k n", p=P)[:, :, n0:n0 + n]

        marks = {}
        MOD_EARLY = 10

        def add(name, items):
            marks[name] = len(stream)
            stream.extend(items)

        ada, kva, win = A["ada_w"], A["kv_ada_w"], A["hgrn_w_in"]
        add("mod0", [w_cols(ada[0], 512 * j) for j in range(MOD_EARLY)])
        add("hgrn_in", [w_cols(win[0], D * part + 512 * c) for part in (1, 0, 2, 3) for c in range(2)])
        add("hgrn_out", [w_cols(A["hgrn_w_out"][0], 512 * c) for c in range(2)])
        add("peer_q0", [w_cols(A["peer_w_q"][0], 512 * c) for c in range(2)])
        add("mod1", [w_cols(ada[0], 512 * j) for j in range(MOD_EARLY, 12)] + [w_cols(kva, 512 * j) for j in range(4)] + [w_cols(ada[1], 512 * j) for j in range(12)])
        add("kv", [w_cols(A["kv_w"], 512 * c) for c in range(4)])
        add("sb_q", [w_cols(A["sb_w_q"][0], 512 * c) for c in range(2)])
        add("sb_out", [w_cols(A["sb_w_out"][0], 512 * c) for c in range(2)])
        add("peer_q1", [w_cols(A["peer_w_q"][1], 512 * c) for c in range(2)])
        w2 = A["w_in_2"][0]
        w2q = w2.rearrange("(k p) n -> p k n", p=P)[:, :, 1024:1536].rearrange("p k (a j c) -> a p k j c", a=2, c=64)
        add("in2", [w_cols(w2, 0), w_cols(w2, 512), w2q, w_cols(w2, 1536, 256)]
            + [w_cols(w2, 1792 + 512 * c) for c in range(4)])
        add("conv_out", [A["w_conv_out_2"][0].rearrange("(k p) n -> p k n", p=P)])
        add("attn_out", [A["w_attn_out_2"][0].rearrange("(a j p) n -> a p j n", a=2, p=64)])
        add("out2", [w_cols(A["w_out_2"][0], 512 * c) for c in range(2)])

        def load_weights(sp):
            for i, src in enumerate(stream):
                if i >= 2:
                    sp.wait_ge(sem("w_used"), i - 1)
                for l in range(2):
                    if 0 <= i - MOD_W[l] < len(MODS[l]):
                        mod_bias_dma(sp, l, i - MOD_W[l])
                if i == marks["in2"] + 2:
                    dst = wslot(i).rearrange("p k (j a c) -> p k j a c", a=2, c=64)
                    for a in range(2):
                        for k in range(KD):
                            sp.dma_start(dst[:, k, :, a, :], src[a][:, k]).then_inc(sem(f"w_ready{i % 2}"), 16)
                    continue
                if i == marks["attn_out"]:
                    dst = wslot(i).rearrange("p k n -> p (k n)").rearrange("p (j n) -> p j n", n=D)
                    for a in range(2):
                        sp.dma_start(dst[64 * a:64 * a + 64], src[a]).then_inc(sem(f"w_ready{i % 2}"), 16)
                    continue
                dst = wslot(i)
                if i == marks["conv_out"]:
                    dst = dst.rearrange("p k n -> p (k n)").rearrange("p (j n) -> p j n", n=D)
                elif src.shape[2] != 512:
                    dst = dst[:, :, 0:src.shape[2]]
                sp.dma_start(dst, src).then_inc(sem(f"w_ready{i % 2}"), 16)

        def w_arrived(pe, i):
            n = i // 2 + 1
            for c, more in ((marks["in2"] + 2, 2 * KD - 1), (marks["attn_out"], 1)):
                if i >= c and i % 2 == c % 2:
                    n += more
            pe.wait_ge(sem(f"w_ready{i % 2}"), 16 * n)

        ENG = ("pe", "act", "dve", "pool")

        def enter(eng, n):
            if n:
                for e in ENG:
                    eng.wait_ge(sem(f"left_{e}"), n)

        def leave(eng, who):
            eng.drain().then_inc(sem(f"left_{who}"), 1)

        chained = {"dve": 0, "act": 0, "pool": 0}

        def linker(eng, who):
            def link(ins):
                chained[who] += 1
                ins.then_inc(sem(f"chain_{who}"), 1)
                eng.wait_ge(sem(f"chain_{who}"), chained[who])
            return link

        def matmuls(pe, o, lhs, rhs, n, start=True, stop=True):
            for k in range(n):
                last = pe.matmul(o, lhsT=lhs(k), rhs=rhs(k), start=start and k == 0, stop=stop and k == n - 1)
            return last

        H = lambda t, n0=0, n=D: mem("h", t * D + n0, n)
        MOD0 = dict(sh1=("moda", 0), sc1=("moda", 1), g1=("moda", 2), sh2=("moda", 3), sc2=("moda", 4), g2=("moda", 5))
        names1 = ["shkv", "sckv", "sh1", "sc1", "g1", "sh2", "sc2", "g2"]
        MOD1 = {n: ("r5", i) for i, n in enumerate(names1)}
        mod = lambda m, n0=0, n=D: mem(m[0], m[1] * D + n0, n)

        def bias_row(l, j):
            return A["ada_b"][l:l + 1, 512 * j:512 * j + 512]

        mods0 = [(bias_row(0, j), MOD0[n], half, n[:2] == "sc") for j in range(12)
                 for n, half in [(["sh1", "sc1", "g1", "sh2", "sc2", "g2"][j // 2], j % 2)]]
        mods1 = [((A["kv_ada_b"].rearrange("(a n) -> a n", a=1)[:, 512 * j:512 * j + 512] if j < 4 else bias_row(1, j - 4)),
                  MOD1[names1[j // 2]], j % 2, names1[j // 2][:2] == "sc") for j in range(16)]
        MODS = {0: mods0[:MOD_EARLY], 1: mods0[MOD_EARLY:] + mods1}
        MOD_BANKS = {0: (0, 1), 1: (0, 1)}
        MOD_ROWS = {0: lambda i: mem("t", 2 * D + 512 * (i % 2), 512, parts=(0, 1)),
                    1: lambda i: mem("not_first", 0, 512, parts=(0, 1)) if i % 2 else mem("moda", 4 * D + 512, 512, parts=(0, 1))}
        MOD_W = {0: marks["mod0"], 1: marks["mod1"]}

        def mod_pe(pe, l, js):
            for j in js:
                g = j + MOD_EARLY * l
                if g >= 2:
                    pe.wait_ge(sem("mod_out"), g - 1)
                pe.wait_ge(sem(f"mod_bias{g % 2}"), 16 * (g // 2 + 1))
                w_arrived(pe, MOD_W[l] + j)
                w = wslot(MOD_W[l] + j)
                o = bank(MOD_BANKS[l][j % 2])
                matmuls(pe, o, lambda k: mem("c_rep", k * P, P), lambda k: w[:, k, :], KD, stop=False)\
                    .then_inc(sem("w_used"), 1)
                pe.matmul(o, lhsT=mem("ones", 0, P, parts=(0, 1)), rhs=MOD_ROWS[l](j), start=False, stop=True)\
                    .then_inc(sem("mod_sum"), 1)

        def mod_act(act, l, js):
            for j in js:
                g = j + MOD_EARLY * l
                _, slot, half, is_scale = MODS[l][j]
                act.wait_ge(sem("mod_sum"), g + 1)
                act.activation(mod(slot, 512 * half, 512), bank(MOD_BANKS[l][j % 2]), ACT.Identity,
                               bias=col(COL_EPS + 1) if is_scale else 0.0).then_inc(sem("mod_out"), 1)

        def mod_bias_dma(eng, l, j):
            g = j + MOD_EARLY * l
            if g >= 2:
                eng.wait_ge(sem("mod_sum"), g - 1)
            if l == 1 and j == 0:
                eng.wait_ge(sem("norm_xn"), 2 * TT)
            eng.dma_start(MOD_ROWS[l](j), MODS[l][j][0]).then_inc(sem(f"mod_bias{g % 2}"), 16)

        def setup_sp(sp):
            sp.dma_start(mem("tiny", 0, KD), A["c"][0].rearrange("(k p) -> p k", p=P),
                         allow_slow_non_contiguous=True).then_inc(sem("c_in"), 16)

        def setup_pool(pool):
            pool.memset(mem("ones", 0, P), 1.0)
            pool.memset(mem("negones", 0, P), -1.0)
            pool.memset(mem("ident", 0, P), 0.0)
            pool.memset(mem("not_first", 0, SEQ), 1.0)
            pool.memset(mem("cols", COL_EPS, 1), EPS)
            pool.iota(mem("iota", 0, 64), pattern=[[1, 64]], base=0, channel_multiplier=0,
                      allow_small_or_imprecise_dtypes=True)
            pool.memset(mem("chunk_causal", 0, P, dt=I32), 1)
            link = linker(pool, "pool")
            link(pool.memset(mem("cols", COL_EPS + 1, 1), 1.0))
            pool.affine_select(out=ident, in_=ident, compare_op=ALU.not_equal, fill=1.0, base=0,
                               pattern=[[-1, P]], channel_multiplier=1)
            nf = mem("not_first", 0, SEQ // CHUNK, CHUNK)
            pool.affine_select(out=nf, in_=nf, compare_op=ALU.not_equal, fill=0.0, base=0,
                               pattern=[[0, SEQ // CHUNK], [1, CHUNK]], channel_multiplier=0)
            pool.affine_select(out=mem("negtri", 0, P), in_=mem("negones", 0, P), compare_op=ALU.is_ge, fill=0.0,
                               base=0, pattern=[[-1, P]], channel_multiplier=1)
            pool.affine_select(out=mem("before", 0, P), in_=ones, compare_op=ALU.is_gt, fill=0.0,
                               base=0, pattern=[[1, P]], channel_multiplier=-1)
            cc = mem("chunk_causal", 0, CPT, CHUNK, dt=I32)
            link(pool.affine_select(out=cc, in_=cc, compare_op=ALU.is_ge, fill=0.0, base=0,
                                    pattern=[[-CHUNK, CPT], [0, CHUNK]], channel_multiplier=1))
            pool.affine_select(out=cc, in_=cc, compare_op=ALU.is_ge, fill=0.0, base=0,
                               pattern=[[CHUNK, CPT], [1, CHUNK]], channel_multiplier=-1)
            pool.drain().then_inc(sem("consts"), 1)

        def setup_act(act):
            act.dma_start(mem("cols", COL_L0, 8), A["hgrn_lb_logits"][0].rearrange("(h p) -> p h", p=P),
                          allow_slow_non_contiguous=True).then_inc(sem("cols_in"), 16)
            act.dma_start(mem("cols", COL_L1, 8), A["hgrn_lb_logits"][1].rearrange("(h p) -> p h", p=P),
                          allow_slow_non_contiguous=True).then_inc(sem("cols_in"), 16)
            act.dma_start(mem("cols", COL_ON, 8), A["hgrn_onorm_g"][0].rearrange("(h p) -> p h", p=P),
                          allow_slow_non_contiguous=True).then_inc(sem("cols_in"), 16)
            act.dma_start(mem("t", 0, D), A["norm_mix_g"][0:1].broadcast_to([P, D])).then_inc(sem("g_in"), 16)
            act.dma_start(mem("t", D, D), A["norm_ffn_g"][0:1].broadcast_to([P, D])).then_inc(sem("g_in"), 16)
            act.wait_ge(sem("c_in"), 16)
            act.activation(mem("tiny", 8, KD), mem("tiny", 0, KD), ACT.Silu).then_inc(sem("c_silu"), 1)
            act.wait_ge(sem("lb_diff"), 1)
            act.activation(mem("cols", COL_LB, 8), mem("cols", COL_L0, 8), ACT.Sigmoid).then_inc(sem("lb"), 1)
            mod_act(act, 0, range(2))
            act.dma_start(mem("h", 0, TT, D), A["x"][0].rearrange("(t p) d -> p t d", p=P)).then_inc(sem("x_in"), 16)
            mod_act(act, 0, range(2, MOD_EARLY))

        def setup_dve(dve):
            link = linker(dve, "dve")
            dve.wait_ge(sem("c_silu"), 1)
            dve.tensor_copy(mem("c_rep", 0, KD, P), mem("tiny", 8, (1, KD), (0, P))).then_inc(sem("c_rep"), 1)
            dve.wait_ge(sem("cols_in"), 48)
            dve.tensor_tensor(mem("cols", COL_L0, 8), mem("cols", COL_L0, 8), mem("cols", COL_L1, 8), ALU.subtract)\
               .then_inc(sem("lb_diff"), 1)
            dve.wait_ge(sem("consts"), 1)
            dve.wait_ge(sem("lb"), 1)
            dve.tensor_scalar(mem("cols", COL_OMLB, 8), mem("cols", COL_LB, 8), -1.0, 1.0, ALU.mult, ALU.add)
            dve.wait_ge(sem("g_in"), 32)
            dve.wait_ge(sem("mod_out"), 4)
            dve.tensor_tensor(mod(MOD0["sc1"]), mod(MOD0["sc1"]), mem("t", 0, D), ALU.mult)
            dve.wait_ge(sem("mod_out"), 10)
            dve.tensor_tensor(mod(MOD0["sc2"]), mod(MOD0["sc2"]), mem("t", D, D), ALU.mult)
            dve.wait_ge(sem("x_in"), 16)

        def setup_pe(pe):
            pe.wait_ge(sem("consts"), 1)
            pe.wait_ge(sem("c_rep"), 1)
            mod_pe(pe, 0, range(MOD_EARLY))

        norms_turned, norms_rooted = [0], [0]

        def norm(n, scale, shift, xn, xT, again=False, ready=None):
            rooted = norms_rooted[0] * TT
            norms_rooted[0] += not again
            first = n * TT
            turned = norms_turned[0] * 2 * TT
            norms_turned[0] += xT is not None

            def act_part(act):
                for t in range(0 if again else TT):
                    if ready:
                        ready(act, t)
                    act.activation(mem("t", 2 * D, D), H(t), ACT.Square,
                                   accum_out=mem("cols", COL_SS + t, 1)).then_inc(sem("norm_sq"), 1)
                    act.wait_ge(sem("norm_sq"), rooted + t + 1)
                    act.activation(mem("cols", COL_RMS + t, 1), mem("cols", COL_SS + t, 1), ACT.Sqrt, scale=1.0 / D,
                                   bias=col(COL_EPS)).then_inc(sem("norm_rms"), 1)
                if xT is not None:
                    for t in range(TT):
                        for a in range(2):
                            act.wait_ge(sem("norm_tr"), turned + 2 * t + a + 1)
                            act.activation(mem(xT, 4 * a * SEQ + t * P, (SEQ, 4), P),
                                           bank((2 * t + a) % 4, 0, 4, P), ACT.Copy).then_inc(sem("norm_xT"), 1)

            def dve_part(dve):
                link = linker(dve, "dve")
                for t in range(TT):
                    if not again:
                        dve.wait_ge(sem("norm_rms"), rooted + t + 1)
                        link(dve.reciprocal(mem("cols", COL_RSTD + t, 1), mem("cols", COL_RMS + t, 1)))
                    if xn is xn_temp and t >= 2:
                        dve.wait_ge(sem("norm_tr"), turned + 2 * (t - 1))
                    ins = dve.scalar_tensor_tensor(xn(t), H(t), mem("cols", COL_RSTD + t, 1), scale, ALU.mult, ALU.mult)
                    if shift is not None:
                        link(ins)
                        ins = dve.tensor_tensor(xn(t), xn(t), shift, ALU.add)
                    ins.then_inc(sem("norm_xn"), 1)

            def pe_part(pe):
                if xT is None:
                    return
                for t in range(TT):
                    pe.wait_ge(sem("norm_xn"), first + t + 1)
                    for a in range(2):
                        g = 2 * t + a
                        if g >= 4:
                            pe.wait_ge(sem("norm_xT"), turned + g - 3)
                        for j in range(4):
                            last = pe.transpose(bank(g % 4, j * P, P), xn(t)[:, (4 * a + j) * P:(4 * a + j + 1) * P], ident)
                        last.then_inc(sem("norm_tr"), 1)
            return dict(pe=pe_part, act=act_part, dve=dve_part)

        xn_temp = lambda t: mem("t", (t % 2) * D, D)
        XT = lambda r, k, t0=0, n=SEQ: mem(r, k * SEQ + t0, n)

        def out_proj(nth, first, lhs, kn, gate, n_chunks=2):
            banks = 8
            before = nth * n_chunks * TT

            def pe_part(pe):
                for c in range(n_chunks):
                    w_arrived(pe, first + c)
                    w = wslot(first + c)
                    for t in range(TT):
                        g = c * TT + t
                        ins = matmuls(pe, bank(g % banks), lambda k: lhs(k, t), lambda k: w[:, k, :], kn)
                        ins.then_inc(sem("proj_mm"), 1)
                    pe.drain().then_inc(sem("w_used"), 1)

            def dve_part(dve):
                link = linker(dve, "dve")
                for c in range(n_chunks):
                    for t in range(TT):
                        g = c * TT + t
                        dve.wait_ge(sem("proj_mm"), before + g + 1)
                        src = bank(g % banks)
                        if gate is not None:
                            tmp = mem("t", (g % 4) * 512, 512)
                            link(dve.tensor_tensor(tmp, src, mod(gate, 512 * c, 512), ALU.mult))
                            src = tmp
                        ins = dve.tensor_tensor(H(t, 512 * c, 512), H(t, 512 * c, 512), src, ALU.add)
                        if c == n_chunks - 1:
                            ins.then_inc(sem("rows_done"), 1)

            def ready(act, t):
                act.wait_ge(sem("rows_done"), nth * TT + t + 1)
            return dict(pe=pe_part, dve=dve_part, ready=ready)

        FM = lambda r, h, t0=0, n=SEQ: mem(r, h * SEQ + t0, n)
        EXP_LAST = lambda h=0, n=HEADS: mem("tiny", 128 + h * 32, n * 32)

        def hgrn_in_pe(pe):
            c0 = marks["hgrn_in"]
            for c in range(8):
                w_arrived(pe, c0 + c)
                w = wslot(c0 + c)
                for j in range(4):
                    b = (4 * c + j) % 8
                    if 2 <= c < 4:
                        pe.wait_ge(sem("f_out"), 4 * (c - 2) + j + 1)
                    elif 4 <= c < 6:
                        pe.wait_ge(sem("q_out"), 4 * (c - 4) + j + 1)
                    elif c >= 6:
                        pe.wait_ge(sem("v_out"), 4 * (c - 6) + j + 1)
                    if 4 <= c < 6:
                        ins = matmuls(pe, bank(b), lambda k: XT("r0", k, j * P, P), lambda k: w[:, k, :], KD)
                    else:
                        ins = matmuls(pe, bank(b), lambda k: w[:, k, j * P:(j + 1) * P], lambda k: XT("r0", k), KD)
                    ins.then_inc(sem("hg_mm"), 1)
                pe.drain().then_inc(sem("w_used"), 1)

        def hgrn_in_act(act):
            for h in range(HEADS):
                act.wait_ge(sem("hg_mm"), h + 1)
                act.activation(FM("r1", h), bank(h), ACT.Sigmoid).then_inc(sem("f_out"), 1)
            for h in range(HEADS):
                act.wait_ge(sem("hg_mm"), 8 + h + 1)
                act.activation(FM("r3", h), bank(h), ACT.Silu).then_inc(sem("q_out"), 1)
            for h in range(HEADS):
                act.wait_ge(sem("fgate"), h + 1)
                act.activation(FM("r2", h), FM("r1", h), ACT.Ln).then_inc(sem("ln_f"), 1)
            for h in range(HEADS):
                act.wait_ge(sem("cum"), h + 1)
                if h >= 2:
                    act.wait_ge(sem("qd"), h - 1)
                act.activation(mem("t", (h % 2) * SEQ, SEQ), FM("r2", h), ACT.Exp).then_inc(sem("e_cum"), 1)
                act.activation(FM("r4", h), FM("r2", h), ACT.Exp, scale=-1.0)
                act.activation(EXP_LAST(h, 1), mem("r2", h * SEQ + CHUNK - 1, (CHUNK, SEQ // CHUNK)), ACT.Exp)\
                   .then_inc(sem("e_neg"), 1)
            for h in range(HEADS):
                act.wait_ge(sem("rest"), h + 1)
                act.activation(FM("r2", h), FM("r2", h), ACT.Exp).then_inc(sem("e_rest"), 1)
            for h in range(HEADS):
                act.wait_ge(sem("hg_mm"), 24 + h + 1)
                act.activation(FM("r5", h), bank(h), ACT.Silu)

        def hgrn_in_dve(dve):
            for h in range(HEADS):
                dve.wait_ge(sem("f_out"), h + 1)
                dve.tensor_scalar(FM("r1", h), FM("r1", h), mem("cols", COL_OMLB + h, 1), mem("cols", COL_LB + h, 1),
                                  ALU.mult, ALU.add).then_inc(sem("fgate"), 1)
            for h in range(HEADS):
                dve.wait_ge(sem("ln_f"), h + 1)
                dve.tensor_scalar(FM("r1", h), FM("r1", h), -1.0, 1.0, ALU.mult, ALU.add)
                dve.tensor_tensor_scan(FM("r2", h), mem("not_first", 0, SEQ), FM("r2", h), 0.0, ALU.mult, ALU.add)\
                   .then_inc(sem("cum"), 1)
            for c in range(8):
                dve.wait_ge(sem("hg_mm"), 16 + c + 1)
                dve.tensor_copy(mem("r6", (c % 4) * D + (c // 4) * 512, 512), bank(c)).then_inc(sem("v_out"), 1)
                h = c
                dve.wait_ge(sem("e_cum"), h + 1)
                dve.tensor_tensor(FM("r3", h), FM("r3", h), mem("t", (h % 2) * SEQ, SEQ), ALU.mult).then_inc(sem("qd"), 1)
                dve.wait_ge(sem("e_neg"), h + 1)
                dve.tensor_tensor(FM("r4", h), FM("r4", h), FM("r1", h), ALU.mult)
                x = mem("r2", h * SEQ, SEQ // CHUNK, CHUNK)
                last = mem("r2", h * SEQ + CHUNK - 1, (CHUNK, SEQ // CHUNK), (0, CHUNK))
                dve.tensor_tensor(mem("t", D + (h % 2) * SEQ, SEQ // CHUNK, CHUNK), last, x, ALU.subtract).then_inc(sem("rest_t"), 1)
                dve.wait_ge(sem("rest_t"), h + 1)
                dve.tensor_copy(FM("r2", h), mem("t", D + (h % 2) * SEQ, SEQ)).then_inc(sem("rest"), 1)
            for h in range(HEADS):
                dve.wait_ge(sem("e_rest"), h + 1)
                dve.tensor_tensor(FM("r1", h), FM("r1", h), FM("r2", h), ALU.mult)

        LEVELS = 4
        SCT = lambda t, h, n=1: mem("r0", t * D + h * P, n * P)
        STATE = lambda par, h, n=1: mem("r4", par * D + h * P, n * P)
        K2 = lambda par, h, n=1: mem("r4", 2 * D + par * D + h * P, n * P)
        MASK = lambda lv, *dims: mem("chunk_causal", 0, *dims, dt=I32) if lv == 0 else mem("not_first", (lv - 1) * P, *dims, dt=I32)
        NCH = SEQ // CHUNK
        DECAY_AT = [(("tiny", 128)), ("t", 0), ("t", HEADS * NCH // 2), ("t", HEADS * NCH * 3 // 4)]

        def decay(lv, t, odd, n, w):
            per = NCH >> lv
            region, off = DECAY_AT[lv]
            return mem(region, off + t * (per // TT) + odd, (per, HEADS), (2, n), (0, w))

        def hgrn_scan_pool(pool):
            link = linker(pool, "pool")
            for t in range(TT):
                pool.memset(SCT(t, 0, HEADS), 0.0)
            link(pool.memset(mem("not_first", 0, 3 * P, dt=I32), 0))
            for lv in range(1, LEVELS):
                w = CHUNK << (lv - 1)
                n = P // (2 * w)
                view = mem("not_first", (lv - 1) * P + w, (2 * w, n), w, dt=I32)
                link(pool.memset(view, 1))
                link(pool.affine_select(out=view, in_=view, compare_op=ALU.is_ge, fill=0.0, base=0,
                                        pattern=[[-2 * w, n], [0, w]], channel_multiplier=1))
                link(pool.affine_select(out=view, in_=view, compare_op=ALU.is_ge, fill=0.0, base=w - 1,
                                        pattern=[[2 * w, n], [0, w]], channel_multiplier=-1))
            pool.sem_inc(sem("masks"), 1)
            zero_slots(pool)

        def hgrn_scan_pe(pe):
            for lv in range(LEVELS):
                for t in range(TT):
                    if lv:
                        pe.wait_ge(sem("level"), (lv - 1) * TT + t + 1)
                    for a in range(2):
                        for j in range(4):
                            h = 4 * a + j
                            last = pe.matmul(bank(2 * t + a, j * P, P), lhsT=FM("r1" if lv else "r4", h, t * P, P),
                                             rhs=FM("r3", h, t * P, P), start=True, stop=True)
                        last.then_inc(sem("sc_mm"), 1)
            pe.wait_ge(sem("level"), LEVELS * TT)
            for t in range(TT):
                if t + 1 < TT:
                    for a in range(2):
                        if t:
                            pe.wait_ge(sem("k2_out"), 2 * (t - 1) + a + 1)
                        for j in range(4):
                            last = pe.transpose(bank(6 + a, j * P, P), FM("r1", 4 * a + j, t * P, P), ident)
                        last.then_inc(sem("k2_tr"), 1)
                if t:
                    for a in range(2):
                        if t > 1:
                            pe.wait_ge(sem("o_out"), 2 * (t - 1) + a + 1)
                        pe.wait_ge(sem("state"), 2 * (t - 1) + a + 1)
                        outputs(pe, t, a)
                else:
                    for a in range(2):
                        outputs(pe, t, a)
                if t + 1 < TT:
                    for a in range(2):
                        pe.wait_ge(sem("k2_out"), 2 * t + a + 1)
                        if t >= 2:
                            pe.wait_ge(sem("state"), 2 * (t - 2) + a + 1)
                        for j in range(4):
                            h = 4 * a + j
                            last = pe.matmul(bank(2 + 2 * (t % 2) + a, j * P, P), lhsT=K2(t % 2, h),
                                             rhs=mem("r6", t * D + h * P, P), start=True, stop=True)
                        last.then_inc(sem("delta"), 1)

        def outputs(pe, t, a):
            if t == 1:
                pe.wait_ge(sem("o_out"), a + 1)
            for j in range(4):
                h = 4 * a + j
                last = pe.matmul(bank(a, j * P, P), lhsT=mem("r6", t * D + h * P, P), rhs=SCT(t, h), start=True, stop=t == 0)
                if t:
                    last = pe.matmul(bank(a, j * P, P), lhsT=STATE(t % 2, h), rhs=FM("r3", h, t * P, P), start=False, stop=True)
            last.then_inc(sem("o_mm"), 1)

        def hgrn_scan_act(act):
            for t in range(TT):
                if t + 1 < TT:
                    for a in range(2):
                        act.wait_ge(sem("k2_tr"), 2 * t + a + 1)
                        if t >= 2:
                            act.wait_ge(sem("delta"), 2 * (t - 2) + a + 1)
                        act.activation(K2(t % 2, 4 * a, 4), bank(6 + a), ACT.Copy).then_inc(sem("k2_out"), 1)
                for a in range(2):
                    act.wait_ge(sem("o_mm"), 2 * t + a + 1)
                    act.activation(mem("r2", 4 * a * SEQ + t * P, (SEQ, 4), P), bank(a, 0, 4, P), ACT.Copy)\
                       .then_inc(sem("o_out"), 1)

        def hgrn_scan_dve(dve):
            link = linker(dve, "dve")
            for lv in range(1, LEVELS):
                n = HEADS * (NCH >> lv)
                (src, so), (dst, do) = DECAY_AT[lv - 1], DECAY_AT[lv]
                link(dve.tensor_tensor(mem(dst, do, n), mem(src, so, (2, n)), mem(src, so + 1, (2, n)), ALU.mult))
            dve.wait_ge(sem("masks"), 1)
            for lv in range(LEVELS):
                w = (CHUNK << lv) // 2
                n = P // (2 * w)
                for t in range(TT):
                    for a in range(2):
                        dve.wait_ge(sem("sc_mm"), 2 * (lv * TT + t) + a + 1)
                        last = dve.copy_predicated(mem("r0", t * D + 4 * a * P, 4, P), MASK(lv, (0, 4), P), bank(2 * t + a, 0, 4, P))
                    if lv:
                        q = mem("r3", t * P + w, (SEQ, HEADS), (2 * w, n), w)
                        k = mem("r1", t * P, (SEQ, HEADS), (2 * w, n), w)
                        dve.tensor_tensor(q, q, decay(lv - 1, t, 0, n, w), ALU.mult)
                        last = dve.tensor_tensor(k, k, decay(lv - 1, t, 1, n, w), ALU.mult)
                    last.then_inc(sem("level"), 1)
                    dve.wait_ge(sem("level"), lv * TT + t + 1)
            for t in range(TT - 1):
                for a in range(2):
                    dve.wait_ge(sem("delta"), 2 * t + a + 1)
                    if t == 0:
                        last = dve.tensor_copy(STATE(1, 4 * a, 4), bank(2 + a))
                    else:
                        dve.wait_ge(sem("state"), 2 * (t - 1) + a + 1)
                        if t >= 2:
                            dve.wait_ge(sem("o_mm"), 2 * (t - 1) + a + 1)
                        for j in range(4):
                            h = 4 * a + j
                            region, off = DECAY_AT[LEVELS - 1]
                            last = dve.scalar_tensor_tensor(STATE((t + 1) % 2, h), STATE(t % 2, h),
                                                            mem(region, off + h * TT + t, 1),
                                                            bank(2 + 2 * (t % 2) + a, j * P, P), ALU.mult, ALU.add)
                    last.then_inc(sem("state"), 1)

        def hgrn_out_norm_act(act):
            for h in range(HEADS):
                act.activation(FM("r1", h), FM("r2", h), ACT.Square).then_inc(sem("osq"), 1)
            for h in range(HEADS):
                act.wait_ge(sem("osq_mm"), h + 1)
                act.activation(FM("r4", h), bank(h), ACT.Ln, scale=1.0 / P, bias=col(COL_EPS)).then_inc(sem("o_ln"), 1)
            for h in range(HEADS):
                act.wait_ge(sem("o_ln"), h + 1)
                act.activation(FM("r4", h), FM("r4", h), ACT.Exp, scale=-0.5).then_inc(sem("o_rstd"), 1)

        def hgrn_out_norm_pe(pe):
            for h in range(HEADS):
                pe.wait_ge(sem("osq"), h + 1)
                pe.matmul(bank(h), lhsT=ones, rhs=FM("r1", h), start=True, stop=True).then_inc(sem("osq_mm"), 1)

        def hgrn_out_norm_dve(dve):
            for h in range(HEADS):
                dve.scalar_tensor_tensor(FM("r5", h), FM("r5", h), mem("cols", COL_ON + h, 1), FM("r2", h),
                                         ALU.mult, ALU.mult).then_inc(sem("o_gated"), 1)
            for h in range(HEADS):
                dve.wait_ge(sem("o_gated"), h + 1)
                dve.wait_ge(sem("o_rstd"), h + 1)
                dve.tensor_tensor(FM("r2", h), FM("r5", h), FM("r4", h), ALU.mult)

        Q2 = 2 * PH
        NG = NSEL // GR
        NR = 4
        TURNS = NG // NR
        DVE_ROWS = 2
        RING = lambda r, k: mem(("r2", "r4", "r3", ("moda", "moda", "moda", "t")[k])[r], k * D if r < 3 else (0, 1, 3, 2)[k] * D, D)
        SK_RAW = mem("r3", 0, Q2, P)
        SKT = lambda g, n=1: mem("r3", D + g * P, n * P)
        SC = lambda t, g: mem("r1", t * D + g * P, P)
        SC_REST = lambda g: mem("t", g * P, P)
        DIAG = lambda i: mem("t", D + i * P, P)
        small = lambda off, *dims, dt=None: mem("moda", 2 * D + off, *dims, dt=dt)
        O_V, O_I, O_IF, O_BEST, O_FLAT, O_A, O_B, O_AF, O_BF, O_E1, O_E2 = 0, 128, 256, 384, 448, 512, 576, 640, 704, 768, 832
        O_SUM, O_HH, O_ST = 896, 912, 928
        par_small = lambda off, t, *dims, dt=None: mem("moda", 4 * D + (t % 2) * 256 + off, *dims, dt=dt)
        par_reg = lambda off, t: layout["moda"] + 4 * D + (t % 2) * 256 + off
        O_GATE, O_IDX, O_HID, O_W = 0, 64, 128, 192

        def peer_load_keys(act, l):
            act.dma_start(SK_RAW, A["peer_subkeys"][l].rearrange("h p n d -> n (h p) d")).then_inc(sem("keys_in"), 16)

        def peer_query(l):
            first = marks[f"peer_q{l}"]

            def pe_part(pe):
                for c in range(2):
                    w_arrived(pe, first + c)
                    w = wslot(first + c)
                    for j in range(4):
                        matmuls(pe, bank(4 * c + j), lambda k: w[:, k, j * P:(j + 1) * P], lambda k: XT("r1", k), KD)\
                            .then_inc(sem("pq_mm"), 1)
                    pe.drain().then_inc(sem("w_used"), 1)
                pe.wait_ge(sem("keys_in"), 16 * (l + 1))
                for a in range(2):
                    pe.wait_ge(sem("pq_out"), Q2 * l + a + 1)
                    for j in range(4):
                        last = pe.transpose(bank(a, j * P, P), SK_RAW[:, 4 * a + j, :], ident)
                    last.then_inc(sem("key_tr"), 1)
                pe.wait_ge(sem("pq_out"), Q2 * (l + 1))
                pe.wait_ge(sem("skt"), 2 * (l + 1))
                for t in range(TT):
                    for a in range(2):
                        for j in range(4):
                            g = 4 * a + j
                            last = pe.matmul(bank(2 * t + a, j * P, P), lhsT=FM("r2", g, t * P, P), rhs=SKT(g),
                                             start=True, stop=True)
                        last.then_inc(sem("sc_mm_p"), 1)

            def act_part(act):
                for g in range(Q2):
                    act.wait_ge(sem("pq_mm"), Q2 * l + g + 1)
                    act.activation(FM("r2", g), bank(g), ACT.Copy).then_inc(sem("pq_out"), 1)
                for a in range(2):
                    act.wait_ge(sem("key_tr"), 2 * l + a + 1)
                    act.activation(SKT(4 * a, 4), bank(a), ACT.Copy).then_inc(sem("skt"), 1)
                for i in range(2 * TT):
                    act.wait_ge(sem("sc_mm_p"), 2 * TT * l + i + 1)
                    act.activation(mem("r1", i * 512, 512), bank(i), ACT.Copy)
            return dict(pe=pe_part, act=act_part)

        def peer(l):
            MOD = (MOD0, MOD1)[l]
            T0 = TT * l
            u_tab, v_tab = (A[n].rearrange("l n d -> (l n) d") for n in ("peer_u", "peer_v"))
            def route_dve(dve, t, link):
                V = lambda g, o, n=8: small(O_V + g * PK + o, n)
                I = lambda g, o: small(O_I + g * PK + o, 8, dt=U32)
                for g in range(Q2):
                    last = dve.max(V(g, 0), SC(t, g))
                link(last)
                for g in range(Q2):
                    dve.max_index(I(g, 0), V(g, 0), SC(t, g))
                    last = dve.match_replace(SC_REST(g), V(g, 0), SC(t, g), -3e38)
                link(last)
                for g in range(Q2):
                    last = dve.max(V(g, 8), SC_REST(g))
                link(last)
                for g in range(Q2):
                    last = dve.max_index(I(g, 8), V(g, 8), SC_REST(g))
                link(last)
                C1 = lambda h: mem("t", h * 256, 256)
                link(dve.tensor_tensor(mem("t", 0, PH, PK, PK), small(O_V, (2 * PK, PH), (1, PK), (0, PK)),
                                       small(O_V + PK, (2 * PK, PH), (0, PK), (1, PK)), ALU.add))
                dve.tensor_copy(small(O_IF, Q2 * PK), small(O_I, Q2 * PK, dt=U32))
                B = lambda h, o: small(O_BEST + h * PK + o, 8)
                Fl = lambda h, o: small(O_FLAT + h * PK + o, 8, dt=U32)
                for h in range(PH):
                    last = dve.max(B(h, 0), C1(h))
                link(last)
                for h in range(PH):
                    dve.max_index(Fl(h, 0), B(h, 0), C1(h))
                    last = dve.match_replace(C1(h), B(h, 0), C1(h), -3e38)
                link(last)
                for h in range(PH):
                    last = dve.max(B(h, 8), C1(h))
                link(last)
                gate = par_small(O_GATE, t, PH, PK)
                dve.tensor_tensor(gate, small(O_BEST, PH, PK), small(O_BEST, (PK, PH), (0, PK)), ALU.subtract)\
                   .then_inc(sem("best"), 1)
                for h in range(PH):
                    last = dve.max_index(Fl(h, 8), B(h, 8), C1(h))
                link(last)
                dve.tensor_single_scalar(small(O_A, NSEL, dt=U32), small(O_FLAT, NSEL, dt=U32), 4, ALU.logical_shift_right)
                link(dve.tensor_single_scalar(small(O_B, NSEL, dt=U32), small(O_FLAT, NSEL, dt=U32), PK - 1, ALU.bitwise_and))
                dve.tensor_copy(small(O_AF, NSEL), small(O_A, NSEL, dt=U32))
                link(dve.tensor_copy(small(O_BF, NSEL), small(O_B, NSEL, dt=U32)))
                oh = (mem("t", 0, NSEL, PK), mem("t", 0, PH, PK, PK))
                for o_sel, o_out, which in ((O_AF, O_E1, 0), (O_BF, O_E2, 1)):
                    link(dve.tensor_tensor(oh[0], small(o_sel, (1, NSEL), (0, PK)), mem("iota", 0, (0, NSEL), (1, PK)), ALU.is_equal))
                    link(dve.tensor_tensor(oh[1], oh[1], small(O_IF + which * PK, (2 * PK, PH), (0, PK), (1, PK)), ALU.mult))
                    link(dve.tensor_reduce(small(o_out, NSEL), oh[0], AXIS_X, ALU.add))
                link(dve.scalar_tensor_tensor(small(O_E1, NSEL), small(O_E1, NSEL), float(NKEYS), small(O_E2, NSEL),
                                              ALU.mult, ALU.add))
                if l:
                    link(dve.tensor_scalar(small(O_E1, NSEL), small(O_E1, NSEL), float(l * NKEYS * NKEYS), None, ALU.add))
                dve.tensor_copy(par_small(O_IDX, t, NSEL, dt=U32), small(O_E1, NSEL)).then_inc(sem("experts"), 1)

            def mod_part(t):
                n = len(MODS[1])
                return range(n * t // TT, n * (t + 1) // TT)

            def dve_used(t):
                return (T0 + t) * ((TURNS // 2) * NR + 1) + 1

            def gather_pool(pool, t, v):
                tab = (u_tab, v_tab)[v]
                used = sem(("u_used", "v_used")[v])
                base = (T0 + t) * NG

                def group(i, r):
                    st = small(O_ST + r * GR, GR, dt=U32)
                    first = isinstance(i, int) and i == 0
                    if first:
                        if v:
                            pool.wait_ge(sem("u_used"), base + NG - NR + r + 1)
                        elif T0 + t:
                            pool.wait_ge(sem("v_used"), base - NR + r + 1)
                            pool.wait_ge(sem("v_used_dve"), dve_used(t) - NR + r)
                        src = par_small(O_IDX + r * GR, t, GR, dt=U32)
                    elif isinstance(i, int):
                        pool.wait_ge(used, i * NR + (base - NR + r + 1))
                        src = par_small(O_IDX + (i * NR + r) * GR, t, GR, dt=U32)
                    else:
                        pool.wait_ge(used, i * NR + (base - NR + r + 1))
                        pool.sem_inc(sem("pool_step"), 1)
                        src = arena[:, bass.ds(i * (NR * GR) + (par_reg(O_IDX, t) + r * GR), GR)].bitcast(U32)
                    pool.tensor_copy(st, src).then_inc(sem("staged"), 1)
                    pool.wait_ge(sem("staged"), i * NR + ((2 * (T0 + t) + v) * NG + r + 1))
                    pool.sem_inc(sem("pool_step"), 1)
                    for k in range(GR):
                        pool.indirect_dma_start(RING(r, k), None, tab,
                                                bass.IndirectOffsetOnAxis(ap=st[:, k:k + 1], axis=0))\
                            .then_inc(sem(f"ring{r}"), 16)
                if not v:
                    pool.wait_ge(sem("experts"), T0 + t + 1)
                for r in range(NR):
                    group(0, r)
                with pool.Fori(1, TURNS - v) as i:
                    for r in range(NR):
                        group(i, r)
                if v:
                    for r in range(NR):
                        pool.wait_ge(sem("v_used_dve"), dve_used(t) + (TURNS // 2 - 2) * NR + r + 1)
                        group(TURNS - 1, r)

            def rows_arrived(eng, i, r, t, v):
                turns = (2 * (T0 + t) + v) * (NG // NR)
                eng.wait_ge(sem(f"ring{r}"), i * (16 * GR) + 16 * GR * (turns + 1))

            def dot_dve(dve, t):
                with dve.Fori(0, NG // NR) as i:
                    for r in range(NR):
                        rows_arrived(dve, i, r, t, 0)
                        for k in range(GR):
                            last = dve.tensor_tensor_reduce(out=RING(r, k), in0=RING(r, k), in1=mem("r0", t * D, D), scale=1.0,
                                                            scalar=0.0, op0=ALU.mult, op1=ALU.add,
                                                            accum_out=small(O_HH + (r % 2) * GR + k, 1))
                        last.then_inc(sem("dots"), 1)
                        dve.wait_ge(sem("dots"), i * NR + ((T0 + t) * NG + r + 1))
                        dve.tensor_copy(arena[:, bass.ds(i * (NR * GR) + (par_reg(O_HID, t) + r * GR), GR)],
                                        small(O_HH + (r % 2) * GR, GR)).then_inc(sem("u_used"), 1)

            def gelu_act(act, t):
                act.wait_ge(sem("u_used"), (T0 + t + 1) * NG)
                act.activation(par_small(O_W, t, NSEL), par_small(O_HID, t, NSEL), ACT.Gelu).then_inc(sem("gelu"), 1)

            def weights_dve(dve, t, link):
                gate = par_small(O_GATE, t, PH, PK)
                dve.wait_ge(sem("gate_exp"), T0 + t + 1)
                link(dve.tensor_reduce(small(O_SUM, PH), gate, AXIS_X, ALU.add))
                link(dve.reciprocal(small(O_SUM, PH), small(O_SUM, PH)))
                link(dve.tensor_tensor(gate, gate, small(O_SUM, (1, PH), (0, PK)), ALU.mult))
                dve.wait_ge(sem("gelu"), T0 + t + 1)
                dve.tensor_tensor(par_small(O_W, t, NSEL), par_small(O_W, t, NSEL), par_small(O_GATE, t, NSEL), ALU.mult)\
                   .then_inc(sem("weights"), 1)

            def diag_act(act, t):
                act.wait_ge(sem("weights"), T0 + t + 1)
                base = (T0 + t) * NG

                def groups(i, rows=GR):
                    for half in range(2):
                        if base or not isinstance(i, int):
                            act.wait_ge(sem("v_used"), i * 2 + (base + half - 1))
                        for k in range(rows):
                            ins = act.activation(DIAG(half * GR + k), ident, ACT.Copy,
                                                 scale=arena[:, bass.ds(i * (2 * GR) + (par_reg(O_W, t) + half * GR + k), 1)])
                        ins.then_inc(sem("diag"), 1)
                groups(0)
                with act.Fori(1, NG // 4) as i:
                    groups(i)
                with act.Fori(NG // 4, NG // 2) as i:
                    groups(i, GR - DVE_ROWS)

            def sum_pe(pe, t):
                base = (T0 + t) * NG
                acc = (4 + 2 * (t % 2), 5 + 2 * (t % 2))
                if T0 + t >= 2:
                    pe.wait_ge(sem("acc_used"), T0 + t - 1)

                def turn(i, rows=GR, first=False):
                    for r in range(NR):
                        rows_arrived(pe, i, r, t, 1)
                        pe.wait_ge(sem("diag"), i * NR + (base + r + 1))
                        for k in range(rows):
                            for n in range(2):
                                last = pe.matmul(bank(acc[n]), lhsT=DIAG((r % 2) * GR + k), rhs=RING(r, k)[:, n * 512:(n + 1) * 512],
                                                 start=first and r == 0 and k == 0, stop=False, skip_group_check=True)
                        last.then_inc(sem("v_used"), 1)
                turn(0, first=True)
                for i in range(1, TURNS // 2):
                    turn(i)
                with pe.Fori(TURNS // 2, TURNS) as i:
                    turn(i, GR - DVE_ROWS)

            def sum_dve(dve, t, link):
                acc = mem("t", 0, D)
                dve.memset(acc, 0.0).then_inc(sem("v_used_dve"), 1)
                with dve.Fori(TURNS // 2, TURNS) as i:
                    for r in range(NR):
                        rows_arrived(dve, i, r, t, 1)
                        for k in range(DVE_ROWS):
                            n = dve_used(t) + r - (TURNS // 2) * NR
                            if k:
                                dve.wait_ge(sem("acc"), i * (NR * (DVE_ROWS - 1)) + ((n - 1 - (T0 + t)) * (DVE_ROWS - 1) + k))
                            else:
                                dve.wait_ge(sem("v_used_dve"), i * NR + n)
                            w = arena[:, bass.ds(i * (NR * GR) + (par_reg(O_W, t) + r * GR + GR - DVE_ROWS + k), 1)]
                            dve.scalar_tensor_tensor(acc, RING(r, GR - DVE_ROWS + k), w, acc, ALU.mult, ALU.add)\
                               .then_inc(sem("acc" if k < DVE_ROWS - 1 else "v_used_dve"), 1)
                dve.wait_ge(sem("v_used_dve"), dve_used(t + 1) - 1)

            def finish_dve(dve, t, link):
                dve.wait_ge(sem("v_used"), (T0 + t + 1) * NG)
                if T0 + t == 0:
                    dve.wait_ge(sem("mod_out"), 12)
                acc = 4 + 2 * (t % 2)
                dve.tensor_tensor(mem("t", 0, 512), mem("t", 0, 512), bank(acc), ALU.add)
                link(dve.tensor_tensor(mem("t", 512, 512), mem("t", 512, 512), bank(acc + 1), ALU.add))
                link(dve.tensor_tensor(mem("t", 0, D), mem("t", 0, D), mod(MOD["g2"]), ALU.mult))
                dve.tensor_tensor(H(t), H(t), mem("t", 0, D), ALU.add).then_inc(sem("acc_used"), 1)
                dve.wait_ge(sem("acc_used"), T0 + t + 1)

            def pe_part(pe):
                for t in range(TT):
                    if l == 0:
                        mod_pe(pe, 1, mod_part(t))
                    sum_pe(pe, t)

            def act_part(act):
                for t in range(TT):
                    act.wait_ge(sem("best"), T0 + t + 1)
                    gate = par_small(O_GATE, t, NSEL)
                    act.activation(gate, gate, ACT.Exp).then_inc(sem("gate_exp"), 1)
                    if l == 0:
                        mod_act(act, 1, mod_part(t))
                    if l == 0 and t == TT - 1:
                        act.wait_ge(sem("experts"), TT)
                        scale_rows_act(act)
                    gelu_act(act, t)
                    diag_act(act, t)

            def dve_part(dve):
                link = linker(dve, "dve")
                route_dve(dve, 0, link)
                for t in range(TT):
                    dot_dve(dve, t)
                    weights_dve(dve, t, link)
                    if t + 1 < TT:
                        route_dve(dve, t + 1, link)
                    sum_dve(dve, t, link)
                    if l == 0 and t == TT - 1:
                        scale_rows_dve(dve)
                    finish_dve(dve, t, link)

            def pool_part(pool):
                for t in range(TT):
                    gather_pool(pool, t, 0)
                    gather_pool(pool, t, 1)
            return dict(pe=pe_part, act=act_part, dve=dve_part, pool=pool_part)

        def scale_rows_act(act):
            for i, row in enumerate((A["kv_norm_g"].rearrange("(a n) -> a n", a=1), A["norm_mix_g"][1:2],
                                     A["norm_ffn_g"][1:2])):
                act.dma_start(mem("r1", i * D, D), row.broadcast_to([P, D])).then_inc(sem("scale_rows"), 16)

        def scale_rows_dve(dve):
            dve.wait_ge(sem("scale_rows"), 48)
            dve.wait_ge(sem("mod_out"), 28)
            for i, m in enumerate(("sckv", "sc1", "sc2")):
                dve.tensor_tensor(mod(MOD1[m]), mod(MOD1[m]), mem("r1", i * D, D), ALU.mult)

        def kv_pe(pe):
            first = marks["kv"]
            for c in range(4):
                w_arrived(pe, first + c)
                w = wslot(first + c)
                for j in range(4):
                    if c < 2:
                        ins = matmuls(pe, bank(4 * c + j), lambda k: w[:, k, j * P:(j + 1) * P], lambda k: XT("r0", k), KD)
                    else:
                        pe.wait_ge(sem("sbk_out"), 4 * (c - 2) + j + 1)
                        ins = matmuls(pe, bank(4 * (c - 2) + j), lambda k: XT("r0", k, j * P, P), lambda k: w[:, k, :], KD)
                    ins.then_inc(sem("kv_mm"), 1)
                pe.drain().then_inc(sem("w_used"), 1)

        def kv_act(act):
            for h in range(HEADS):
                act.wait_ge(sem("kv_mm"), h + 1)
                act.activation(FM("r1", h), bank(h), ACT.Copy).then_inc(sem("sbk_out"), 1)

        def kv_dve(dve):
            for c in range(8):
                dve.wait_ge(sem("kv_mm"), 8 + c + 1)
                dve.tensor_copy(mem("r2", (c % 4) * D + (c // 4) * 512, 512), bank(c)).then_inc(sem("kv_out"), 1)

        def sbq_pe(pe):
            first = marks["sb_q"]
            for c in range(2):
                w_arrived(pe, first + c)
                w = wslot(first + c)
                for j in range(4):
                    matmuls(pe, bank(4 * c + j), lambda k: w[:, k, j * P:(j + 1) * P], lambda k: XT("r4", k), KD)\
                        .then_inc(sem("sbq_mm"), 1)
                pe.drain().then_inc(sem("w_used"), 1)

        def sbq_act(act):
            for h in range(HEADS):
                act.wait_ge(sem("sbq_mm"), h + 1)
                act.activation(FM("r3", h), bank(h), ACT.Copy, scale=float(P) ** -0.5)

        BLK = {0: 0, 1: 512, 3: 896, 2: 1024}
        NQ = [SEQ - P * n for n in range(TT)]
        NZ = sum(NQ)
        ZB = lambda h, off, n: bank(3 * (h % 2), off, n)
        ZC = lambda h, off=0, n=NZ: mem("t", (h % 2) * NZ + off, n)
        SP_ = lambda h, off=0, n=NZ: mem("moda", (h % 2) * NZ + off, n)
        AW = lambda h, off=0, n=NZ: mem("moda", (2 + h % 3) * NZ + off, n) if h % 3 < 2 else mem("r0", off, n)

        def sb_pe(pe):
            def scores(h):
                if h >= 2:
                    pe.wait_ge(sem("a_exp"), h - 1)
                for n in (0, 1, 3, 2):
                    last = pe.matmul(ZB(h, BLK[n], NQ[n]), lhsT=FM("r1", h, n * P, P), rhs=FM("r3", h, n * P, NQ[n]),
                                     start=n != 3, stop=False, skip_group_check=True)
                last.then_inc(sem("z_mm"), 1)

            def values(h):
                pe.wait_ge(sem("a_sel"), h + 1)
                if h >= 2:
                    pe.wait_ge(sem("sbo_out"), h - 1)
                for n in range(TT):
                    last = pe.matmul(bank(6 + h % 2, n * P, NQ[n]), lhsT=mem("r2", n * D + h * P, P),
                                     rhs=AW(h, BLK[n], NQ[n]), start=n == 0, stop=n == TT - 1, skip_group_check=True)
                last.then_inc(sem("av_mm"), 1)
            scores(0)
            scores(1)
            for h in range(HEADS):
                pe.wait_ge(sem("sp"), h + 1)
                for n in range(TT):
                    for m in range(n, TT):
                        last = pe.matmul(ZB(h, BLK[n] + (m - n) * P, NQ[m]), lhsT=mem("negtri" if m == n else "negones", 0, P),
                                         rhs=SP_(h, BLK[m], NQ[m]), start=False, stop=m == TT - 1, skip_group_check=True)
                last.then_inc(sem("cs_mm"), 1)
                if h:
                    values(h - 1)
                if h + 2 < HEADS:
                    scores(h + 2)
            values(HEADS - 1)

        def sb_dve(dve):
            link = linker(dve, "dve")

            def first(h):
                dve.wait_ge(sem("z_mm"), h + 1)
                link(dve.tensor_copy(ZC(h), ZB(h, 0, NZ)))
                if h >= 3:
                    dve.wait_ge(sem("av_mm"), h - 2)
                dve.scalar_tensor_tensor(AW(h), ZC(h), -1.0, ZC(h), ALU.mult, ALU.min).then_inc(sem("neg_abs"), 1)

            def second(h):
                dve.wait_ge(sem("ln1p"), h + 1)
                if h >= 2:
                    dve.wait_ge(sem("cs_mm"), h - 1)
                link(dve.scalar_tensor_tensor(SP_(h), ZC(h), 0.0, AW(h), ALU.max, ALU.add))
                for n in range(TT):
                    last = dve.tensor_tensor(SP_(h, BLK[n], P), SP_(h, BLK[n], P), mem("before", 0, P), ALU.mult)
                last.then_inc(sem("sp"), 1)
            first(0)
            first(1)
            second(0)
            second(1)
            for h in range(2, HEADS):
                first(h)
                second(h)

        def sb_act(act):
            def ln(h):
                act.wait_ge(sem("neg_abs"), h + 1)
                act.activation(AW(h), AW(h), ACT.Exp).then_inc(sem("e_abs"), 1)
                act.wait_ge(sem("e_abs"), h + 1)
                act.activation(AW(h), AW(h), ACT.Ln, bias=col(COL_EPS + 1)).then_inc(sem("ln1p"), 1)
            ln(0)
            ln(1)
            for h in range(HEADS):
                act.wait_ge(sem("cs_mm"), h + 1)
                act.activation(AW(h), ZB(h, 0, NZ), ACT.Exp).then_inc(sem("a_exp"), 1)
                if h:
                    act.wait_ge(sem("av_mm"), h)
                    act.activation(FM("r4", h - 1), bank(6 + (h - 1) % 2), ACT.Copy).then_inc(sem("sbo_out"), 1)
                if h + 2 < HEADS:
                    ln(h + 2)
            act.wait_ge(sem("av_mm"), HEADS)
            act.activation(FM("r4", HEADS - 1), bank(6 + (HEADS - 1) % 2), ACT.Copy)

        def sb_pool(pool):
            for h in range(HEADS):
                pool.wait_ge(sem("a_exp"), h + 1)
                for n in range(TT):
                    last = pool.affine_select(out=AW(h, BLK[n], P), in_=AW(h, BLK[n], P), compare_op=ALU.is_gt, fill=0.0,
                                              base=0, pattern=[[1, P]], channel_multiplier=-1)
                last.then_inc(sem("a_sel"), 1)

        ROW2 = lambda i: mem("moda", i * D, D)

        def rows2_act(act):
            for i, name in enumerate(("final_norm_g", "g_mix_2", "g_ffn_2", "g_final_2")):
                row = A[name].rearrange("(a n) -> a n", a=1) if i in (0, 3) else A[name][0:1]
                act.dma_start(ROW2(i), row.broadcast_to([P, D])).then_inc(sem("rows2"), 16)

        def rows2_dve(dve):
            dve.wait_ge(sem("rows2"), 64)

        CW, CC = 31, 4
        PADW = CW - 1 + SEQ
        CV = lambda c, o=0, n=PADW: mem("r1", c * PADW + o, n)
        Y = lambda c: mem("r2", c * SEQ, SEQ)
        CROWS = CW + 3
        CCOL = lambda c, r, n=1: mem("tiny", c * CROWS + r, n)
        Q_2 = lambda j, t0=0, n=SEQ, parts=(0, P): mem("r6", j * SEQ + t0, n, parts=parts)
        K_2 = lambda t0, n, parts=(0, P): mem("r6", 4 * SEQ + t0, n, parts=parts)
        V_2 = lambda blk, c0=0, n=P: mem("r6", 4 * SEQ + 5 * P + blk * P + c0, n)
        conv_rows = mem("r3", 0, 512, parts=(0, CROWS))

        def conv_rows_dma(act):
            act.dma_start(mem("r3", 0, 512, parts=(0, CW)), A["w_dw_2"][0].rearrange("w a c -> w (a c)")).then_inc(sem("conv_rows"), 16)
            for i, name in enumerate(("b_dw_2", "ln_conv_g_2", "ln_conv_b_2")):
                act.dma_start(mem("r3", 0, 512, parts=(CW + i, 1)), A[name][0:1]).then_inc(sem("conv_rows"), 16)

        def in2_pe(pe):
            pe.wait_ge(sem("conv_rows"), 64)
            for c in range(CC):
                last = pe.transpose(bank(7, c * CROWS, CROWS), conv_rows[:, c * P:(c + 1) * P], mem("ident", 0, CROWS, parts=(0, CROWS)))
            last.then_inc(sem("conv_tr"), 1)
            first = marks["in2"]
            g = 0
            for c in range(8):
                w_arrived(pe, first + c)
                w = wslot(first + c)
                for j in range(4 if c != 3 else 2):
                    if g == 7:
                        pe.wait_ge(sem("conv_cols"), 1)
                    if 8 <= g < 12:
                        pe.wait_ge(sem("cv_out"), g - 7)
                    elif g >= 12:
                        pe.wait_ge(sem("in2_out"), g - 11)
                    b = g % 8
                    if c == 3 and j == 1:
                        for t in range(TT):
                            for k in range(KD):
                                last = pe.matmul(bank(b, t * P, P), lhsT=XT("r0", k, t * P, P), rhs=w[:, k, P:2 * P],
                                                 start=k == 0, stop=k == KD - 1)
                    else:
                        last = matmuls(pe, bank(b), lambda k: w[:, k, j * P:(j + 1) * P], lambda k: XT("r0", k), KD)
                    last.then_inc(sem("in2_mm"), 1)
                    g += 1
                pe.drain().then_inc(sem("w_used"), 1)
            pe.wait_ge(sem("in2_out"), 26)
            pe.wait_ge(sem("conv_done"), 1)
            matmuls(pe, bank(0), lambda c: ones, lambda c: Y(c), CC).then_inc(sem("ln_sum"), 1)
            pe.wait_ge(sem("ln_sq"), CC)
            matmuls(pe, bank(1), lambda c: ones, lambda c: mem("r3", c * SEQ, SEQ), CC).then_inc(sem("ln_sum"), 1)

        def in2_act(act):
            act.wait_ge(sem("conv_tr"), 1)
            act.activation(mem("tiny", 0, CC * CROWS), bank(7, 0, CC * CROWS), ACT.Copy).then_inc(sem("conv_cols"), 1)
            for g in range(4, 30):
                act.wait_ge(sem("in2_mm"), g + 1)
                src = bank(g % 8)
                if g < 8:
                    ins = act.activation(mem("t", (g - 4) * SEQ, SEQ), src, ACT.Sigmoid)
                elif g < 12:
                    ins = act.activation(Q_2(g - 8), src, ACT.Copy, scale=0.125)
                elif g == 12:
                    ins = act.activation(K_2(P, SEQ), src, ACT.Copy)
                elif g == 13:
                    ins = act.activation(V_2(1, 0, SEQ), src, ACT.Copy)
                elif g < 22:
                    ins = act.activation(FM("r4", g - 14), src, ACT.Sigmoid)
                else:
                    ins = act.activation(FM("r5", g - 22), src, ACT.Sigmoid)
                ins.then_inc(sem("in2_out"), 1)
            for c in range(CC):
                act.wait_ge(sem("centred"), c + 1)
                act.activation(mem("r3", c * SEQ, SEQ), Y(c), ACT.Square).then_inc(sem("ln_sq"), 1)
            act.wait_ge(sem("ln_sum"), 2)
            act.activation(mem("t", 0, SEQ), bank(1), ACT.Sqrt, scale=1.0 / 512, bias=col(COL_EPS)).then_inc(sem("ln_rms"), 1)
            for c in range(CC):
                act.wait_ge(sem("normed"), c + 1)
                act.activation(Y(c), Y(c), ACT.Silu, scale=CCOL(c, CW + 1), bias=CCOL(c, CW + 2))

        def in2_pool(pool):
            pool.memset(K_2(0, P), 0.0)
            pool.memset(V_2(0), 0.0)

        def in2_dve(dve):
            link = linker(dve, "dve")
            dve.memset(mem("r1", 0, (PADW, CC), CW - 1), 0.0)
            for c in range(CC):
                dve.wait_ge(sem("in2_out"), c + 1)
                dve.tensor_tensor(CV(c, CW - 1, SEQ), bank(c), mem("t", c * SEQ, SEQ), ALU.mult).then_inc(sem("cv_out"), 1)
            dve.wait_ge(sem("cv_out"), CC)
            dve.wait_ge(sem("conv_cols"), 1)
            for c in range(CC):
                dve.tensor_scalar(Y(c), CV(c, 0, SEQ), CCOL(c, 0), CCOL(c, CW), ALU.mult, ALU.add).then_inc(sem("tap"), 1)
            with dve.Fori(0, CW - 1) as i:
                for c in range(CC):
                    dve.wait_ge(sem("tap"), i * CC + (c + 1))
                    dve.scalar_tensor_tensor(Y(c), arena[:, bass.ds(i + (layout["r1"] + c * PADW + 1), SEQ)],
                                             arena[:, bass.ds(i + (layout["tiny"] + c * CROWS + 1), 1)], Y(c),
                                             ALU.mult, ALU.add).then_inc(sem("tap"), 1)
            dve.drain().then_inc(sem("conv_done"), 1)
            dve.wait_ge(sem("ln_sum"), 1)
            for c in range(CC):
                dve.scalar_tensor_tensor(Y(c), bank(0), -1.0 / 512, Y(c), ALU.mult, ALU.add).then_inc(sem("centred"), 1)
            dve.wait_ge(sem("ln_rms"), 1)
            link(dve.reciprocal(mem("t", 0, SEQ), mem("t", 0, SEQ)))
            dve.wait_ge(sem("ln_sq"), CC)
            for c in range(CC):
                dve.tensor_tensor(Y(c), Y(c), mem("t", 0, SEQ), ALU.mult).then_inc(sem("normed"), 1)

        AH = 8
        REL = mem("r3", 0, 2 * P)
        WIN = mem("r3", 256, 2 * P)
        BIAS2 = lambda h: mem("r3", 512 + (h % 2) * 256, 2 * P)
        SINKS = lambda h=0, n=1: mem("r3", 1024 + h, n)
        st2 = lambda off, h, n=TT: mem("r3", 1040 + (h % 2) * 64 + off, n)
        S2 = lambda h, o=0, n=2 * P * TT: mem("t", (h % 2) * D + o, n)
        PT2 = lambda h, o=0, n=P: mem("moda", (4 + h % 2) * D + o, n)
        O2 = lambda h, t0=0, n=SEQ: mem("r0", (h % 4) * SEQ + t0, n, parts=(64 * (h // 4), 64))
        SLOPE = [2.0 ** (-8.0 * (h + 1) / AH) for h in range(AH)]

        def attn2_pe(pe):
            def scores(h):
                pr = (64 * (h // 4), 64)
                if h >= 2:
                    pe.wait_ge(sem("s2_out"), h - 1)
                for n in range(TT):
                    b = 2 * (h % 2) + n // 2
                    last = pe.matmul(bank(b, (n % 2) * 256, 256), lhsT=Q_2(h % 4, n * P, P, parts=pr),
                                     rhs=K_2(n * P, 2 * P, parts=pr), start=True, stop=True)
                last.then_inc(sem("s2_mm"), 1)
            scores(0)
            scores(1)
            for h in range(AH):
                pe.wait_ge(sem("p2"), h + 1)
                for a in range(2):
                    if h:
                        pe.wait_ge(sem("pt2_out"), 2 * (h - 1) + a + 1)
                    for j in range(4):
                        last = pe.transpose(bank(4 + a, j * P, P), S2(h, (4 * a + j) * P, P), ident)
                    last.then_inc(sem("pt2_tr"), 1)
                if h + 2 < AH:
                    scores(h + 2)
                pe.wait_ge(sem("pt2_out"), 2 * h + 2)
                if h >= 2:
                    pe.wait_ge(sem("o2_out"), h - 1)
                for n in range(TT):
                    for kb in range(2):
                        last = pe.matmul(bank(6 + h % 2, n * P, P, parts=(64 * (h // 4), 64)),
                                         lhsT=V_2(n + kb, 64 * (h // 4), 64), rhs=PT2(h, (2 * n + kb) * P, P),
                                         start=kb == 0, stop=kb == 1)
                last.then_inc(sem("o2_mm"), 1)

        def attn2_act(act):
            act.dma_start(SINKS(0, AH), A["sinks_2"][0:1].broadcast_to([P, AH])).then_inc(sem("sinks"), 16)
            act.wait_ge(sem("sinks"), 16)

            def exps(h):
                act.wait_ge(sem("m2"), h + 1)
                for n in range(TT):
                    act.activation(S2(h, n * 256, 256), S2(h, n * 256, 256), ACT.Exp, bias=st2(n, h, 1),
                                   accum_out=st2(8 + n, h, 1))
                act.activation(st2(16, h), st2(0, h), ACT.Exp, bias=SINKS(h)).then_inc(sem("e2"), 1)

            def outputs2(h):
                act.wait_ge(sem("o2_mm"), h + 1)
                act.activation(O2(h), bank(6 + h % 2, 0, 512, parts=(64 * (h // 4), 64)), ACT.Copy)\
                   .then_inc(sem("o2_out"), 1)
            exps(0)
            exps(1)
            for h in range(AH):
                for a in range(2):
                    act.wait_ge(sem("pt2_tr"), 2 * h + a + 1)
                    if a == 0 and h >= 2:
                        act.wait_ge(sem("o2_mm"), h - 1)
                    act.activation(PT2(h, a * 512, 512), bank(4 + a), ACT.Copy).then_inc(sem("pt2_out"), 1)
                if h + 2 < AH:
                    exps(h + 2)
                if h:
                    outputs2(h - 1)
            outputs2(AH - 1)

        def attn2_pool(pool):
            pool.iota(REL, pattern=[[-1, 2 * P]], base=P, channel_multiplier=1, allow_small_or_imprecise_dtypes=True)
            link = linker(pool, "pool")
            link(pool.memset(WIN, 0.0))
            link(pool.affine_select(out=WIN, in_=WIN, compare_op=ALU.is_ge, fill=NEG, base=P, pattern=[[-1, 2 * P]],
                                    channel_multiplier=1))
            pool.affine_select(out=WIN, in_=WIN, compare_op=ALU.is_ge, fill=NEG, base=-1, pattern=[[1, 2 * P]],
                               channel_multiplier=-1).then_inc(sem("window"), 1)

        def attn2_dve(dve):
            link = linker(dve, "dve")
            dve.wait_ge(sem("window"), 1)
            dve.wait_ge(sem("sinks"), 16)

            def first(h):
                link(dve.scalar_tensor_tensor(BIAS2(h), REL, -SLOPE[h], WIN, ALU.mult, ALU.add))
                dve.wait_ge(sem("s2_mm"), h + 1)
                if h >= 2:
                    dve.wait_ge(sem("pt2_tr"), 2 * (h - 1))
                for a in range(2):
                    last = dve.tensor_tensor(mem("t", (h % 2) * D + a * 512, 2, 256), bank(2 * (h % 2) + a, 0, 2, 256),
                                             mem("r3", 512 + (h % 2) * 256, (0, 2), (1, 256)), ALU.add)
                last.then_inc(sem("s2_out"), 1)
                dve.wait_ge(sem("s2_out"), h + 1)
                link(dve.memset(S2(h, 0, P), NEG))
                link(dve.tensor_reduce(st2(0, h), mem("t", (h % 2) * D, TT, 256), AXIS_X, ALU.max))
                dve.tensor_scalar(st2(0, h), st2(0, h), SINKS(h), -1.0, ALU.max, ALU.mult).then_inc(sem("m2"), 1)

            def second(h):
                dve.wait_ge(sem("e2"), h + 1)
                link(dve.tensor_tensor(st2(24, h), st2(8, h), st2(16, h), ALU.add))
                link(dve.reciprocal(st2(24, h), st2(24, h)))
                for n in range(TT):
                    last = dve.tensor_scalar(S2(h, n * 256, 256), S2(h, n * 256, 256), st2(24 + n, h, 1), None, ALU.mult)
                last.then_inc(sem("p2"), 1)
            first(0)
            first(1)
            for h in range(AH):
                second(h)
                if h + 2 < AH:
                    first(h + 2)

        def merge_pe(pe):
            for c, (name, kn) in enumerate((("conv_out", 4), ("attn_out", 4))):
                i = marks[name]
                w_arrived(pe, i)
                w = wslot(i).rearrange("p k n -> p (k n)").rearrange("p (j n) -> p j n", n=D)
                src = "r0" if c else "r2"
                for m in range(KD):
                    if c:
                        pe.wait_ge(sem("merge_out"), m + 1)
                    matmuls(pe, bank(m), lambda k: w[:, k, m * P:(m + 1) * P], lambda k: mem(src, k * SEQ, SEQ), kn)\
                        .then_inc(sem("merge_mm"), 1)
                pe.drain().then_inc(sem("w_used"), 1)

        def merge_dve(dve):
            link = linker(dve, "dve")
            for m in range(KD):
                dve.wait_ge(sem("merge_mm"), m + 1)
                dve.tensor_tensor(FM("r4", m), FM("r4", m), bank(m), ALU.mult).then_inc(sem("merge_out"), 1)
            for m in range(KD):
                dve.wait_ge(sem("merge_mm"), KD + m + 1)
                link(dve.tensor_tensor(FM("r5", m), FM("r5", m), bank(m), ALU.mult))
                dve.tensor_tensor(FM("r4", m), FM("r4", m), FM("r5", m), ALU.add)

        NGRP, EPG, TOPE, FF = 4, 8, 2, 512
        NE = NGRP * EPG
        SLOTS = 128
        AHEAD = 3
        MAXB = NE + SEQ * TOPE // SLOTS
        NF = FF // P
        x_slots = nc.dram_tensor("x_slots", [(MAXB + AHEAD) * SLOTS, D], F32, kind="Internal").ap()
        y_slots = x_slots
        ZROWS = (MAXB + AHEAD) * SLOTS

        def zero_slots(pool):
            linker(pool, "pool")(pool.memset(mem("t", D, D), 0.0))
            for done in range(0, ZROWS, P):
                n = min(P, ZROWS - done)
                pool.dma_start(x_slots[done:done + n, :], mem("t", D, D, parts=(0, n))).then_inc(sem("cleared"), 16)
            pool.wait_ge(sem("cleared"), 16 * N_CLEAR)

        N_CLEAR = -(-ZROWS // P)
        m2 = lambda off, *dims, dt=None: mem("moda", 4 * D + off, *dims, dt=dt)
        NL = NGRP + NE
        (M_LG, M_GP, M_GM, M_GI, M_GF, M_OG, M_PG, M_EI, M_EM, M_EX, M_EXF, M_W, M_ID) = (
            0, 160, 192, 224, 256, 260, 276, 280, 312, 344, 376, 384, 392)
        (M_OH, M_A, M_CNT, M_NB, M_INC, M_BS, M_PB, M_DEST, M_DSTI, M_NBI, M_BSI, M_TOT, M_D1, M_R) = (
            400, 656, 784, 816, 848, 880, 912, 1040, 1048, 1056, 1088, 1120, 1124, 1128)
        M_ROUTER = 1472
        ROUTER = lambda k: m2(M_ROUTER + k * NL, NL)
        RB = m2(M_ROUTER + KD * NL, NL)
        M_ENDI = 1408
        M_BIG = 1152

        def route2_dma(act):
            act.dma_start(m2(M_ROUTER, (NL, KD), NGRP), A["w_group_2"][0].rearrange("(k p) n -> p k n", p=P),
                          allow_slow_non_contiguous=True).then_inc(sem("router"), 16)
            act.dma_start(m2(M_ROUTER + NGRP, (NL, KD), NE), A["w_expert_2"][0].rearrange("(k p) n -> p k n", p=P))\
               .then_inc(sem("router"), 16)
            act.dma_start(m2(M_ROUTER + KD * NL, NGRP), A["b_group_2"][0:1].broadcast_to([P, NGRP])).then_inc(sem("router"), 16)
            act.dma_start(m2(M_ROUTER + KD * NL + NGRP, NE), A["b_expert_2"][0:1].broadcast_to([P, NE])).then_inc(sem("router"), 16)

        def route2_pe(pe):
            pe.wait_ge(sem("router"), 64)
            for t in range(TT):
                matmuls(pe, bank(t, 0, NL), lambda k: XT("w0", k, t * P, P), ROUTER, KD).then_inc(sem("logits"), 1)
            pe.wait_ge(sem("chosen"), 1)
            for t in range(TT):
                for u in range(t + 1):
                    pe.matmul(bank(4, t * NE, NE), lhsT=mem("before", 0, P) if u == t else ones,
                              rhs=m2(M_A + u * NE, NE), start=u == 0, stop=u == t)
            matmuls(pe, bank(5, 0, NE), lambda t: ones, lambda t: m2(M_A + t * NE, NE), TT).then_inc(sem("counted"), 1)

        def route2_act(act):
            act.wait_ge(sem("g_shift"), 1)
            act.activation(m2(M_BIG, TT * NGRP), m2(M_BIG, TT * NGRP), ACT.Exp).then_inc(sem("g_exp"), 1)
            act.wait_ge(sem("e_shift"), 1)
            act.activation(m2(M_D1, TT), m2(M_D1, TT), ACT.Exp).then_inc(sem("e_exp"), 1)

        def route2_dve(dve):
            link = linker(dve, "dve")
            dve.memset(m2(M_GP, TT, EPG), -3e38)
            dve.wait_ge(sem("router"), 64)
            for t in range(TT):
                dve.wait_ge(sem("logits"), t + 1)
                last = dve.tensor_tensor(m2(M_LG + t * NL, NL), bank(t, 0, NL), RB, ALU.add)
            link(last)
            link(dve.tensor_copy(m2(M_GP, (EPG, TT), NGRP), m2(M_LG, (NL, TT), NGRP)))
            for t in range(TT):
                last = dve.max(m2(M_GM + t * 8, 8), m2(M_GP + t * EPG, EPG))
            link(last)
            for t in range(TT):
                last = dve.max_index(m2(M_GI + t * 8, 8, dt=U32), m2(M_GM + t * 8, 8), m2(M_GP + t * EPG, EPG))
            link(last)
            dve.tensor_tensor(m2(M_BIG, TT, NGRP), m2(M_LG, (NL, TT), NGRP), m2(M_GM, (8, TT), (0, NGRP)), ALU.subtract)\
               .then_inc(sem("g_shift"), 1)
            link(dve.tensor_copy(m2(M_GF, TT), m2(M_GI, (8, TT), dt=U32)))
            link(dve.tensor_tensor(m2(M_OG, TT, NGRP), m2(M_GF, (1, TT), (0, NGRP)), mem("iota", 0, (0, TT), (1, NGRP)), ALU.is_equal))
            dve.wait_ge(sem("g_exp"), 1)
            link(dve.tensor_reduce(m2(M_PG, TT), m2(M_BIG, TT, NGRP), AXIS_X, ALU.add))
            link(dve.reciprocal(m2(M_PG, TT), m2(M_PG, TT)))
            link(dve.tensor_tensor(m2(M_BIG, TT, NGRP, EPG), m2(M_LG + NGRP, (NL, TT), (EPG, NGRP), (1, EPG)),
                                   m2(M_OG, (NGRP, TT), (1, NGRP), (0, EPG)), ALU.mult))
            link(dve.tensor_reduce(m2(M_EI, TT, EPG), m2(M_BIG, (NE, TT), (1, EPG), (EPG, NGRP)), AXIS_X, ALU.add))
            for t in range(TT):
                last = dve.max(m2(M_EM + t * 8, 8), m2(M_EI + t * 8, 8))
            link(last)
            for t in range(TT):
                last = dve.max_index(m2(M_EX + t * 8, 8, dt=U32), m2(M_EM + t * 8, 8), m2(M_EI + t * 8, 8))
            link(last)
            link(dve.tensor_copy(m2(M_EXF, TT, TOPE), m2(M_EX, (8, TT), (1, TOPE), dt=U32)))
            link(dve.scalar_tensor_tensor(m2(M_ID, TT, TOPE), m2(M_GF, (1, TT), (0, TOPE)), float(EPG), m2(M_EXF, TT, TOPE),
                                          ALU.mult, ALU.add))
            link(dve.tensor_tensor(m2(M_OH, TT * TOPE, NE), m2(M_ID, (1, TT * TOPE), (0, NE)), mem("iota", 0, (0, TT * TOPE), (1, NE)),
                                   ALU.is_equal))
            dve.tensor_tensor(m2(M_A, TT, NE), m2(M_OH, (TOPE * NE, TT), NE), m2(M_OH + NE, (TOPE * NE, TT), NE), ALU.add)\
               .then_inc(sem("chosen"), 1)
            dve.tensor_tensor(m2(M_D1, TT), m2(M_EM + 1, (8, TT)), m2(M_EM, (8, TT)), ALU.subtract).then_inc(sem("e_shift"), 1)
            dve.wait_ge(sem("e_exp"), 1)
            link(dve.tensor_scalar(m2(M_R, TT), m2(M_D1, TT), 1.0, None, ALU.add))
            link(dve.reciprocal(m2(M_R, TT), m2(M_R, TT)))
            link(dve.tensor_tensor(m2(M_R, TT), m2(M_R, TT), m2(M_PG, TT), ALU.mult))
            dve.tensor_copy(m2(M_W, (TOPE, TT)), m2(M_R, TT))
            dve.tensor_tensor(m2(M_W + 1, (TOPE, TT)), m2(M_R, TT), m2(M_D1, TT), ALU.mult)
            dve.wait_ge(sem("counted"), 1)
            link(dve.tensor_copy(m2(M_CNT, NE), bank(5, 0, NE)))
            link(dve.tensor_scalar(m2(M_EI, EPG), mem("iota", 0, EPG), float(SLOTS), None, ALU.mult))
            link(dve.tensor_tensor(m2(M_BIG, NE, EPG), m2(M_CNT, (1, NE), (0, EPG)), m2(M_EI, (0, NE), (1, EPG)), ALU.is_gt))
            link(dve.tensor_reduce(m2(M_NB, NE), m2(M_BIG, NE, EPG), AXIS_X, ALU.add))
            link(dve.tensor_scalar(m2(M_NB, NE), m2(M_NB, NE), 1.0, None, ALU.max))
            link(dve.tensor_tensor_scan(m2(M_INC, NE), mem("ones", 0, NE), m2(M_NB, NE), 0.0, ALU.mult, ALU.add))
            link(dve.tensor_tensor(m2(M_BS, NE), m2(M_INC, NE), m2(M_NB, NE), ALU.subtract))
            dve.tensor_copy(m2(M_NBI, NE, dt=I32), m2(M_NB, NE))
            dve.tensor_copy(m2(M_BSI, NE, dt=I32), m2(M_BS, NE))
            dve.tensor_copy(m2(M_ENDI, NE, dt=I32), m2(M_INC, NE))
            dve.tensor_copy(m2(M_TOT, 1, dt=I32), m2(M_INC + NE - 1, 1))
            link(dve.scalar_tensor_tensor(m2(M_PB, TT, NE), m2(M_BS, (0, TT), (1, NE)), float(SLOTS), bank(4, 0, TT, NE),
                                          ALU.mult, ALU.add))
            link(dve.tensor_tensor(m2(M_BIG, TT, TOPE, NE), m2(M_OH, TT, TOPE, NE), m2(M_PB, (NE, TT), (0, TOPE), (1, NE)), ALU.mult))
            link(dve.tensor_reduce(m2(M_DEST, TT * TOPE), m2(M_BIG, TT * TOPE, NE), AXIS_X, ALU.add))
            dve.tensor_copy(m2(M_DSTI, TT * TOPE, dt=U32), m2(M_DEST, TT * TOPE)).then_inc(sem("slots"), 1)

        def dispatch_pool(pool):
            pool.wait_ge(sem("slots"), 1)
            for i in range(TT * TOPE):
                pool.indirect_dma_start(x_slots, bass.IndirectOffsetOnAxis(ap=m2(M_DSTI + i, 1, dt=U32), axis=0),
                                        mem("r0", (i // TOPE) * D, D), None).then_inc(sem("sent"), 16)
            pool.wait_ge(sem("sent"), 16 * TT * TOPE)

        EW = [[mem(r, 0, KD, FF) for r in ("r1", "r2")] + [mem("r3", 0, NF, D)],
              [mem(r, 0, KD, FF) for r in ("r4", "r5")] + [mem("r6", 0, NF, D)]]
        eg = A["w_gate_2"][0].rearrange("e (k p) n -> e p k n", p=P)
        eu = A["w_up_2"][0].rearrange("e (k p) n -> e p k n", p=P)
        ed = A["w_down_2"][0].rearrange("e (k p) n -> e p k n", p=P)
        XR = mem("w0", 0, D, parts=(0, SLOTS))
        XB = mem("w0", D, D, parts=(0, SLOTS))
        XBT = mem("w0", 2 * D, KD, SLOTS)
        SG = mem("w0", 3 * D, NF, SLOTS)
        HT = mem("w0", 3 * D + 512, NF, SLOTS)
        YB = lambda n0=0, n=D, parts=SLOTS: mem("w1", n0, n, parts=(0, parts))

        def expert_weights_sp(sp):
            def load(e, s):
                for m, tab in enumerate((eg, eu, ed)):
                    sp.dma_start(EW[s][m], tab[e]).then_inc(sem(f"ew{s}_{m}"), 16)
            load(0, 0)
            sp.wait_ge(sem("rows_done"), 3 * TT)
            load(1, 1)
            sp.wait_ge(sem("slots"), 1)
            with sp.Fori(1, NE // 2) as i:
                for s in range(2):
                    done = sp.value_load(arena[0:1, bass.ds(i * 2 + (layout["moda"] + 4 * D + M_ENDI + s - 2), 1)].bitcast(I32),
                                         min_val=1, max_val=MAXB)
                    sp.wait_ge(sem("y_mm"), done)
                    load(i * 2 + s, s)

        def experts_pe(pe):
            def transposes(wait):
                pe.wait_ge(sem("x_staged"), wait)
                pe.sem_inc(sem("pe_step"), 1)
                for k in range(KD):
                    last = pe.transpose(bank(k // 4, (k % 4) * SLOTS, SLOTS), XB[:, k * P:(k + 1) * P], mem("ident", 0, SLOTS, parts=(0, SLOTS)))
                last.then_inc(sem("xb_tr"), 1)
            transposes(1)
            ob = layout["moda"] + 4 * D
            with pe.Fori(0, NE // 2) as i:
                for s in range(2):
                    nb = pe.value_load(arena[0:1, bass.ds(i * 2 + (ob + M_NBI + s), 1)].bitcast(I32), min_val=1, max_val=8)
                    bs = pe.value_load(arena[0:1, bass.ds(i * 2 + (ob + M_BSI + s), 1)].bitcast(I32), min_val=0, max_val=MAXB - 1)
                    for m in range(3):
                        pe.wait_ge(sem(f"ew{s}_{m}"), i * 16 + 16)
                        pe.sem_inc(sem("pe_step"), 1)
                    with pe.Fori(0, nb) as j:
                        g = bs + j
                        pe.wait_ge(sem("xbT"), g + 1)
                        for m in range(2):
                            for f in range(NF):
                                last = matmuls(pe, bank(2 + m, f * SLOTS, SLOTS), lambda k: EW[s][m][:, k, f * P:(f + 1) * P],
                                               lambda k: XBT[:, k, :], KD)
                            last.then_inc(sem("gate_mm" if m == 0 else "up_mm"), 1)
                        transposes(g + 2)
                        pe.wait_ge(sem("hT"), g + 1)
                        pe.wait_ge(sem("y_out"), g + 1)
                        for n in range(2):
                            last = matmuls(pe, bank(4 + n, 0, 512, parts=(0, SLOTS)), lambda k: HT[:, k, :],
                                           lambda k: EW[s][2][:, k, n * 512:(n + 1) * 512], NF)
                        last.then_inc(sem("y_mm"), 1)

        def n_blocks(eng):
            return eng.value_load(m2(M_TOT, 1, dt=I32)[0:1], min_val=NE, max_val=MAXB)

        def experts_act(act):
            n = n_blocks(act)
            with act.Fori(0, n) as g:
                act.wait_ge(sem("gate_mm"), g + 1)
                act.activation(SG, bank(2, 0, NF, SLOTS), ACT.Silu).then_inc(sem("silu"), 1)

        def experts_dve(dve):
            n = n_blocks(dve)

            def stage(arrived):
                dve.wait_ge(sem("x_block"), arrived)
                dve.tensor_copy(XB, XR).then_inc(sem("x_staged"), 1)

            def transposed():
                for a in range(2):
                    last = dve.tensor_copy(XBT[:, 4 * a:4 * a + 4, :], bank(a, 0, 4, SLOTS))
                last.then_inc(sem("xbT"), 1)
            stage(16)
            dve.sem_inc(sem("y_out"), 1)
            dve.wait_ge(sem("xb_tr"), 1)
            transposed()
            stage(32)
            with dve.Fori(0, n) as g:
                dve.wait_ge(sem("up_mm"), g + 1)
                dve.wait_ge(sem("silu"), g + 1)
                dve.tensor_tensor(HT, SG, bank(3, 0, NF, SLOTS), ALU.mult).then_inc(sem("hT"), 1)
                dve.wait_ge(sem("xb_tr"), g + 2)
                transposed()
                stage(g * 16 + 48)
                dve.wait_ge(sem("y_mm"), g + 1)
                dve.wait_ge(sem("y_stored"), g * 16 + 16)
                dve.tensor_copy(YB(0, 512), bank(4, 0, 512, parts=(0, SLOTS)))
                dve.tensor_copy(YB(512, 512), bank(5, 0, 512, parts=(0, SLOTS))).then_inc(sem("y_out"), 1)

        def experts_pool(pool):
            n = n_blocks(pool)

            def load(src):
                pool.dma_start(XR, src).then_inc(sem("x_block"), 16)
            load(x_slots[0:SLOTS, :])
            pool.dma_start(YB(parts=1), x_slots[0:1, :]).then_inc(sem("y_stored"), 16)
            for k in (1, 2):
                pool.wait_ge(sem("x_staged"), k)
                load(x_slots[k * SLOTS:(k + 1) * SLOTS, :])
            with pool.Fori(0, n) as g:
                pool.wait_ge(sem("x_staged"), g + 3)
                pool.sem_inc(sem("pool_step"), 1)
                load(x_slots[bass.ds(g * SLOTS + AHEAD * SLOTS, SLOTS), :])
                pool.wait_ge(sem("y_out"), g + 2)
                pool.sem_inc(sem("pool_step"), 1)
                pool.dma_start(y_slots[bass.ds(g * SLOTS, SLOTS), :], YB()).then_inc(sem("y_stored"), 16)
            pool.wait_ge(sem("x_block"), 16)
            pool.wait_ge(sem("y_stored"), n * 16 + 16)
            pool.sem_inc(sem("pool_step"), 1)

        def combine_pool(pool):
            for i in range(TT * TOPE):
                pool.indirect_dma_start(mem("r1" if i < 4 else "r2", (i % 4) * D, D), None, y_slots,
                                        bass.IndirectOffsetOnAxis(ap=m2(M_DSTI + i, 1, dt=U32), axis=0))\
                    .then_inc(sem(f"y_back{i // TOPE}"), 16)

        def combine_dve(dve):
            for t in range(TT):
                dve.wait_ge(sem(f"y_back{t}"), 16 * TOPE)
                for k in range(TOPE):
                    i = t * TOPE + k
                    if k:
                        dve.wait_ge(sem("combined"), i)
                    dve.scalar_tensor_tensor(H(t), mem("r1" if i < 4 else "r2", (i % 4) * D, D), m2(M_W + i, 1), H(t),
                                             ALU.mult, ALU.add).then_inc(sem("combined"), 1)

        nothing = lambda eng: None
        PHASES = []

        def phase(pe=nothing, act=nothing, dve=nothing, pool=nothing):
            PHASES.append(dict(pe=pe, act=act, dve=dve, pool=pool))

        def both(proj, norm_, before=nothing):
            return (lambda pe: (proj["pe"](pe), norm_["pe"](pe)),
                    lambda act: (before(act), norm_["act"](act)),
                    lambda dve: (proj["dve"](dve), norm_["dve"](dve)))

        phase(setup_pe, setup_act, setup_dve, setup_pool)
        phase(**norm(0, mod(MOD0["sc1"]), mod(MOD0["sh1"]), xn_temp, "r0"))
        phase(hgrn_in_pe, hgrn_in_act, hgrn_in_dve)
        phase(hgrn_scan_pe, hgrn_scan_act, hgrn_scan_dve, hgrn_scan_pool)
        phase(hgrn_out_norm_pe, hgrn_out_norm_act, hgrn_out_norm_dve)
        o0 = out_proj(0, marks["hgrn_out"], lambda k, t: FM("r2", k, t * P, P), KD, MOD0["g1"])
        n1 = norm(1, mod(MOD0["sc2"]), mod(MOD0["sh2"]), lambda t: mem("r0", t * D, D), "r1", ready=o0["ready"])
        phase(*both(o0, n1, before=lambda act: peer_load_keys(act, 0)))
        phase(**peer_query(0))
        phase(**peer(0))
        phase(**norm(2, mod(MOD1["sckv"]), mod(MOD1["shkv"]), xn_temp, "r0"))
        n3 = norm(3, mod(MOD1["sc1"]), mod(MOD1["sh1"]), lambda t: mem("r3", t * D, D), "r4", again=True)
        turned3 = norms_turned[0] * 2 * TT

        def kvq_pe(pe):
            kv_pe(pe)
            pe.wait_ge(sem("kv_out"), 8)
            n3["pe"](pe)
            pe.wait_ge(sem("norm_xT"), turned3)
            sbq_pe(pe)
        phase(kvq_pe, lambda act: (kv_act(act), n3["act"](act), sbq_act(act)), lambda dve: (n3["dve"](dve), kv_dve(dve)))
        phase(sb_pe, sb_act, sb_dve, sb_pool)
        o1 = out_proj(1, marks["sb_out"], lambda k, t: FM("r4", k, t * P, P), KD, MOD1["g1"])
        n4 = norm(4, mod(MOD1["sc2"]), mod(MOD1["sh2"]), lambda t: mem("r0", t * D, D), "r1", ready=o1["ready"])
        phase(*both(o1, n4, before=lambda act: peer_load_keys(act, 1)))
        phase(**peer_query(1))
        phase(**peer(1))
        n5 = norm(5, ROW2(0), None, H, None)
        n6 = norm(6, ROW2(1), None, xn_temp, "r0", ready=lambda act, t: act.wait_ge(sem("norm_xn"), 5 * TT + t + 1))
        phase(n6["pe"], lambda act: (rows2_act(act), conv_rows_dma(act), n5["act"](act), n6["act"](act)),
              lambda dve: (rows2_dve(dve), n5["dve"](dve), n6["dve"](dve)))
        phase(in2_pe, in2_act, in2_dve, in2_pool)
        phase(attn2_pe, attn2_act, attn2_dve, attn2_pool)
        phase(merge_pe, nothing, merge_dve)
        o2 = out_proj(2, marks["out2"], lambda k, t: FM("r4", k, t * P, P), KD, None)
        n7 = norm(7, ROW2(2), None, lambda t: mem("r0", t * D, D), "w0", ready=o2["ready"])
        FREED = len(PHASES)
        phase(*both(o2, n7, before=route2_dma))
        phase(route2_pe, route2_act, route2_dve, dispatch_pool)
        phase(experts_pe, experts_act, experts_dve, experts_pool)
        n8 = norm(8, ROW2(3), None, H, None, ready=lambda act, t: act.wait_ge(sem("combined"), TOPE * (t + 1)))
        phase(nothing, n8["act"], lambda dve: (combine_dve(dve), n8["dve"](dve)), combine_pool)

        block = ctx.enter_context(nc.Block())

        @block.sync
        def _(sp):
            setup_sp(sp)
            load_weights(sp)
            enter(sp, FREED)
            expert_weights_sp(sp)
            for t in range(TT):
                sp.wait_ge(sem("norm_xn"), 8 * TT + t + 1)
                sp.dma_start(out[0, t * P:(t + 1) * P, :], H(t)).then_inc(sem("stored"), 16)
            sp.wait_ge(sem("stored"), 16 * TT)

        @block.tensor
        def _(pe):
            for n, p in enumerate(PHASES):
                enter(pe, n)
                p["pe"](pe)
                leave(pe, "pe")

        @block.scalar
        def _(act):
            for n, p in enumerate(PHASES):
                enter(act, n)
                p["act"](act)
                leave(act, "act")

        @block.vector
        def _(dve):
            for n, p in enumerate(PHASES):
                enter(dve, n)
                p["dve"](dve)
                leave(dve, "dve")

        @block.gpsimd
        def _(pool):
            for n, p in enumerate(PHASES):
                enter(pool, n)
                p["pool"](pool)
                leave(pool, "pool")


_INS = [
    "x", "c", "ada_w", "ada_b", "norm_mix_g", "norm_ffn_g", "hgrn_w_in", "hgrn_lb_logits", "hgrn_onorm_g",
    "hgrn_w_out", "kv_ada_w", "kv_ada_b", "kv_norm_g", "kv_w", "sb_w_q", "sb_w_out", "peer_w_q",
    "peer_subkeys", "peer_u", "peer_v", "final_norm_g", "g_mix_2", "w_in_2", "w_dw_2", "b_dw_2",
    "ln_conv_g_2", "ln_conv_b_2", "sinks_2", "w_conv_out_2", "w_attn_out_2", "w_out_2", "g_ffn_2",
    "w_group_2", "b_group_2", "w_expert_2", "b_expert_2", "w_gate_2", "w_up_2", "w_down_2", "g_final_2",
]


def kernel(**inputs):
    import numpy as _np
    import concourse.bacc as _bacc
    from concourse import mybir as _mybir
    from concourse.bass_utils import run_bass_kernel_spmd as _run

    nc = _bacc.Bacc("TRN2", target_bir_lowering=False, num_devices=1)
    arrays, args = {}, {}
    for name in _INS:
        a = _np.ascontiguousarray(inputs[name])
        arrays[f"in_{name}_dram"] = a
        args[name] = nc.dram_tensor(f"in_{name}_dram", a.shape, _mybir.dt.from_np(a.dtype), kind="ExternalInput").ap()
    out = nc.dram_tensor("out_dram", (1, SEQ, D), F32, kind="ExternalOutput").ap()
    build_program(nc, args, out)
    r = _run(nc, [arrays], core_ids=[0])
    return r.results[0]["out_dram"]
```
